# Optimizing a Trainium2 kernel written in Bass

```python
import math
import jax, jax.numpy as jnp
from jax import lax
import numpy as np

D_MODEL = 1024
BATCH = 1
SEQ = 512
DEPTH = 2
DEC_BATCH = 8
DEC_SEQ = 1
PAST_LEN = 4096
PAGE_SIZE = 128

N_EVEN = (DEPTH + 1) // 2
N_ODD = DEPTH // 2
GLA_HEADS = 4
GLA_DK = D_MODEL // 16
GLA_DV = D_MODEL // 8
GLA_RANK = 16
GLA_TAU = 16.0
RET_HEADS = 4
RET_DK = D_MODEL // 8
RET_DV = D_MODEL // 8
CHUNK = 64
CONV_W = 3
D_FF = D_MODEL * 11 // 4
ROPE_BASE = 10000.0
NORM_EPS = 1e-5
ALPHA = (2 * DEPTH) ** 0.25
BETA = (8 * DEPTH) ** -0.25
GLA_QK = GLA_HEADS * GLA_DK
GLA_V = GLA_HEADS * GLA_DV
RET_QK = RET_HEADS * RET_DK
RET_V = RET_HEADS * RET_DV
MIX_SPLITS = (GLA_QK, GLA_QK, GLA_V, GLA_RANK, GLA_V, RET_QK, RET_QK, RET_V, RET_V)
MIX_IN = sum(MIX_SPLITS)
MIX_V = GLA_V + RET_V

kernel_name = "gla_retnet_shortconv_convffn_deepnorm_step"

def _split_points(sizes):
    pts, acc = [], 0
    for s in sizes[:-1]:
        acc += s
        pts.append(acc)
    return pts

def layer_norm(x, g, b):
    xf = x.astype(jnp.float32)
    mu = jnp.mean(xf, axis=-1, keepdims=True)
    var = jnp.mean(jnp.square(xf - mu), axis=-1, keepdims=True)
    return ((xf - mu) * lax.rsqrt(var + NORM_EPS) * g + b).astype(x.dtype)

def rms_head_norm(o, g):
    of = o.astype(jnp.float32)
    return (of * lax.rsqrt(jnp.mean(of * of, axis=-1, keepdims=True) + NORM_EPS) * g).astype(o.dtype)

def group_norm_heads(o, g, b):
    h, dv = o.shape[-2], o.shape[-1]
    of = o.astype(jnp.float32)
    mu = jnp.mean(of, axis=-1, keepdims=True)
    var = jnp.mean(jnp.square(of - mu), axis=-1, keepdims=True)
    return ((of - mu) * lax.rsqrt(var + NORM_EPS) * g.reshape(h, dv) + b.reshape(h, dv)).astype(o.dtype)

def rotary(x, pos):
    d = x.shape[-1]
    inv_freq = 1.0 / (ROPE_BASE ** (jnp.arange(0, d, 2, dtype=jnp.float32) / d))
    ang = pos[:, None] * inv_freq[None, :]
    cos, sin = jnp.cos(ang)[:, None, :], jnp.sin(ang)[:, None, :]
    xf = x.astype(jnp.float32)
    x1, x2 = xf[..., : d // 2], xf[..., d // 2:]
    return jnp.concatenate([x1 * cos - x2 * sin, x2 * cos + x1 * sin], axis=-1).astype(x.dtype)

def chunked_gated_linear_attention(q, k, v, log_a, s0):
    bsz, t_len, h, _ = q.shape
    dv = v.shape[-1]
    c = min(CHUNK, t_len)
    pad = (-t_len) % c

    def prep(a):
        a = jnp.pad(a.astype(jnp.float32), ((0, 0), (0, pad), (0, 0), (0, 0)))
        n = a.shape[1] // c
        return a.reshape(bsz, n, c, h, a.shape[-1]).transpose(1, 0, 3, 2, 4)

    qc, kc, vc, ac = prep(q), prep(k), prep(v), prep(log_a)
    causal = jnp.tril(jnp.ones((c, c), dtype=bool))

    def step(state, xs):
        qb, kb, vb, ab = xs
        cum = jnp.cumsum(ab, axis=2)
        diff = cum[:, :, :, None, :] - cum[:, :, None, :, :]
        decay = jnp.exp(jnp.where(causal[:, :, None], diff, -jnp.inf))
        if ab.shape[-1] == 1:
            scores = jnp.einsum('bhtd,bhsd->bhts', qb, kb) * decay[..., 0]
        else:
            scores = jnp.einsum('bhtd,bhsd,bhtsd->bhts', qb, kb, decay)
        out = (jnp.einsum('bhts,bhsv->bhtv', scores, vb)
               + jnp.einsum('bhtd,bhdv->bhtv', qb * jnp.exp(cum), state))
        last = cum[:, :, -1:, :]
        state = (jnp.swapaxes(jnp.exp(last), -1, -2) * state
                 + jnp.einsum('bhsd,bhsv->bhdv', kb * jnp.exp(last - cum), vb))
        return state, out

    s_fin, oc = lax.scan(step, s0.astype(jnp.float32), (qc, kc, vc, ac))
    o = oc.transpose(1, 0, 3, 2, 4).reshape(bsz, -1, h, dv)[:, :t_len]
    return o.astype(v.dtype), s_fin.astype(s0.dtype)

def causal_dwconv(u, buf, w, b):
    t_len = u.shape[1]
    ub = jnp.concatenate([buf.astype(u.dtype), u], axis=1)
    y = b + sum(w[j] * ub[:, j:j + t_len] for j in range(CONV_W))
    return y, ub[:, -(CONV_W - 1):]

def gla_retention_mixer(x, pos, s_gla, s_ret, w_in, w_gate_up, b_gate, g_gla, g_ret, b_ret, w_out):
    bsz, t_len, _ = x.shape
    z = x @ w_in
    q_g, k_g, v_g, a_lr, r_g, q_r, k_r, v_r, g_r = jnp.split(z, _split_points(MIX_SPLITS), axis=-1)

    def heads(a, h):
        return a.reshape(bsz, t_len, h, -1)

    log_a = jax.nn.log_sigmoid((a_lr @ w_gate_up + b_gate).astype(jnp.float32)) / GLA_TAU
    o_g, s_gla = chunked_gated_linear_attention(
        heads(q_g, GLA_HEADS) * (GLA_DK ** -0.5), heads(k_g, GLA_HEADS),
        heads(v_g, GLA_HEADS), heads(log_a, GLA_HEADS), s_gla)
    o_g = rms_head_norm(o_g, g_gla) * jax.nn.silu(heads(r_g, GLA_HEADS))

    qr = rotary(heads(q_r, RET_HEADS), pos)
    kr = rotary(heads(k_r, RET_HEADS), pos) * (RET_DK ** -0.5)
    log_gamma = jnp.log1p(-jnp.exp2(-5.0 - jnp.arange(RET_HEADS, dtype=jnp.float32)))
    log_g = jnp.broadcast_to(log_gamma[:, None], (bsz, t_len, RET_HEADS, 1))
    o_r, s_ret = chunked_gated_linear_attention(qr, kr, heads(v_r, RET_HEADS), log_g, s_ret)
    o_r = group_norm_heads(o_r, g_ret, b_ret) * jax.nn.silu(heads(g_r, RET_HEADS))

    y = jnp.concatenate([o_g.reshape(bsz, t_len, GLA_V), o_r.reshape(bsz, t_len, RET_V)], axis=-1) @ w_out
    return y, s_gla, s_ret

def short_conv_mixer(x, s_conv, w_in, w_dw, b_dw, w_out):
    gate_b, gate_c, h = jnp.split(x @ w_in, 3, axis=-1)
    conv, s_conv = causal_dwconv(gate_c * h, s_conv, w_dw, b_dw)
    return (gate_b * conv) @ w_out, s_conv

def conv_ffn(x, s_ffn, w_in, w_dw, b_dw, w_out):
    u = x @ w_in
    c, s_ffn = causal_dwconv(u, s_ffn, w_dw, b_dw)
    a, g = jnp.split(c, 2, axis=-1)
    return (jax.nn.silu(g) * a) @ w_out, s_ffn

def run_trunk(x, pos, st_gla, st_ret, st_conv, st_ffn, weights):
    (w_mix_in, w_gla_gate_up, b_gla_gate, g_gla_norm, g_ret_norm, b_ret_norm, w_mix_out,
     w_sc_in, w_sc_dw, b_sc_dw, w_sc_out, ln1_g, ln1_b,
     w_ffn_in, w_ffn_dw, b_ffn_dw, w_ffn_out, ln2_g, ln2_b) = weights
    new_gla, new_ret, new_conv, new_ffn = [], [], [], []
    for layer in range(DEPTH):
        i = layer // 2
        if layer % 2 == 0:
            h, sg, sr = gla_retention_mixer(x, pos, st_gla[i], st_ret[i], w_mix_in[i], w_gla_gate_up[i],
                                            b_gla_gate[i], g_gla_norm[i], g_ret_norm[i], b_ret_norm[i],
                                            w_mix_out[i])
            new_gla.append(sg)
            new_ret.append(sr)
        else:
            h, sc = short_conv_mixer(x, st_conv[i], w_sc_in[i], w_sc_dw[i], b_sc_dw[i], w_sc_out[i])
            new_conv.append(sc)
        x = layer_norm(ALPHA * x + h, ln1_g[layer], ln1_b[layer])
        h, sf = conv_ffn(x, st_ffn[layer], w_ffn_in[layer], w_ffn_dw[layer], b_ffn_dw[layer], w_ffn_out[layer])
        new_ffn.append(sf)
        x = layer_norm(ALPHA * x + h, ln2_g[layer], ln2_b[layer])
    return x, jnp.stack(new_gla), jnp.stack(new_ret), jnp.stack(new_conv), jnp.stack(new_ffn)

def setup_inputs(seed: int = 0) -> dict:
    key = jax.random.key(seed)
    ks = iter(jax.random.split(key, 32))

    def nrm(shape, scale):
        return jax.random.normal(next(ks), shape, jnp.float32) * scale

    return {
        "x_prompt": nrm((BATCH, SEQ, D_MODEL), 1.0),
        "x_sample": nrm((DEC_BATCH, DEC_SEQ, D_MODEL), 1.0),
        "state_gla": nrm((N_EVEN, DEC_BATCH, GLA_HEADS, GLA_DK, GLA_DV), 1.0),
        "state_ret": nrm((N_EVEN, DEC_BATCH, RET_HEADS, RET_DK, RET_DV), 1.0),
        "state_conv": nrm((N_ODD, DEC_BATCH, CONV_W - 1, D_MODEL), 1.0),
        "state_ffn": nrm((DEPTH, DEC_BATCH, CONV_W - 1, 2 * D_FF), 1.0),
        "w_mix_in": nrm((N_EVEN, D_MODEL, MIX_IN), D_MODEL ** -0.5),
        "w_gla_gate_up": nrm((N_EVEN, GLA_RANK, GLA_QK), GLA_RANK ** -0.5),
        "b_gla_gate": nrm((N_EVEN, GLA_QK), 0.01),
        "g_gla_norm": 1.0 + nrm((N_EVEN, GLA_DV), 0.01),
        "g_ret_norm": 1.0 + nrm((N_EVEN, RET_V), 0.01),
        "b_ret_norm": nrm((N_EVEN, RET_V), 0.01),
        "w_mix_out": nrm((N_EVEN, MIX_V, D_MODEL), BETA * MIX_V ** -0.5),
        "w_sc_in": nrm((N_ODD, D_MODEL, 3 * D_MODEL), D_MODEL ** -0.5),
        "w_sc_dw": nrm((N_ODD, CONV_W, D_MODEL), CONV_W ** -0.5),
        "b_sc_dw": nrm((N_ODD, D_MODEL), 0.01),
        "w_sc_out": nrm((N_ODD, D_MODEL, D_MODEL), BETA * D_MODEL ** -0.5),
        "ln1_g": 1.0 + nrm((DEPTH, D_MODEL), 0.01),
        "ln1_b": nrm((DEPTH, D_MODEL), 0.01),
        "w_ffn_in": nrm((DEPTH, D_MODEL, 2 * D_FF), D_MODEL ** -0.5),
        "w_ffn_dw": nrm((DEPTH, CONV_W, 2 * D_FF), CONV_W ** -0.5),
        "b_ffn_dw": nrm((DEPTH, 2 * D_FF), 0.01),
        "w_ffn_out": nrm((DEPTH, D_FF, D_MODEL), BETA * D_FF ** -0.5),
        "ln2_g": 1.0 + nrm((DEPTH, D_MODEL), 0.01),
        "ln2_b": nrm((DEPTH, D_MODEL), 0.01),
    }

def reference(x_prompt, x_sample, state_gla, state_ret, state_conv, state_ffn,
              w_mix_in, w_gla_gate_up, b_gla_gate, g_gla_norm, g_ret_norm, b_ret_norm, w_mix_out,
              w_sc_in, w_sc_dw, b_sc_dw, w_sc_out, ln1_g, ln1_b,
              w_ffn_in, w_ffn_dw, b_ffn_dw, w_ffn_out, ln2_g, ln2_b):
    weights = (w_mix_in, w_gla_gate_up, b_gla_gate, g_gla_norm, g_ret_norm, b_ret_norm, w_mix_out,
               w_sc_in, w_sc_dw, b_sc_dw, w_sc_out, ln1_g, ln1_b,
               w_ffn_in, w_ffn_dw, b_ffn_dw, w_ffn_out, ln2_g, ln2_b)
    bp, tp = x_prompt.shape[0], x_prompt.shape[1]
    dt = x_prompt.dtype
    z_gla = jnp.zeros((N_EVEN, bp, GLA_HEADS, GLA_DK, GLA_DV), dt)
    z_ret = jnp.zeros((N_EVEN, bp, RET_HEADS, RET_DK, RET_DV), dt)
    z_conv = jnp.zeros((N_ODD, bp, CONV_W - 1, D_MODEL), dt)
    z_ffn = jnp.zeros((DEPTH, bp, CONV_W - 1, 2 * D_FF), dt)
    pos_p = jnp.arange(tp, dtype=jnp.float32)
    y_prompt, gla_p, ret_p, conv_p, ffn_p = run_trunk(x_prompt, pos_p, z_gla, z_ret, z_conv, z_ffn, weights)
    pos_s = PAST_LEN + jnp.arange(x_sample.shape[1], dtype=jnp.float32)
    y_sample, gla_s, ret_s, conv_s, ffn_s = run_trunk(x_sample, pos_s, state_gla, state_ret,
                                                      state_conv, state_ffn, weights)
    return (y_prompt, y_sample, gla_p, gla_s, ret_p, ret_s, conv_p, conv_s, ffn_p, ffn_s)


_drawn_inputs = setup_inputs


def setup_inputs(seed=0):
    import zlib

    import numpy as np

    out = dict(_drawn_inputs(seed))
    spreads = {}
    factors = {'b_gla_gate': 8.0,
     'g_gla_norm': 26.389,
     'g_ret_norm': 28.154,
     'b_ret_norm': 29.071,
     'b_sc_dw': 48.714,
     'ln1_g': 3.63,
     'ln1_b': 3.747,
     'b_ffn_dw': 8.0,
     'ln2_g': 3.806,
     'ln2_b': 3.745}
    for name, (base, spread) in spreads.items():
        noise = np.random.default_rng([zlib.crc32(name.encode()), seed]).standard_normal(out[name].shape)
        drawn = base * np.exp(spread * noise) if base else spread * noise
        out[name] = __import__('jax').numpy.asarray(drawn.astype(out[name].dtype))
    for name, factor in factors.items():
        out[name] = (out[name] * factor).astype(out[name].dtype)
    return out
```

```python
from contextlib import ExitStack

import numpy as np
import concourse.bass as bass
from concourse import mybir
from concourse.alu_op_type import AluOpType as ALU

ACT = mybir.ActivationFunctionType
F32 = mybir.dt.float32
F32R = mybir.dt.float32r
U8 = mybir.dt.uint8
AX_X = mybir.AxisListType.X

P = 128
D = 1024
KD = D // P
T = 512
NS = 8
N = T + NS
HA = 256
FF = 2816
NF = FF // P
NU = 2 * NF
CW = 3
GH, GDK, DV, RH, RDK = 4, 64, 128, 4, 128
RANK = 16
C = 128
NC = T // C
LEVELS = 7
EPS = 1e-5
DEPTH = 2
PAST = 4096
ALPHA = (2 * DEPTH) ** 0.25
TAU = 16.0
A_LR = 2 * GH * GDK + GH * DV
MIX_IN = 3600

QG, KG, VG, RG, QR, KR, VR, GR = 0, 2, 4, 8, 12, 16, 20, 24
NZ = 28

V_LN = 4
COL_LN1G, COL_LN1B, COL_LN2G, COL_LN2B = 0, 16, 32, 48
COL_SCW, COL_SCB, COL_BG, COL_GG, COL_GR, COL_BR = 64, 88, 96, 98, 99, 103
N_V = 107

GAMMA = [1.0 - 2.0 ** (-5.0 - h) for h in range(RH)]


def host_constants():
    ident = np.eye(P, dtype=np.float32)
    s = np.arange(C)[:, None]
    t = np.arange(C)[None, :]
    g = np.array(GAMMA, np.float64)
    dec = np.stack([np.where(s <= t, np.power(x, (t - s).astype(np.float64)), 0.0) * RDK ** -0.5 for x in g], 1)
    gpow = np.broadcast_to(np.power(g[:, None], np.arange(1, C + 1)[None, :])[None], (P, RH, C))
    kdec = np.power(g[None, :], (C - 1 - np.arange(C))[:, None].astype(np.float64)) * RDK ** -0.5
    inv = (np.float32(1.0) / np.power(np.float32(10000.0), np.arange(0, RDK, 2, dtype=np.float32) / np.float32(RDK))).astype(np.float32)
    pos = np.concatenate([np.arange(T), np.full(NS, PAST)]).astype(np.float32)
    ang = inv[:, None] * pos[None, :]
    cos = np.concatenate([np.cos(ang), np.cos(ang)], 0)
    sin = np.concatenate([np.sin(ang), -np.sin(ang)], 0)
    f = np.concatenate([dec.reshape(P, -1), gpow.reshape(P, -1), kdec], 1).astype(np.float32)
    rot = np.concatenate([cos, sin], 1).astype(np.float32)
    masks = []
    for l in range(LEVELS):
        h = C >> (l + 1)
        masks.append((s // (2 * h) == t // (2 * h)) & (s % (2 * h) < h) & (t % (2 * h) >= h))
    masks.append(s == t)
    m = np.stack(masks, 1).astype(np.float32)
    return ident, np.ascontiguousarray(f), np.ascontiguousarray(rot), np.ascontiguousarray(m)


def build(nc, x_prompt, x_sample, state_gla, state_ret, state_conv, state_ffn, w_mix_in, w_gla_gate_up,
          b_gla_gate, g_gla_norm, g_ret_norm, b_ret_norm, w_mix_out, w_sc_in, w_sc_dw, b_sc_dw, w_sc_out,
          ln1_g, ln1_b, w_ffn_in, w_ffn_dw, b_ffn_dw, w_ffn_out, ln2_g, ln2_b,
          c_ident, c_decay, c_rotary, c_masks,
          y_prompt, y_sample, gla_p, gla_s, ret_p, ret_s, conv_p, conv_s, ffn_p, ffn_s):
    ctx = ExitStack()
    base = nc.sbuf_base
    base += -base % 64
    room = nc.sbuf_usable_end - base - 64
    at = [base]

    def place(name, shape, dt, offset=None):
        n = int(np.prod(shape[1:])) * (1 if dt == U8 else 4)
        o = at[0] if offset is None else offset
        if offset is None:
            at[0] += n + -n % 64
        assert at[0] <= base + room and o + n <= base + room
        return nc.alloc_sbuf_tensor_at(name, shape, dt, offset=o)

    with ctx:
        slab = ctx.enter_context(nc.sbuf_tensor("slab", [P, room // 4], F32))
        B = 4 * N
        x32 = place("x32", [P, KD, N], F32)
        ATT2 = at[0]
        x_hi = place("x_hi", [P, KD, N], F32R)
        x_lo = place("x_lo", [P, KD, N], F32R)
        H = at[0]
        h_hi = place("h_hi", [P, NF, N], F32R, H)
        h_lo = place("h_lo", [P, NF, N], F32R, H + NF * B)
        at[0] = H + 2 * NF * B
        w_raw = place("w_raw", [P, 2, KD, 256], F32)
        w_hi = place("w_hi", [P, 2, KD, 256], F32R)
        w_lo = place("w_lo", [P, 2, KD, 256], F32R)

        ident = place("ident", [P, P], F32)
        ones = place("ones", [P, P], F32)
        vecs = place("vecs", [P, 5, P], F32)
        past_ffn = place("past_ffn", [P, DEPTH, NS, NU], F32)
        past_conv = place("past_conv", [P, NS, KD], F32)
        w_up = place("w_up", [RANK, 2 * P], F32, at[0])
        last_rows = place("last_rows", [P, NU, 2 + NS], F32)
        eps = place("eps", [P, 1], F32)
        eps_copy = place("eps_copy", [P, 1], F32)
        ones_one = place("ones_one", [P, 1], F32)

        z = place("z", [P, NZ, N], F32, H)
        rot = place("rot", [P, 2, N], F32, H + NZ * B)
        o_att = place("o_att", [P, KD, N], F32, H + 30 * B)
        k_tok = place("k_tok", [P, NC, 512], F32, H + 38 * B)
        log_a = place("log_a", [P, 2, N], F32, H + 38 * B + 8192)
        cum = place("cum", [P, 2, T], F32, ATT2)
        dd = place("dd", [P, 2, T], F32, ATT2 + 4096)
        q_t = place("q_t", [P, 2, T], F32, ATT2 + 8192)
        k_t = place("k_t", [P, 2, T], F32, ATT2 + 12288)
        sc = place("sc", [P, 4, T], F32, ATT2 + 16384)
        v_tok = place("v_tok", [P, NC, 512], F32, ATT2 + 24576)
        gate_t = place("gate_t", [P, 2, N], F32, ATT2 + 16384)
        gate_m = place("gate_m", [P, 2, N], F32, ATT2 + 24576)
        rot_a = place("rot_a", [P, 4, N], F32, ATT2)
        rot_b = place("rot_b", [P, 4, N], F32, ATT2 + 4 * B)
        q_dec = place("q_dec", [P, RH, T], F32, ATT2)
        x_tok = place("x_tok", [P, 5, D], F32, H + NZ * B)
        v_rows = place("v_rows", [P, 5, P], F32, H + 38 * B)
        s_rows0 = place("s_rows0", [NU, 2 * NS, P], F32, H + 38 * B + 2560)

        shared = at[0]
        masks = place("masks", [P, LEVELS + 1, P], U8)
        decay = place("decay", [P, 2 * RH * C + RH], F32)
        samp = place("samp", [P, 2, NS, DV], F32)
        s_rows1 = place("s_rows1", [NU, 2 * NS, P], F32, at[0] - 8192)
        state = place("state", [P, 2, 4, DV], F32)
        tok_s = place("tok_s", [NS, 8, P], F32)
        v_blk = place("v_blk", [NS, NS, DV], F32)
        s_rows2 = place("s_rows2", [2 * NS, KD, P], F32, at[0] - 4096)
        a_lr = place("a_lr", [RANK, N], F32, H + 32 * B)
        mask_rows = place("mask_rows", [P, LEVELS + 1, P], F32, H + 34 * B)
        e_last = place("e_last", [P, 2, NC], F32)
        a_samp = place("a_samp", [P, 2, NS], F32)
        stat = place("stat", [P, 2, N], F32, ATT2)
        stat2 = place("stat2", [P, N], F32, ATT2 + 2 * B)
        tmp_past = place("tmp_past", [P, NS, NU], F32, H + 30 * B)
        end_att = at[0]
        at[0] = shared
        tmp = place("tmp", [P, 8, N], F32)
        row_out = place("row_out", [NU, 2 + NS, P], F32)
        ln_sum = place("ln_sum", [P, N], F32)
        ln_rstd = place("ln_rstd", [P, N], F32)
        ln_sq = tmp
        y_tok = place("y_tok", [P, 2, D], F32, H)
        at[0] = max(at[0], end_att)

        ps_t = ctx.enter_context(nc.psum_tensor("ps", [P, 8 * 512], F32))
        ps = ps_t[:, :]

        def bank(b, rows=P, lo=0, n=512):
            return ps_t[0:rows, b * 512 + lo:b * 512 + lo + n]

        def acc(slot):
            o = slot * 1024 + 256
            return ps_t[:, o:o + N]

        HALVES = [(0, HA), (HA, N)]

        def acc_half(slot, half):
            lo, hi = HALVES[half]
            o = slot * 1024 + 256
            return ps_t[:, o + lo:o + hi]

        made = {}

        def sem(name):
            if name not in made:
                made[name] = ctx.enter_context(nc.semaphore(name))
            return made[name]

        def bc(ap, dim, n):
            a = ap.unsqueeze(dim)
            return a.broadcast_to([*a.shape[:dim], n, *a.shape[dim + 1:]])

        def wsrc(w, k0, k, c0, c):
            return w[k0 * P:(k0 + k) * P, c0:c0 + c].rearrange("(k p) c -> p k c", p=P)

        units = [(w_mix_in[0], 0, KD, A_LR, P)]
        for j in range(NZ // 2):
            c0 = 256 * j
            units.append((w_mix_in[0], 0, KD, c0 + (RANK if c0 >= A_LR else 0), 256))
        U_MIXIN = 0
        U_MIXOUT = len(units)
        units += [(w_mix_out[0], 0, KD, 256 * j, 256) for j in range(4)]
        U_IN, U_OUT = [0, 0], [0, 0]

        def ffn_units(l):
            U_IN[l] = len(units)
            for j in range(NF // 2):
                units.append((w_ffn_in[l], 0, KD, 256 * j, 256))
                units.append((w_ffn_in[l], 0, KD, FF + 256 * j, 256))
            U_OUT[l] = len(units)
            for j in range(4):
                for k0, k in K_GROUPS:
                    units.append((w_ffn_out[l], k0, k, 256 * j, 256))

        K_GROUPS = [(0, 8), (8, 8), (16, 6)]
        ffn_units(0)
        U_SCIN = len(units)
        for j in range(4):
            for part in range(3):
                units.append((w_sc_in[0], 0, KD, part * D + 256 * j, 256))
        U_SCOUT = len(units)
        units += [(w_sc_out[0], 0, KD, 256 * j, 256) for j in range(4)]
        ffn_units(1)
        n_units = len(units)

        Q_MIXIN = 0
        Q_MIXOUT = Q_MIXIN + 2 + NZ
        Q_IN = [Q_MIXOUT + KD, 0]
        Q_OUT = [Q_IN[0] + NU, 0]
        Q_SCIN = Q_OUT[0] + KD
        Q_SCOUT = Q_SCIN + 3 * KD
        Q_IN[1] = Q_SCOUT + KD
        Q_OUT[1] = Q_IN[1] + NU

        raw_loaded = [sem("raw_loaded0"), sem("raw_loaded1")]
        hi_made, lo_made = sem("hi_made"), sem("lo_made")
        tile0_done, unit_used, acc_free = sem("tile0_done"), sem("unit_used"), sem("acc_free")

        PR_MIXIN = 1
        PR_MIXOUT = PR_MIXIN + NZ // 2
        PR_IN = [PR_MIXOUT + 4, 0]
        PR_OUT = [PR_IN[0] + NF, 0]
        PR_SCIN = PR_OUT[0] + 4
        PR_SCOUT = PR_SCIN + 12
        PR_IN[1] = PR_SCOUT + 4
        PR_OUT[1] = PR_IN[1] + NF

        def load_unit(e, u):
            w, k0, k, c0, c = units[u]
            if u >= 2:
                e.wait_ge(lo_made, u - 1)
            e.dma_start(w_raw[:, u % 2, 0:k, 0:c],
                        w[k0 * P:(k0 + k) * P, c0:c0 + c].rearrange("(k p) c -> p k c", p=P)
                        ).then_inc(raw_loaded[u % 2], 16)

        def make_hi(e, u, par, loaded, k=KD, c=256):
            e.wait_ge(raw_loaded[par], loaded)
            if not (isinstance(u, int) and u < 2):
                e.wait_ge(unit_used, u - 1)
            e.activation(w_hi[:, par, 0:k, 0:c], w_raw[:, par, 0:k, 0:c], ACT.Copy).then_inc(hi_made, 1)

        def make_lo(e, u, par, k=KD, c=256):
            e.wait_ge(hi_made, u + 1)
            e.tensor_tensor(w_lo[:, par, 0:k, 0:c], w_raw[:, par, 0:k, 0:c],
                            w_hi[:, par, 0:k, 0:c].bitcast(F32), ALU.subtract).then_inc(lo_made, 1)

        def stage_hi(e, u):
            if u < n_units:
                make_hi(e, u, u % 2, 16 * (u // 2 + 1), units[u][2], units[u][4])

        def stage_lo(e, u):
            if u < n_units:
                make_lo(e, u, u % 2, units[u][2], units[u][4])

        def mm_tile(e, par, f, ks, xh, xl, first=True, last=True):
            for half, (lo, hi) in enumerate(HALVES):
                out = acc_half(f, half)
                for i, k in enumerate(ks):
                    wh = w_hi[:, par, i, f * P:(f + 1) * P]
                    wl = w_lo[:, par, i, f * P:(f + 1) * P]
                    e.matmul(out, wh, xh[:, k, lo:hi], start=(first and i == 0), stop=False)
                    e.matmul(out, wh, xl[:, k, lo:hi], start=False, stop=False)
                    mm = e.matmul(out, wl, xh[:, k, lo:hi], start=False, stop=(last and i == len(ks) - 1))
            return mm

        def mm_units(e, u, pr, n, par, xh, xl):
            for j in range(n):
                e.wait_ge(lo_made, u + j + 1)
                for f, done in enumerate((tile0_done, unit_used)):
                    e.wait_ge(acc_free, 2 * (pr + j) + f - 1)
                    mm_tile(e, (par + j) % 2, f, range(KD), xh, xl).then_inc(done, 1)

        def acc_wait(e, pr, u, f):
            if f == 0:
                e.wait_ge(tile0_done, pr)
            else:
                e.wait_ge(unit_used, u + 1)

        def vec(g, col, n=1):
            return vecs[:, g, col:col + n]

        def ffn_vec(l, j, tile):
            return vecs[:, 2 * l + j // 2, bass.ds((j % 2) * NU + tile, 1)]

        block = ctx.enter_context(nc.Block())

        stored = sem("stored")
        n_stored = [0]

        @block.sync
        def _(e):
            load, vec_loaded = sem("x_loaded"), sem("vec_loaded")
            e.dma_start(ident[:, :], c_ident).then_inc(load, 16)
            e.dma_start(x_tok[:, 0:4, :], x_prompt[0].rearrange("(t p) d -> p t d", p=P)).then_inc(load, 16)
            e.dma_start(x_tok[0:NS, 4, :], x_sample[:, 0, :]).then_inc(load, 16)
            load_unit(e, 0)
            load_unit(e, 1)
            def rows(g, r, src):
                n = src.shape[0]
                e.dma_start(v_rows[r:r + n, g, :], src).then_inc(vec_loaded, 16)
            for l in range(DEPTH):
                for j in range(4):
                    src = w_ffn_dw[l, j] if j < 3 else b_ffn_dw[l]
                    rows(2 * l + j // 2, (j % 2) * NU, src.rearrange("(t p) -> t p", p=P))
            for r, src in ((COL_LN1G, ln1_g), (COL_LN1B, ln1_b), (COL_LN2G, ln2_g), (COL_LN2B, ln2_b),
                           (COL_SCW, w_sc_dw[0]), (COL_SCB, b_sc_dw), (COL_BG, b_gla_gate),
                           (COL_GG, g_gla_norm), (COL_GR, g_ret_norm), (COL_BR, b_ret_norm)):
                rows(V_LN, r, src.rearrange("l (t p) -> (l t) p", p=P))
            for l, dst in ((0, s_rows0), (1, s_rows1)):
                e.dma_start(dst[:, :, :], state_ffn[l].rearrange("b j (t p) -> t (b j) p", p=P)
                            ).then_inc(sem("states_loaded"), 16)
            e.dma_start(s_rows2[:, :, :], state_conv[0].rearrange("b j (t p) -> (b j) t p", p=P)
                        ).then_inc(sem("states_loaded"), 16)
            e.dma_start(decay[:, :], c_decay).then_inc(sem("tables_loaded"), 16)
            e.dma_start(w_up[:, :], w_gla_gate_up[0]).then_inc(sem("tables_loaded"), 16)
            for l in range(DEPTH):
                e.dma_start(ffn_s[l, :, 0, :], state_ffn[l, :, 1, :]).then_inc(stored, 16)
            e.dma_start(conv_s[0, :, 0, :], state_conv[0, :, 1, :]).then_inc(stored, 16)
            n_stored[0] += 3
            e.wait_ge(sem("x_turned"), 8)
            e.dma_start(mask_rows[:, :, :], c_masks).then_inc(sem("tables_loaded"), 16)
            e.dma_start(rot[:, :, :], c_rotary).then_inc(sem("rot_loaded"), 16)
            for u in range(2, U_MIXOUT + 2):
                load_unit(e, u)
            e.wait_ge(sem("past_turned"), 3)
            for g in range(2):
                for j in range(2):
                    e.dma_start(samp[j * GDK:(j + 1) * GDK, g, :, :],
                                state_gla[0, :, 2 * g + j].rearrange("b d v -> d b v")
                                ).then_inc(sem("gla_s_loaded"), 16)
            e.wait_ge(sem("gla_state"), NC)
            for g in range(2):
                e.dma_start(gla_p[0, 0, 2 * g:2 * g + 2].rearrange("h d v -> (h d) v"),
                            state[:, (NC - 1) % 2, g, :]).then_inc(sem("gla_p_stored"), 16)
            e.wait_ge(sem("gla_s_made"), 2)
            for g in range(2):
                for j in range(2):
                    e.dma_start(gla_s[0, :, 2 * g + j].rearrange("b d v -> d b v"),
                                samp[j * GDK:(j + 1) * GDK, g, :, :]).then_inc(sem("gla_s_stored"), 16)
            e.wait_ge(sem("gla_s_stored"), 64)
            e.wait_ge(sem("gla_s_read"), 1)
            for h in range(RH):
                if h >= 2:
                    e.wait_ge(sem("ret_s_stored"), 16 * (h - 1))
                    e.wait_ge(sem("ret_s_read"), h - 1)
                e.dma_start(samp[:, h % 2, :, :], state_ret[0, :, h].rearrange("b d v -> d b v")
                            ).then_inc(sem("ret_s_loaded%d" % (h % 2)), 16)
                if h >= 1:
                    e.wait_ge(sem("ret_s_made"), h)
                    e.dma_start(ret_s[0, :, h - 1].rearrange("b d v -> d b v"),
                                samp[:, (h - 1) % 2, :, :]).then_inc(sem("ret_s_stored"), 16)
            e.wait_ge(sem("ret_s_made"), RH)
            e.dma_start(ret_s[0, :, RH - 1].rearrange("b d v -> d b v"),
                        samp[:, (RH - 1) % 2, :, :]).then_inc(sem("ret_s_stored"), 16)
            e.wait_ge(sem("ret_state"), NC)
            e.dma_start(ret_p[0, 0].rearrange("h d v -> d h v"), state[:, (NC - 1) % 2, :, :]).then_inc(stored, 16)
            n_stored[0] += 1

            def store_rows(n, tiles, p_dst, s_dst):
                e.wait_ge(sem("rows_out"), n)
                e.dma_start(p_dst.rearrange("n (t p) -> t n p", p=P), row_out[0:tiles, 0:2, :]
                            ).then_inc(sem("rows_stored"), 16)
                e.dma_start(s_dst.rearrange("b (t p) -> t b p", p=P), row_out[0:tiles, 2:2 + NS, :]
                            ).then_inc(sem("rows_stored"), 16)

            for u in range(U_MIXOUT + 2, U_OUT[0] + 3):
                load_unit(e, u)
            store_rows(1, NU, ffn_p[0, 0], ffn_s[0, :, 1, :])
            for u in range(U_OUT[0] + 3, U_SCOUT + 3):
                load_unit(e, u)
            store_rows(2, KD, conv_p[0, 0], conv_s[0, :, 1, :])
            for u in range(U_SCOUT + 3, U_OUT[1] + 3):
                load_unit(e, u)
            store_rows(3, NU, ffn_p[1, 0], ffn_s[1, :, 1, :])
            for u in range(U_OUT[1] + 3, n_units):
                load_unit(e, u)
            for j in range(5):
                e.wait_ge(sem("y_out"), j + 1)
                dst = y_prompt[0, j * P:(j + 1) * P, :] if j < 4 else y_sample[:, 0, :]
                e.dma_start(dst, y_tok[0:P if j < 4 else NS, j % 2, :]).then_inc(sem("y_stored%d" % (j % 2)), 16)
            e.wait_ge(stored, 16 * n_stored[0])
            e.wait_ge(sem("gla_p_stored"), 32)
            e.wait_ge(sem("gla_s_stored"), 64)
            e.wait_ge(sem("ret_s_stored"), 64)
            e.wait_ge(sem("rows_stored"), 96)
            e.wait_ge(sem("y_stored0"), 48)
            e.wait_ge(sem("y_stored1"), 32)

        @block.tensor
        def _(e):
            e.wait_ge(sem("x_loaded"), 48)
            for f in range(KD):
                if f >= 4:
                    e.wait_ge(sem("x_copied"), f - 3)
                for j in range(5):
                    n = P if j < 4 else NS
                    o = (f % 4) * 1024 + 256 + j * P
                    tr = e.transpose(ps_t[:, o:o + n], x_tok[0:n, j, f * P:(f + 1) * P], ident[0:n, 0:n])
                tr.then_inc(sem("x_turned"), 1)
            e.wait_ge(sem("x_copied"), KD)
            e.wait_ge(sem("x_made"), KD)
            e.wait_ge(lo_made, 1)
            mm_tile(e, 0, 0, range(KD), x_hi, x_lo).then_inc(unit_used, 1)
            with e.Fori(0, NZ // 4) as i:
                mm_units(e, 1 + 2 * i, PR_MIXIN + 2 * i, 2, 1, x_hi, x_lo)
            e.wait_ge(sem("vec_loaded"), 18 * 16)
            for g in range(5):
                n = 2 * NU if g < V_LN else N_V
                tr = e.transpose(bank(4, P, g * 88, n), v_rows[0:n, g, :], ident[0:n, 0:n])
            tr.then_inc(sem("vecs_turned"), 1)
            e.wait_ge(sem("states_loaded"), 48)
            for t in range(KD):
                tr = e.transpose(bank(7, P, t * 16, 16), s_rows2[:, t, :], ident[0:16, 0:16])
            tr.then_inc(sem("past_turned"), 1)
            for l, src in enumerate((s_rows0, s_rows1)):
                if l:
                    e.wait_ge(sem("past_made"), 2)
                for r in range(2 * NS):
                    tr = e.transpose(bank(5 + r // 8, P, (r % 8) * NU, NU), src[:, r, :], ident[0:NU, 0:NU])
                tr.then_inc(sem("past_turned"), 1)
            e.wait_ge(sem("tables_loaded"), 48)
            e.wait_ge(acc_free, 2 * PR_MIXOUT)
            for g in range(2):
                for half, (lo, hi) in enumerate(HALVES):
                    mm = e.matmul(acc_half(g, half), w_up[:, g * P:(g + 1) * P], a_lr[:, lo:hi], start=True, stop=True)
            mm.then_inc(sem("gate_summed"), 1)
            for l in range(LEVELS + 1):
                if l < LEVELS:
                    e.wait_ge(sem("level_made"), l + 1)
                if l == 0:
                    e.wait_ge(sem("past_made"), DEPTH + 1)
                    e.wait_ge(sem("vecs_made"), 1)
                else:
                    e.wait_ge(sem("level_added"), l)
                for h in range(GH):
                    p = slice((h % 2) * GDK, (h % 2 + 1) * GDK)
                    for c in range(NC):
                        t = slice(c * C, (c + 1) * C)
                        if l < LEVELS:
                            k, q = k_t[p, h // 2, t], q_t[p, h // 2, t]
                        else:
                            k, q = z[p, KG + h // 2, t], z[p, QG + h // 2, t]
                        mm = e.matmul(bank(4 + h, P, c * C, C), k, q, start=True, stop=True)
                mm.then_inc(sem("level_summed"), 1)
            e.wait_ge(sem("level_added"), LEVELS + 1)
            for c in range(NC):
                for h in range(GH):
                    tr = e.transpose(bank(4 + c, P, h * DV, DV), z[:, VG + h, c * C:(c + 1) * C], ident[:, :])
            tr.then_inc(sem("gv_turned"), 1)
            e.wait_ge(sem("gk_decayed"), 1)
            for c in range(NC):
                for g in range(2):
                    tr = e.transpose(bank(c // 2, P, (c % 2) * 256 + g * P, P), k_t[:, g, c * C:(c + 1) * C], ident[:, :])
            tr.then_inc(sem("gk_turned"), 1)
            e.wait_ge(sem("gv_copied"), 1)
            e.wait_ge(sem("gk_copied"), 1)
            e.wait_ge(sem("gq_decayed"), 1)

            def chunks(heads, state_mm, out_state, name):
                for c in range(NC):
                    t = slice(c * C, (c + 1) * C)
                    if c >= 2:
                        e.wait_ge(sem(name + "_state"), c - 1)
                    state_mm(c).then_inc(sem(name + "_inc"), 1)
                    if c:
                        e.wait_ge(sem(name + "_state"), c)
                    for h in range(heads):
                        mm = e.matmul(bank(4 + h, P, c * C, C), v_tok[:, c, h * DV:(h + 1) * DV], sc[:, h, t],
                                      start=True, stop=(c == 0))
                        if c:
                            mm = out_state(c, h, bank(4 + h, P, c * C, C), t)
                    mm.then_inc(sem(name + "_out"), 1)

            def gla_inc(c):
                for g in range(2):
                    mm = e.matmul(bank(c % 2, P, g * 256, 256), k_tok[:, c, g * P:(g + 1) * P],
                                  v_tok[:, c, g * 256:(g + 1) * 256], start=True, stop=True)
                return mm

            def gla_out(c, h, out, t):
                p = slice((h % 2) * GDK, (h % 2 + 1) * GDK)
                return e.matmul(out, state[p, (c - 1) % 2, h // 2, :], q_t[p, h // 2, t], start=False, stop=True)

            chunks(GH, gla_inc, gla_out, "gla")

            e.wait_ge(sem("gla_copied"), 1)
            for j in range(2):
                e.transpose(bank(4, NS, j * P, P), z[:, KG + j, T:N], ident[:, :])
            for j in range(4):
                tr = e.transpose(bank(5, NS, j * P, P), z[:, VG + j, T:N], ident[:, :])
            tr.then_inc(sem("gs_turned"), 1)
            e.wait_ge(sem("gs_copied"), 1)
            e.wait_ge(sem("gla_state"), NC)
            for h in range(GH):
                g, j = h // 2, h % 2
                e.wait_ge(sem("v_blk_made"), h + 1)
                for i in range(2):
                    mm = e.matmul(ps_t[j * GDK:(j + 1) * GDK, (2 * g + i) * 512:(2 * g + i + 1) * 512],
                                  tok_s[:, g, j * GDK:(j + 1) * GDK],
                                  v_blk[:, 4 * i:4 * i + 4, :], start=True, stop=True)
                mm.then_inc(sem("outer_summed"), 1)
            for g in range(2):
                e.wait_ge(sem("gla_s_made"), g + 1)
                for h in (2 * g, 2 * g + 1):
                    p = slice((h % 2) * GDK, (h % 2 + 1) * GDK)
                    for b in range(NS):
                        mm = e.matmul(bank(6 + h % 2, P, g * NS + b, 1), samp[p, g, b, :], z[p, QG + g, T + b:T + b + 1],
                                      start=True, stop=True)
            mm.then_inc(sem("gla_s_read"), 1)

            e.wait_ge(sem("rotated"), 2)
            e.wait_ge(sem("gs_out_copied"), 1)
            for h in range(RH):
                for c in range(NC):
                    t = slice(c * C, (c + 1) * C)
                    mm = e.matmul(bank(4 + h, P, c * C, C), z[:, KR + h, t], z[:, QR + h, t], start=True, stop=True)
            mm.then_inc(sem("rs_summed"), 1)
            for c in range(NC):
                for h in range(RH):
                    tr = e.transpose(bank(c, P, h * DV, DV), z[:, VR + h, c * C:(c + 1) * C], ident[:, :])
            tr.then_inc(sem("rv_turned"), 1)
            e.wait_ge(sem("rs_decayed"), 1)
            for c in range(NC):
                for h in range(RH):
                    tr = e.transpose(bank(4 + c, P, h * RDK, RDK), z[:, KR + h, c * C:(c + 1) * C], ident[:, :])
            tr.then_inc(sem("rk_turned"), 1)
            e.wait_ge(sem("rv_copied"), 1)
            e.wait_ge(sem("rk_decayed"), 1)

            def ret_inc(c):
                for h in range(RH):
                    mm = e.matmul(bank(c % 2, P, h * DV, DV), k_tok[:, c, h * RDK:(h + 1) * RDK],
                                  v_tok[:, c, h * DV:(h + 1) * DV], start=True, stop=True)
                return mm

            def ret_out(c, h, out, t):
                return e.matmul(out, state[:, (c - 1) % 2, h, :], q_dec[:, h, t], start=False, stop=True)

            chunks(RH, ret_inc, ret_out, "ret")
            e.wait_ge(sem("ret_copied"), 1)
            for j in range(4):
                e.transpose(bank(4, NS, j * P, P), z[:, KR + j, T:N], ident[:, :])
                tr = e.transpose(bank(5, NS, j * P, P), z[:, VR + j, T:N], ident[:, :])
            tr.then_inc(sem("rs_turned"), 1)
            e.wait_ge(sem("rs_copied"), 1)
            e.wait_ge(sem("ret_state"), NC)
            for h in range(RH):
                e.wait_ge(sem("v_blk_made"), GH + h + 1)
                for i in range(2):
                    mm = e.matmul(bank(2 * (h % 2) + i), tok_s[:, h, :],
                                  v_blk[:, 4 * i:4 * i + 4, :], start=True, stop=True)
                mm.then_inc(sem("outer_summed"), 1)
                e.wait_ge(sem("ret_s_made"), h + 1)
                for b in range(NS):
                    mm = e.matmul(bank(6, P, h * NS + b, 1), samp[:, h % 2, b, :], z[:, QR + h, T + b:T + b + 1],
                                  start=True, stop=True)
                mm.then_inc(sem("ret_s_read"), 1)
            e.wait_ge(sem("rs_out_copied"), 1)
            for h in range(KD):
                if h >= GH:
                    if h > GH:
                        e.wait_ge(sem("hn_centered"), h - GH)
                    for half, (lo, hi) in enumerate(HALVES):
                        mm = e.matmul(acc_half(2, half), ones[:, :], o_att[:, h, lo:hi], start=True, stop=True)
                    mm.then_inc(sem("hn_mean"), 1)
                e.wait_ge(sem("hn_squared"), h + 1)
                if h:
                    e.wait_ge(sem("hn_std"), h)
                for half, (lo, hi) in enumerate(HALVES):
                    mm = e.matmul(acc_half(3, half), ones[:, :], stat[:, 0, lo:hi], start=True, stop=True)
                mm.then_inc(sem("hn_var"), 1)

            def ln_sums(n):
                e.wait_ge(sem("ln_summed"), n + 1)
                for half, (lo, hi) in enumerate(HALVES):
                    mm = e.matmul(acc_half(2, half), ones[:, :], ln_sum[:, lo:hi], start=True, stop=True)
                mm.then_inc(sem("ln_mean"), 1)
                for f in range(KD):
                    e.wait_ge(sem("ln_squared"), KD * n + f + 1)
                    for half, (lo, hi) in enumerate(HALVES):
                        mm = e.matmul(acc_half(3, half), ones[:, :], ln_sq[:, f, lo:hi], start=(f == 0), stop=(f == KD - 1))
                mm.then_inc(sem("ln_var"), 1)

            def turn_rows(n, tiles, ready):
                e.wait_ge(*ready)
                for r in range(2 + NS):
                    tr = e.transpose(bank(4 + r // 4, tiles, (r % 4) * P, P), last_rows[:, 0:tiles, r], ident[:, :])
                tr.then_inc(sem("rows_turned"), 1)

            def project_out(pr, u, kgroups, n, xh, xl):
                per = len(kgroups)
                with e.Fori(0, 2) as i:
                    for j in range(2):
                        for g, (k0, k) in enumerate(kgroups):
                            par = (u + per * j + g) % 2
                            e.wait_ge(lo_made, u + per * j + g + 1 + 2 * per * i)
                            for f in range(2):
                                if g == 0:
                                    e.wait_ge(acc_free, 2 * (pr + j) + f - 1 + 4 * i)
                                mm = mm_tile(e, par, f, range(k0, k0 + k), xh, xl, g == 0, g == per - 1)
                                if f == 1:
                                    mm.then_inc(unit_used, 1)
                                elif g == per - 1:
                                    mm.then_inc(tile0_done, 1)

            def ffn(l):
                e.wait_ge(sem("x_made"), KD * (2 * l + 2))
                with e.Fori(0, NF // 2) as i:
                    mm_units(e, U_IN[l] + 2 * i, PR_IN[l] + 2 * i, 2, U_IN[l], x_hi, x_lo)
                turn_rows(2 * l, NU, (sem("t_made"), NU * (l + 1)))
                e.wait_ge(sem("h_made"), KD + NF * (l + 1) + KD * l)
                project_out(PR_OUT[l], U_OUT[l], K_GROUPS, 2 * l + 1, h_hi, h_lo)
                e.wait_ge(sem("rows_out"), 2 * l + 1)
                ln_sums(2 * l + 1)

            e.wait_ge(sem("h_made"), KD)
            project_out(PR_MIXOUT, U_MIXOUT, [(0, KD)], 0, h_hi, h_lo)
            ln_sums(0)
            ffn(0)
            e.wait_ge(sem("x_made"), KD * 3)
            with e.Fori(0, 6) as i:
                mm_units(e, U_SCIN + 2 * i, PR_SCIN + 2 * i, 2, U_SCIN, x_hi, x_lo)
            turn_rows(1, KD, (sem("ch_rows"), KD))
            e.wait_ge(sem("h_made"), KD + NF + KD)
            project_out(PR_SCOUT, U_SCOUT, [(0, KD)], 2, h_hi, h_lo)
            e.wait_ge(sem("rows_out"), 2)
            ln_sums(2)
            ffn(1)
            e.wait_ge(sem("x_final"), KD)
            for j in range(5):
                n = P if j < 4 else NS
                if j >= 2:
                    e.wait_ge(sem("y_out"), j - 1)
                for f in range(KD):
                    tr = e.transpose(bank(2 * (j % 2) + f // 4, n, (f % 4) * P, P), x32[:, f, j * P:j * P + n], ident[:, :])
                tr.then_inc(sem("y_turned"), 1)

        @block.scalar
        def _(e):
            step = [0]

            def link(ins):
                step[0] += 1
                ins.then_inc(sem("act_step"), 1)
                e.wait_ge(sem("act_step"), step[0])

            for f in range(KD):
                e.wait_ge(sem("x_copied"), f + 1)
                e.activation(x_hi[:, f, :], x32[:, f, :], ACT.Copy).then_inc(sem("x_hi_made"), 1)
            stage_hi(e, 0)
            stage_hi(e, 1)
            e.wait_ge(unit_used, 1)
            link(e.activation(a_lr[:, :], acc(0)[0:RANK, :], ACT.Copy))
            e.activation(a_samp[0:1, 0, 0:1], a_lr[0:1, 0:1], ACT.Copy).then_inc(acc_free, 1)
            e.activation(a_samp[0:1, 0, 1:2], a_lr[0:1, 0:1], ACT.Copy).then_inc(acc_free, 1)
            with e.Fori(0, NZ // 4) as i:
                for j in range(2):
                    u = 1 + 2 * i + j
                    make_hi(e, u + 1, j, 16 * i + 32)
                    for f in range(2):
                        acc_wait(e, PR_MIXIN + 2 * i + j, u, f)
                        e.activation(z[:, bass.ds(4 * i + 2 * j + f, 1), :], acc(f).unsqueeze(1), ACT.Copy
                                     ).then_inc(acc_free, 1)
            e.wait_ge(sem("vecs_made"), 1)
            e.wait_ge(sem("gate_summed"), 1)
            for g in range(2):
                ins = e.activation(gate_t[:, g, :], acc(g), ACT.Abs, bias=vec(V_LN, COL_BG + g))
            link(ins)
            link(e.activation(gate_t[:, :, :], gate_t[:, :, :], ACT.Exp, scale=-1.0))
            e.activation(gate_t[:, :, :], gate_t[:, :, :], ACT.Ln, bias=1.0).then_inc(sem("gate_ln"), 1)
            for l in range(LEVELS + 1):
                e.wait_ge(sem("dd_made"), l + 1)
                e.activation(dd[:, :, :], dd[:, :, :], ACT.Exp, scale=1.0 / TAU).then_inc(sem("dd_exp"), 1)
            e.wait_ge(sem("gk_decayed"), 1)
            e.activation(dd[:, :, :], cum[:, :, :], ACT.Exp, scale=1.0 / TAU)
            e.activation(e_last[:, :, :], cum[:, :, C - 1::C], ACT.Exp, scale=1.0 / TAU)
            e.activation(a_samp[:, :, :], log_a[:, :, T:N], ACT.Exp, scale=1.0 / TAU).then_inc(sem("cum_exp"), 1)
            e.wait_ge(sem("gv_turned"), 1)
            for c in range(NC):
                ins = e.activation(v_tok[:, c, :], bank(4 + c), ACT.Copy)
            ins.then_inc(sem("gv_copied"), 1)
            e.wait_ge(sem("gk_turned"), 1)
            for c in range(NC):
                ins = e.activation(k_tok[:, c, 0:256], bank(c // 2, P, (c % 2) * 256, 256), ACT.Copy)
            ins.then_inc(sem("gk_copied"), 1)
            e.wait_ge(sem("gla_out"), NC)
            for h in range(GH):
                ins = e.activation(o_att[:, h, 0:T], bank(4 + h), ACT.Copy)
            ins.then_inc(sem("gla_copied"), 1)
            e.wait_ge(sem("gs_turned"), 1)
            e.activation(tok_s[:, 0:2, :], bank(4, NS, 0, 256), ACT.Copy)
            e.activation(tok_s[:, 4:8, :], bank(5, NS), ACT.Copy).then_inc(sem("gs_copied"), 1)
            e.wait_ge(sem("gla_s_read"), 1)
            for j in range(2):
                ins = e.activation(o_att[:, j:GH:2, T:N], bank(6 + j, P, 0, 2 * NS), ACT.Copy)
            ins.then_inc(sem("gs_out_copied"), 1)
            e.activation(z[:, RG:RG + 4, :], z[:, RG:RG + 4, :], ACT.Silu)
            e.activation(z[:, GR:GR + 4, :], z[:, GR:GR + 4, :], ACT.Silu).then_inc(sem("gates_made"), 1)
            e.wait_ge(sem("rv_turned"), 1)
            for c in range(NC):
                ins = e.activation(v_tok[:, c, :], bank(c), ACT.Copy)
            ins.then_inc(sem("rv_copied"), 1)
            e.wait_ge(sem("ret_out"), NC)
            for h in range(RH):
                ins = e.activation(o_att[:, GH + h, 0:T], bank(4 + h), ACT.Copy)
            ins.then_inc(sem("ret_copied"), 1)
            e.wait_ge(sem("rs_turned"), 1)
            e.activation(tok_s[:, 0:4, :], bank(4, NS), ACT.Copy, scale=RDK ** -0.5)
            e.activation(tok_s[:, 4:8, :], bank(5, NS), ACT.Copy).then_inc(sem("rs_copied"), 1)
            e.wait_ge(sem("ret_s_read"), RH)
            link(e.activation(o_att[:, GH:KD, T:N], bank(6, P, 0, RH * NS), ACT.Copy))
            e.activation(eps_copy[:, :], eps[:, :], ACT.Copy).then_inc(sem("rs_out_copied"), 1)
            for h in range(KD):
                if h >= GH:
                    e.wait_ge(sem("hn_centered"), h - GH + 1)
                if h:
                    e.wait_ge(sem("hn_var"), h)
                e.activation(stat[:, 0, :], o_att[:, h, :], ACT.Square).then_inc(sem("hn_squared"), 1)
                e.wait_ge(sem("hn_var"), h + 1)
                if h:
                    e.wait_ge(sem("hn_done"), h)
                e.activation(stat[:, 1, :], acc(3), ACT.Sqrt, bias=eps[:, :], scale=1.0 / DV).then_inc(sem("hn_std"), 1)
            for h in range(KD):
                e.wait_ge(sem("hn_done"), h + 1)
                e.activation(h_hi[:, h, :], o_att[:, h, :], ACT.Copy).then_inc(sem("h_hi_made"), 1)

            def norm(n, g, col_g, col_b, last=False):
                for f in range(KD):
                    e.wait_ge(sem("ln_centered"), KD * n + f + 1)
                    e.activation(ln_sq[:, f, :], x32[:, f, :], ACT.Square).then_inc(sem("ln_squared"), 1)
                e.wait_ge(sem("ln_var"), n + 1)
                e.activation(ln_rstd[:, :], acc(3), ACT.Sqrt, bias=eps[:, :], scale=1.0 / D).then_inc(sem("ln_std"), 1)
                for f in range(KD):
                    e.wait_ge(sem("ln_scaled"), KD * n + f + 1)
                    ins = e.activation(x32[:, f, :], x32[:, f, :], ACT.Identity, bias=vec(g, col_b + f), scale=vec(g, col_g + f))
                    if last:
                        ins.then_inc(sem("x_final"), 1)
                        continue
                    link(ins)
                    e.activation(x_hi[:, f, :], x32[:, f, :], ACT.Copy).then_inc(sem("x_hi_made"), 1)

            def stages(u, n):
                for j in range(n):
                    stage_hi(e, u + j + 1)

            def rows_back(n, tiles):
                e.wait_ge(sem("rows_turned"), n + 1)
                if n:
                    e.wait_ge(sem("rows_stored"), 32 * n)
                for r in range(0, 2 + NS, 4):
                    k = min(4, 2 + NS - r)
                    ins = e.activation(row_out[0:tiles, r:r + k, :], bank(4 + r // 4, tiles, 0, k * P), ACT.Copy)
                ins.then_inc(sem("rows_out"), 1)

            def ffn(l):
                u, pr = U_IN[l], PR_IN[l]
                with e.Fori(0, NF // 2) as i:
                    for s in range(2):
                        make_hi(e, u + 2 * i + s + 1, (u + s + 1) % 2, 16 * ((u + s + 1) // 2 + 1) + 16 * i)
                        if s == 0:
                            e.wait_ge(sem("mul_done"), NF * l + 2 * i + 1)
                        for f in range(2):
                            tile = NF * s + 2 * i + f
                            acc_wait(e, pr + 2 * i + s, u + 2 * i + s, f)
                            e.activation(tmp[:, 2 * s + f, :], acc(f), ACT.Identity,
                                         bias=ffn_vec(l, 3, tile), scale=ffn_vec(l, 2, tile))
                            e.activation(last_rows[:, bass.ds(tile, 1), :], acc(f)[:, T - 2:N].unsqueeze(1), ACT.Copy
                                         ).then_inc(sem("t_made"), 1)
                    for f in range(2):
                        e.wait_ge(acc_free, 2 * (pr + 2 * i + 1) + f + 1)
                        e.activation(tmp[:, 4 + f, :], tmp[:, 2 + f, :], ACT.Silu).then_inc(sem("silu_done"), 1)
                    for f in range(2):
                        e.wait_ge(sem("mul_done"), NF * l + 2 * i + f + 2)
                        e.activation(h_hi[:, bass.ds(2 * i + f, 1), :], tmp[:, 6 + f:7 + f, :], ACT.Copy
                                     ).then_inc(sem("h_hi_made"), 1)
                rows_back(2 * l, NU)
                stages(U_OUT[l], 12)
                norm(2 * l + 1, V_LN, COL_LN2G + KD * l, COL_LN2B + KD * l, last=(l == 1))

            stages(U_MIXOUT, 4)
            norm(0, V_LN, COL_LN1G, COL_LN1B)
            ffn(0)
            for j in range(4):
                for part in range(3):
                    u, pr = U_SCIN + 3 * j + part, PR_SCIN + 3 * j + part
                    stage_hi(e, u + 1)
                    for f in range(2):
                        if part < 2:
                            if part == 0 and j:
                                e.wait_ge(sem("sc_gated"), 2 * j)
                            acc_wait(e, pr, u, f)
                            e.activation(tmp[:, 2 * part + f, :], acc(f), ACT.Copy).then_inc(acc_free, 1)
                        else:
                            e.wait_ge(acc_free, 2 * pr + f + 1)
                            e.activation(tmp[:, 6 + f, :], tmp[:, 4 + f, :], ACT.Identity,
                                         bias=vec(V_LN, COL_SCB + 2 * j + f), scale=vec(V_LN, COL_SCW + 2 * KD + 2 * j + f))
                            e.activation(last_rows[:, 2 * j + f, :], tmp[:, 4 + f, T - 2:N], ACT.Copy
                                         ).then_inc(sem("ch_rows"), 1)
                for f in range(2):
                    e.wait_ge(sem("sc_gated"), 2 * j + f + 1)
                    e.activation(h_hi[:, 2 * j + f, :], tmp[:, 6 + f, :], ACT.Copy).then_inc(sem("h_hi_made"), 1)
            rows_back(1, KD)
            stages(U_SCOUT, 4)
            norm(2, V_LN, COL_LN1G + KD, COL_LN1B + KD)
            ffn(1)
            for j in range(5):
                n = P if j < 4 else NS
                e.wait_ge(sem("y_turned"), j + 1)
                if j >= 2:
                    e.wait_ge(sem("y_stored%d" % (j % 2)), 16 * (j // 2))
                e.activation(y_tok[0:n, j % 2, 0:512], bank(2 * (j % 2), n), ACT.Copy)
                e.activation(y_tok[0:n, j % 2, 512:D], bank(2 * (j % 2) + 1, n), ACT.Copy).then_inc(sem("y_out"), 1)

        @block.vector
        def _(e):
            step = [0]

            def link(ins):
                step[0] += 1
                ins.then_inc(sem("vec_step"), 1)
                e.wait_ge(sem("vec_step"), step[0])

            def split_x(f, n):
                e.wait_ge(sem("x_hi_made"), n)
                e.tensor_tensor(x_lo[:, f, :], x32[:, f, :], x_hi[:, f, :].bitcast(F32), ALU.subtract
                                ).then_inc(sem("x_made"), 1)

            e.memset(ones[:, :], 1.0)
            link(e.memset(eps[:, :], EPS))
            for f in range(KD):
                e.wait_ge(sem("x_turned"), f + 1)
                o = (f % 4) * 1024 + 256
                e.tensor_copy(x32[:, f, :], ps_t[:, o:o + N]).then_inc(sem("x_copied"), 1)
            for f in range(KD):
                split_x(f, f + 1)
            stage_lo(e, 0)
            stage_lo(e, 1)
            with e.Fori(0, NZ // 4) as i:
                for j in range(2):
                    make_lo(e, 2 + 2 * i + j, j)
            e.wait_ge(sem("vecs_turned"), 1)
            for g in range(5):
                n = 2 * NU if g < V_LN else N_V
                ins = e.tensor_copy(vecs[:, g, 0:n], bank(4, P, g * 88, n))
            link(ins)
            e.wait_ge(sem("past_turned"), 1)
            def conv_past(j):
                w = vec(V_LN, COL_SCW + j * KD, KD)
                return bank(7, P, 0, KD * 16).rearrange("p (t b j) -> p b t j", b=NS, j=2)[:, :, :, j], bc(w, 1, NS)
            scratch = tmp_past[:, :, :]
            a, w = conv_past(0)
            e.tensor_tensor(past_conv[:, :, :], a, w, ALU.mult)
            a, w = conv_past(1)
            link(e.tensor_tensor(scratch[:, :, 0:KD], a, w, ALU.mult))
            link(e.tensor_tensor(past_conv[:, :, :], past_conv[:, :, :], scratch[:, :, 0:KD], ALU.add))
            e.memset(ones_one[:, :], 1.0).then_inc(sem("past_made"), 1)
            for l in range(DEPTH):
                e.wait_ge(sem("past_turned"), l + 2)
                for half in range(2):
                    b = slice(4 * half, 4 * half + 4)
                    rows = bank(5 + half, P, 0, 8 * NU).rearrange("p (b j t) -> p b j t", b=4, j=2)
                    for j, out in ((0, past_ffn[:, l, b, :]), (1, scratch[:, b, :])):
                        w = vecs[:, 2 * l, j * NU:(j + 1) * NU]
                        ins = e.tensor_tensor(out, rows[:, :, j, :], bc(w, 1, 4), ALU.mult)
                link(ins)
                e.tensor_tensor(past_ffn[:, l], past_ffn[:, l], scratch, ALU.add).then_inc(sem("past_made"), 1)
                e.wait_ge(sem("past_made"), l + 2)
            e.memset(ones_one[:, :], 1.0).then_inc(sem("vecs_made"), 1)
            e.wait_ge(sem("gate_ln"), 1)
            for g in range(2):
                ins = e.tensor_scalar(gate_m[:, g, :], acc(g), vec(V_LN, COL_BG + g), 0.0, ALU.add, ALU.min)
            link(ins)
            link(e.tensor_tensor(log_a[:, :, :], gate_m[:, :, :], gate_t[:, :, :], ALU.subtract))
            for g in range(2):
                for c in range(NC):
                    t = slice(c * C, (c + 1) * C)
                    ins = e.tensor_tensor_scan(cum[:, g, t], ones[:, :], log_a[:, g, t], 0.0, ALU.mult, ALU.add)
            link(ins)
            e.memset(sc[:, :, :], 0.0)
            e.wait_ge(sem("tables_loaded"), 48)
            e.tensor_copy(masks[:, :, :], mask_rows[:, :, :])
            e.memset(q_t[:, :, :], 0.0)
            e.memset(k_t[:, :, :], 0.0)
            e.wait_ge(acc_free, 2 * PR_MIXOUT)
            link(e.tensor_scalar(z[:, QG:QG + 2, :], z[:, QG:QG + 2, :], GDK ** -0.5, None, ALU.mult))

            def blocks(a, h):
                return a.rearrange("p g (m w) -> p g m w", w=2 * h)

            def level_diff(l):
                h = C >> (l + 1)
                c, d = blocks(cum[:, :, :], h), blocks(dd[:, :, :], h)
                ref = c[:, :, :, h - 1:h].broadcast_to([P, 2, T // (2 * h), h])
                e.tensor_tensor(d[:, :, :, 0:h], ref, c[:, :, :, 0:h], ALU.subtract)
                e.tensor_tensor(d[:, :, :, h:], c[:, :, :, h:], ref, ALU.subtract).then_inc(sem("dd_made"), 1)

            level_diff(0)
            for l in range(LEVELS + 1):
                if l < LEVELS:
                    h = C >> (l + 1)
                    e.wait_ge(sem("dd_exp"), l + 1)
                    d = blocks(dd[:, :, :], h)
                    k, q = blocks(z[:, KG:KG + 2, 0:T], h), blocks(z[:, QG:QG + 2, 0:T], h)
                    e.tensor_tensor(blocks(k_t[:, :, :], h)[:, :, :, 0:h], k[:, :, :, 0:h], d[:, :, :, 0:h], ALU.mult)
                    link(e.tensor_tensor(blocks(q_t[:, :, :], h)[:, :, :, h:], q[:, :, :, h:], d[:, :, :, h:], ALU.mult))
                    e.memset(ones_one[:, :], 1.0).then_inc(sem("level_made"), 1)
                    if l + 1 < LEVELS:
                        level_diff(l + 1)
                    else:
                        for g in range(2):
                            c = cum[:, g, :].rearrange("p (c t) -> p c t", t=C)
                            ins = e.tensor_tensor(dd[:, g, :].rearrange("p (c t) -> p c t", t=C),
                                                  c[:, :, C - 1:C].broadcast_to([P, NC, C]), c, ALU.subtract)
                        ins.then_inc(sem("dd_made"), 1)
                e.wait_ge(sem("level_summed"), l + 1)
                e.copy_predicated(sc[:, :, :].rearrange("p h (c t) -> p (h c) t", t=C), bc(masks[:, l, :], 1, GH * NC),
                                  ps_t[:, 4 * 512:8 * 512].rearrange("p (m t) -> p m t", t=C)).then_inc(sem("level_added"), 1)
                e.wait_ge(sem("level_added"), l + 1)
            e.wait_ge(sem("dd_exp"), LEVELS + 1)
            e.tensor_tensor(k_t[:, :, :], z[:, KG:KG + 2, 0:T], dd[:, :, :], ALU.mult).then_inc(sem("gk_decayed"), 1)
            e.wait_ge(sem("cum_exp"), 1)
            e.tensor_tensor(q_t[:, :, :], z[:, QG:QG + 2, 0:T], dd[:, :, :], ALU.mult).then_inc(sem("gq_decayed"), 1)
            for c in range(NC):
                e.wait_ge(sem("gla_inc"), c + 1)
                for j in range(2):
                    p = slice(j * GDK, (j + 1) * GDK)
                    for g in range(2):
                        inc = ps_t[p, (c % 2) * 512 + g * 256 + j * P:(c % 2) * 512 + g * 256 + (j + 1) * P]
                        if c == 0:
                            ins = e.tensor_copy(state[p, 0, g, :], inc)
                        else:
                            ins = e.scalar_tensor_tensor(state[p, c % 2, g, :], state[p, (c - 1) % 2, g, :],
                                                         e_last[p, g, c:c + 1], inc, ALU.mult, ALU.add)
                ins.then_inc(sem("gla_state"), 1)
                e.wait_ge(sem("gla_state"), c + 1)

            def block_values(h):
                e.tensor_tensor(v_blk[:, :, :], bc(tok_s[:, 4 + h, :], 1, NS), bc(ident[0:NS, 0:NS], 2, DV), ALU.mult
                                ).then_inc(sem("v_blk_made"), 1)

            e.wait_ge(sem("gs_copied"), 1)
            for h in range(GH):
                if h:
                    e.wait_ge(sem("outer_summed"), h)
                block_values(h)
            e.wait_ge(sem("gla_s_loaded"), 64)
            for g in range(2):
                e.wait_ge(sem("outer_summed"), 2 * g + 2)
                for b in range(NS):
                    ins = e.scalar_tensor_tensor(samp[:, g, b, :], samp[:, g, b, :], a_samp[:, g, b:b + 1],
                                                 ps_t[:, g * 1024 + b * DV:g * 1024 + (b + 1) * DV], ALU.mult, ALU.add)
                ins.then_inc(sem("gla_s_made"), 1)
            e.wait_ge(sem("rot_loaded"), 16)
            e.wait_ge(sem("gla_out"), NC)
            for t0 in (QR, KR):
                x = z[:, t0:t0 + 4, :]
                e.tensor_tensor(rot_a[:, :, :], x, bc(rot[:, 0, :], 1, 4), ALU.mult)
                e.tensor_tensor(rot_b[0:64], z[64:128, t0:t0 + 4, :], bc(rot[64:128, 1, :], 1, 4), ALU.mult)
                link(e.tensor_tensor(rot_b[64:128], z[0:64, t0:t0 + 4, :], bc(rot[0:64, 1, :], 1, 4), ALU.mult))
                e.tensor_tensor(x, rot_a[:, :, :], rot_b[:, :, :], ALU.add).then_inc(sem("rotated"), 1)
                e.wait_ge(sem("rotated"), 1 if t0 == QR else 2)

            def per_chunk(a):
                return a.rearrange("p (c t) -> p c t", t=C)

            for h in range(RH):
                ins = e.tensor_tensor(per_chunk(q_dec[:, h, :]), per_chunk(z[:, QR + h, 0:T]),
                                      bc(decay[:, RH * C + h * C:RH * C + (h + 1) * C], 1, NC), ALU.mult)
            link(ins)
            e.wait_ge(sem("rs_summed"), 1)
            for h in range(RH):
                ins = e.tensor_tensor(per_chunk(sc[:, h, :]), per_chunk(bank(4 + h)), bc(decay[:, h * C:(h + 1) * C], 1, NC), ALU.mult)
            ins.then_inc(sem("rs_decayed"), 1)
            e.wait_ge(sem("rk_turned"), 1)
            for c in range(NC):
                ins = e.tensor_tensor(k_tok[:, c, :].rearrange("p (h d) -> p h d", h=RH),
                                      bank(4 + c).rearrange("p (h d) -> p h d", h=RH),
                                      bc(decay[:, 2 * RH * C:2 * RH * C + RH], 2, RDK), ALU.mult)
            ins.then_inc(sem("rk_decayed"), 1)
            e.wait_ge(sem("gla_p_stored"), 32)
            for c in range(NC):
                e.wait_ge(sem("ret_inc"), c + 1)
                if c == 0:
                    ins = e.tensor_copy(state[:, 0, :, :], bank(0))
                else:
                    for h in range(RH):
                        ins = e.scalar_tensor_tensor(state[:, c % 2, h, :], state[:, (c - 1) % 2, h, :], GAMMA[h] ** C,
                                                     bank(c % 2, P, h * DV, DV), ALU.mult, ALU.add)
                ins.then_inc(sem("ret_state"), 1)
                e.wait_ge(sem("ret_state"), c + 1)
            e.wait_ge(sem("rs_copied"), 1)
            block_values(0)
            for h in range(RH):
                e.wait_ge(sem("outer_summed"), GH + h + 1)
                if h + 1 < RH:
                    block_values(h + 1)
                e.wait_ge(sem("ret_s_loaded%d" % (h % 2)), 16 * (h // 2 + 1))
                e.scalar_tensor_tensor(samp[:, h % 2, :, :], samp[:, h % 2, :, :], GAMMA[h],
                                       ps_t[:, (h % 2) * 1024:(h % 2 + 1) * 1024].rearrange("p (b d) -> p b d", b=NS), ALU.mult, ALU.add
                                       ).then_inc(sem("ret_s_made"), 1)
            e.wait_ge(sem("gates_made"), 1)
            for h in range(KD):
                if h >= GH:
                    e.wait_ge(sem("hn_mean"), h - GH + 1)
                    e.scalar_tensor_tensor(o_att[:, h, :], acc(2), -1.0 / DV, o_att[:, h, :], ALU.mult, ALU.add
                                           ).then_inc(sem("hn_centered"), 1)
                e.wait_ge(sem("hn_std"), h + 1)
                link(e.reciprocal(stat[:, 1, :], stat[:, 1, :]))
                gain = vec(V_LN, COL_GG) if h < GH else vec(V_LN, COL_GR + h - GH)
                link(e.scalar_tensor_tensor(o_att[:, h, :], o_att[:, h, :], gain, stat[:, 1, :], ALU.mult, ALU.mult))
                if h < GH:
                    ins = e.tensor_tensor(o_att[:, h, :], o_att[:, h, :], z[:, RG + h, :], ALU.mult)
                else:
                    ins = e.scalar_tensor_tensor(o_att[:, h, :], o_att[:, h, :], vec(V_LN, COL_BR + h - GH),
                                                 z[:, GR + h - GH, :], ALU.add, ALU.mult)
                ins.then_inc(sem("hn_done"), 1)
            e.wait_ge(sem("hn_done"), KD)
            for h in range(KD):
                e.wait_ge(sem("h_hi_made"), h + 1)
                e.tensor_tensor(h_lo[:, h, :], o_att[:, h, :], h_hi[:, h, :].bitcast(F32), ALU.subtract
                                ).then_inc(sem("h_made"), 1)

            def residual(u, pr, per):
                for j in range(4):
                    for g in range(per):
                        stage_lo(e, u + per * j + g + 1)
                    for f in range(2):
                        t = 2 * j + f
                        acc_wait(e, pr + j, u + per * j + per - 1, f)
                        e.scalar_tensor_tensor(x32[:, t, :], x32[:, t, :], ALPHA, acc(f), ALU.mult, ALU.add
                                               ).then_inc(acc_free, 1)
                        e.wait_ge(acc_free, 2 * (pr + j) + f + 1)
                        if t == 0:
                            link(e.tensor_copy(ln_sum[:, :], x32[:, 0, :]))
                        elif t < KD - 1:
                            link(e.tensor_tensor(ln_sum[:, :], ln_sum[:, :], x32[:, t, :], ALU.add))
                        else:
                            e.tensor_tensor(ln_sum[:, :], ln_sum[:, :], x32[:, t, :], ALU.add).then_inc(sem("ln_summed"), 1)

            def norm(n, last=False):
                e.wait_ge(sem("ln_mean"), n + 1)
                for f in range(KD):
                    e.scalar_tensor_tensor(x32[:, f, :], acc(2), -1.0 / D, x32[:, f, :], ALU.mult, ALU.add
                                           ).then_inc(sem("ln_centered"), 1)
                e.wait_ge(sem("ln_std"), n + 1)
                link(e.reciprocal(ln_rstd[:, :], ln_rstd[:, :]))
                for f in range(KD):
                    e.tensor_tensor(x32[:, f, :], x32[:, f, :], ln_rstd[:, :], ALU.mult).then_inc(sem("ln_scaled"), 1)
                if not last:
                    for f in range(KD):
                        split_x(f, KD * (n + 1) + f + 1)

            def ffn(l):
                u, pr = U_IN[l], PR_IN[l]
                with e.Fori(0, NF // 2) as i:
                    for s in range(2):
                        make_lo(e, u + 2 * i + s + 1, (u + s + 1) % 2)
                        for f in range(2):
                            tile = NF * s + 2 * i + f
                            n = NU * l + 4 * i + 2 * s + f
                            t = tmp[:, 2 * s + f, :]
                            e.wait_ge(sem("t_made"), n + 1)
                            e.tensor_tensor(t[:, T:N], t[:, T:N], past_col(l, tile), ALU.add)
                            e.scalar_tensor_tensor(t[:, 1:T], acc(f)[:, 0:T - 1], ffn_vec(l, 1, tile), t[:, 1:T],
                                                   ALU.mult, ALU.add).then_inc(sem("tap_done"), 1)
                            e.wait_ge(sem("tap_done"), n + 1)
                            e.scalar_tensor_tensor(t[:, 2:T], acc(f)[:, 0:T - 2], ffn_vec(l, 0, tile), t[:, 2:T],
                                                   ALU.mult, ALU.add).then_inc(acc_free, 1)
                    for f in range(2):
                        e.wait_ge(sem("silu_done"), NF * l + 2 * i + f + 1)
                        e.tensor_tensor(tmp[:, 6 + f, :], tmp[:, 4 + f, :], tmp[:, f, :], ALU.mult).then_inc(sem("mul_done"), 1)
                    for f in range(2):
                        e.wait_ge(sem("h_hi_made"), KD * (l + 1) + NF * l + 2 * i + f + 1)
                        e.tensor_tensor(h_lo[:, bass.ds(2 * i + f, 1), :], tmp[:, 6 + f:7 + f, :],
                                        h_hi[:, bass.ds(2 * i + f, 1), :].bitcast(F32), ALU.subtract).then_inc(sem("h_made"), 1)
                residual(U_OUT[l], PR_OUT[l], 3)
                norm(2 * l + 1, last=(l == 1))

            def past_col(l, tile):
                return past_ffn[:, l, :, bass.ds(tile, 1)].rearrange("p b o -> p (b o)")

            residual(U_MIXOUT, PR_MIXOUT, 1)
            norm(0)
            e.memset(ones_one[:, :], 1.0).then_inc(sem("mul_done"), 1)
            ffn(0)
            for j in range(4):
                for part in range(3):
                    u, pr = U_SCIN + 3 * j + part, PR_SCIN + 3 * j + part
                    stage_lo(e, u + 1)
                    if part == 2:
                        for f in range(2):
                            acc_wait(e, pr, u, f)
                            e.wait_ge(acc_free, 2 * pr)
                            if j:
                                e.wait_ge(sem("h_hi_made"), KD + NF + 2 * j)
                            e.tensor_tensor(tmp[:, 4 + f, :], acc(f), tmp[:, 2 + f, :], ALU.mult).then_inc(acc_free, 1)
                for f in range(2):
                    t = 2 * j + f
                    y, ch = tmp[:, 6 + f, :], tmp[:, 4 + f, :]
                    e.wait_ge(sem("ch_rows"), t + 1)
                    e.tensor_tensor(y[:, T:N], y[:, T:N], past_conv[:, :, t], ALU.add)
                    link(e.scalar_tensor_tensor(y[:, 1:T], ch[:, 0:T - 1], vec(V_LN, COL_SCW + KD + t), y[:, 1:T], ALU.mult, ALU.add))
                    link(e.scalar_tensor_tensor(y[:, 2:T], ch[:, 0:T - 2], vec(V_LN, COL_SCW + t), y[:, 2:T], ALU.mult, ALU.add))
                    e.tensor_tensor(y, y, tmp[:, f, :], ALU.mult).then_inc(sem("sc_gated"), 1)
                for f in range(2):
                    t = 2 * j + f
                    e.wait_ge(sem("h_hi_made"), KD + NF + t + 1)
                    e.tensor_tensor(h_lo[:, t, :], tmp[:, 6 + f, :], h_hi[:, t, :].bitcast(F32), ALU.subtract
                                    ).then_inc(sem("h_made"), 1)
            residual(U_SCOUT, PR_SCOUT, 1)
            norm(2)
            ffn(1)


INPUTS = ["x_prompt", "x_sample", "state_gla", "state_ret", "state_conv", "state_ffn", "w_mix_in", "w_gla_gate_up",
          "b_gla_gate", "g_gla_norm", "g_ret_norm", "b_ret_norm", "w_mix_out", "w_sc_in", "w_sc_dw", "b_sc_dw",
          "w_sc_out", "ln1_g", "ln1_b", "w_ffn_in", "w_ffn_dw", "b_ffn_dw", "w_ffn_out", "ln2_g", "ln2_b"]
OUTPUTS = [("y_prompt", (1, T, D)), ("y_sample", (NS, 1, D)), ("gla_p", (1, 1, GH, GDK, DV)),
           ("gla_s", (1, NS, GH, GDK, DV)), ("ret_p", (1, 1, RH, RDK, DV)), ("ret_s", (1, NS, RH, RDK, DV)),
           ("conv_p", (1, 1, 2, D)), ("conv_s", (1, NS, 2, D)), ("ffn_p", (DEPTH, 1, 2, 2 * FF)),
           ("ffn_s", (DEPTH, NS, 2, 2 * FF))]


def kernel(**inputs):
    import concourse.bacc as bacc
    from concourse.bass_utils import run_bass_kernel_spmd

    nc = bacc.Bacc("TRN2", target_bir_lowering=False, num_devices=1, dynamic_dma_scratch_size=1024)
    ident, decay, rotary, masks = host_constants()
    arrays = {n: np.ascontiguousarray(inputs[n]) for n in INPUTS}
    arrays |= {"c_ident": ident, "c_decay": decay, "c_rotary": rotary.reshape(P, 2, N), "c_masks": masks}
    args = {n: nc.dram_tensor("in_" + n, a.shape, mybir.dt.from_np(a.dtype), kind="ExternalInput").ap()
            for n, a in arrays.items()}
    for n, shape in OUTPUTS:
        args[n] = nc.dram_tensor("out_" + n, shape, F32, kind="ExternalOutput").ap()
    build(nc, **args)
    r = run_bass_kernel_spmd(nc, [{"in_" + n: a for n, a in arrays.items()}], core_ids=[0])
    return tuple(r.results[0]["out_" + n] for n, _ in OUTPUTS)
```

```python
from contextlib import ExitStack

import numpy as np
import concourse.bass as bass
from concourse import mybir
from concourse.alu_op_type import AluOpType as ALU

ACT = mybir.ActivationFunctionType
F32 = mybir.dt.float32
F32R = mybir.dt.float32r
U8 = mybir.dt.uint8
AX_X = mybir.AxisListType.X

P = 128
D = 1024
KD = D // P
T = 512
NS = 8
N = T + NS
HA = 256
FF = 2816
NF = FF // P
NU = 2 * NF
CW = 3
GH, GDK, DV, RH, RDK = 4, 64, 128, 4, 128
RANK = 16
C = 128
NC = T // C
LEVELS = 7
EPS = 1e-5
DEPTH = 2
PAST = 4096
ALPHA = (2 * DEPTH) ** 0.25
TAU = 16.0
A_LR = 2 * GH * GDK + GH * DV
MIX_IN = 3600

PARTS = [("q_g", 0, 2), ("k_g", 256, 2), ("v_g", 512, 4), ("q_r", 1552, 4), ("k_r", 2064, 4), ("v_r", 2576, 4),
         ("r_g", 1040, 4), ("g_r", 3088, 4)]
NZ = sum(n for _, _, n in PARTS)

V_LN = 4
COL_LN1G, COL_LN1B, COL_LN2G, COL_LN2B = 0, 16, 32, 48
COL_SCW, COL_SCB, COL_BG, COL_GG, COL_GR, COL_BR = 64, 88, 96, 98, 99, 103
N_V = 107

GAMMA = [1.0 - 2.0 ** (-5.0 - h) for h in range(RH)]


def host_constants():
    ident = np.eye(P, dtype=np.float32)
    s = np.arange(C)[:, None]
    t = np.arange(C)[None, :]
    g = np.array(GAMMA, np.float64)
    dec = np.stack([np.where(s <= t, np.power(x, (t - s).astype(np.float64)), 0.0) * RDK ** -0.5 for x in g], 1)
    gpow = np.broadcast_to(np.power(g[:, None], np.arange(1, C + 1)[None, :])[None], (P, RH, C))
    kdec = np.power(g[None, :], (C - 1 - np.arange(C))[:, None].astype(np.float64)) * RDK ** -0.5
    inv = (np.float32(1.0) / np.power(np.float32(10000.0), np.arange(0, RDK, 2, dtype=np.float32) / np.float32(RDK))).astype(np.float32)
    pos = np.concatenate([np.arange(T), np.full(NS, PAST)]).astype(np.float32)
    ang = inv[:, None] * pos[None, :]
    cos = np.concatenate([np.cos(ang), np.cos(ang)], 0)
    sin = np.concatenate([np.sin(ang), -np.sin(ang)], 0)
    f = np.concatenate([dec.reshape(P, -1), gpow.reshape(P, -1), kdec], 1).astype(np.float32)
    rot = np.concatenate([cos, sin], 1).astype(np.float32)
    masks = []
    for l in range(LEVELS):
        h = C >> (l + 1)
        masks.append((s // (2 * h) == t // (2 * h)) & (s % (2 * h) < h) & (t % (2 * h) >= h))
    masks.append(s == t)
    m = np.stack(masks, 1).astype(np.float32)
    return ident, np.ascontiguousarray(f), np.ascontiguousarray(rot), np.ascontiguousarray(m)


def build(nc, x_prompt, x_sample, state_gla, state_ret, state_conv, state_ffn, w_mix_in, w_gla_gate_up,
          b_gla_gate, g_gla_norm, g_ret_norm, b_ret_norm, w_mix_out, w_sc_in, w_sc_dw, b_sc_dw, w_sc_out,
          ln1_g, ln1_b, w_ffn_in, w_ffn_dw, b_ffn_dw, w_ffn_out, ln2_g, ln2_b,
          c_ident, c_decay, c_rotary, c_masks,
          y_prompt, y_sample, gla_p, gla_s, ret_p, ret_s, conv_p, conv_s, ffn_p, ffn_s):
    ctx = ExitStack()
    base = nc.sbuf_base
    base += -base % 64
    room = nc.sbuf_usable_end - base - 64
    at = [base]

    def place(name, shape, dt, offset=None):
        n = int(np.prod(shape[1:])) * (1 if dt == U8 else 4)
        o = at[0] if offset is None else offset
        if offset is None:
            at[0] += n + -n % 64
        assert at[0] <= base + room and o + n <= base + room
        return nc.alloc_sbuf_tensor_at(name, shape, dt, offset=o)

    with ctx:
        slab = ctx.enter_context(nc.sbuf_tensor("slab", [P, room // 4], F32))
        B = 4 * N
        x32 = place("x32", [P, KD, N], F32)
        x_hi = place("x_hi", [P, KD, N], F32R)
        x_lo = place("x_lo", [P, KD, N], F32R)
        H = at[0]
        h_hi = place("h_hi", [P, NF, N], F32R, H)
        h_lo = place("h_lo", [P, NF, N], F32R, H + NF * B)
        at[0] = H + 2 * NF * B
        w_raw = place("w_raw", [P, 2, KD, 256], F32)
        w_hi = place("w_hi", [P, 2, KD, 256], F32R)
        w_lo = place("w_lo", [P, 2, KD, 256], F32R)

        ident = place("ident", [P, P], F32)
        ones = place("ones", [P, P], F32)
        vecs = place("vecs", [P, 5, P], F32)
        past_ffn = place("past_ffn", [P, DEPTH, NS, NU], F32)
        past_conv = place("past_conv", [P, NS, KD], F32)
        w_up = place("w_up", [RANK, 2 * P], F32, at[0])
        last_rows = place("last_rows", [P, NU, 2 + NS], F32)
        eps = place("eps", [P, 1], F32)
        eps_copy = place("eps_copy", [P, 1], F32)
        ones_one = place("ones_one", [P, 1], F32)

        def slot(name, first, shape):
            return place(name, shape, F32, H + first * B)

        zt = {"q_g": slot("q_g", 0, [P, 2, N]), "k_g": slot("k_g", 2, [P, 2, N]), "q_r": slot("q_r", 4, [P, 4, N]),
              "v_g": slot("v_g", 8, [P, 4, N]), "v_r": slot("v_r", 12, [P, 4, N]), "r_g": slot("r_g", 16, [P, 4, N]),
              "k_r": slot("k_r", 22, [P, 4, N]), "g_r": slot("g_r", 30, [P, 4, N])}
        q_g, k_g, v_g, r_g, q_r, k_r, v_r, g_r = (zt[n] for n in ("q_g", "k_g", "v_g", "r_g", "q_r", "k_r", "v_r", "g_r"))
        o_att = [v_g[:, h, :] for h in range(GH)] + [v_r[:, h, :] for h in range(RH)]
        cum = slot("cum", 16, [P, 2, T])
        dd = slot("dd", 18, [P, 2, T])
        q_t = slot("q_t", 30, [P, 2, T])
        k_t = slot("k_t", 32, [P, 2, T])
        q_dec = slot("q_dec", 30, [P, RH, T])
        rot = slot("rot", 20, [P, 2, N])
        sc = slot("sc", 26, [P, 4, T])
        gate_t = slot("gate_t", 26, [P, 2, N])
        v_tok = slot("v_tok", 34, [P, NC, 512])
        gate_m = slot("gate_m", 34, [P, 2, N])
        k_tok = slot("k_tok", 38, [P, NC, 512])
        log_a = slot("log_a", 42, [P, 2, N])
        rot_t = slot("rot_t", 42, [P, 2, N])
        sq = slot("sq", 42, [P, 2, N])
        tok_r = place("tok_r", [NS, 8, P], F32, H + 38 * B)
        v_blk2 = place("v_blk2", [NS, NS, DV], F32, H + 34 * B)
        x_tok = slot("x_tok", 8, [P, 5, D])
        v_rows = slot("v_rows", 34, [P, 5, P])
        s_rows0 = place("s_rows0", [NU, 2 * NS, P], F32, H + 34 * B + 2560)
        past_t = slot("past_t", 22, [P, NS, NU])
        a_lr = place("a_lr", [RANK, N], F32, H + 24 * B)
        mask_rows = slot("mask_rows", 40, [P, LEVELS + 1, P])

        shared = at[0]
        masks = place("masks", [P, LEVELS + 1, P], U8)
        decay = place("decay", [P, 2 * RH * C + RH], F32)
        samp = place("samp", [P, 2, NS, DV], F32)
        s_rows1 = place("s_rows1", [NU, 2 * NS, P], F32, at[0] - 8192)
        state = place("state", [P, 2, 4, DV], F32)
        state_g = place("state_g", [P, NC, 2, DV], F32, at[0] - 4096)
        tok_s = place("tok_s", [NS, 8, P], F32)
        v_blk = place("v_blk", [NS, NS, DV], F32)
        s_rows2 = place("s_rows2", [2 * NS, KD, P], F32, at[0] - 4096)
        e_last = place("e_last", [P, 2, NC], F32)
        a_samp = place("a_samp", [P, 2, NS], F32)
        inv = place("inv", [P, KD, 5], F32)
        end_att = at[0]
        at[0] = shared
        tmp = place("tmp", [P, 8, N], F32)
        row_out = place("row_out", [NU, 2 + NS, P], F32)
        ln_sum = place("ln_sum", [P, N], F32)
        ln_inv = place("ln_inv", [P, 2, 5], F32)
        ln_var = place("ln_var", [P, 3, 5], F32)
        ln_sq, ln_s1, ln_s2 = tmp[:, 0:4, :], tmp[:, 4, :], tmp[:, 5, :]
        y_tok = place("y_tok", [P, 2, D], F32, H)
        at[0] = max(at[0], end_att)

        ps_t = ctx.enter_context(nc.psum_tensor("ps", [P, 8 * 512], F32))
        ps = ps_t[:, :]

        def bank(b, rows=P, lo=0, n=512):
            return ps_t[0:rows, b * 512 + lo:b * 512 + lo + n]

        def acc(slot):
            o = slot * 1024 + 256
            return ps_t[:, o:o + N]

        HALVES = [(0, HA), (HA, N)]

        def acc_half(slot, half):
            lo, hi = HALVES[half]
            o = slot * 1024 + 256
            return ps_t[:, o + lo:o + hi]

        made = {}

        def sem(name):
            if name not in made:
                made[name] = ctx.enter_context(nc.semaphore(name))
            return made[name]

        def bc(ap, dim, n):
            a = ap.unsqueeze(dim)
            return a.broadcast_to([*a.shape[:dim], n, *a.shape[dim + 1:]])

        def wsrc(w, k0, k, c0, c):
            return w[k0 * P:(k0 + k) * P, c0:c0 + c].rearrange("(k p) c -> p k c", p=P)

        units = [(w_mix_in[0], 0, KD, A_LR, P)]
        z_of = [None]
        for name, c0, n in PARTS:
            for j in range(0, n, 2):
                units.append((w_mix_in[0], 0, KD, c0 + j * P, 256))
                z_of.append((name, j))
        U_MIXOUT = len(units)
        units += [(w_mix_out[0], 0, KD, 256 * j, 256) for j in range(4)]
        U_IN, U_OUT = [0, 0], [0, 0]

        def ffn_units(l):
            U_IN[l] = len(units)
            for j in range(NF // 2):
                units.append((w_ffn_in[l], 0, KD, 256 * j, 256))
                units.append((w_ffn_in[l], 0, KD, FF + 256 * j, 256))
            U_OUT[l] = len(units)
            for j in range(4):
                for k0, k in K_GROUPS:
                    units.append((w_ffn_out[l], k0, k, 256 * j, 256))

        K_GROUPS = [(0, 8), (8, 8), (16, 6)]
        ffn_units(0)
        U_SCIN = len(units)
        for j in range(4):
            for part in range(3):
                units.append((w_sc_in[0], 0, KD, part * D + 256 * j, 256))
        U_SCOUT = len(units)
        units += [(w_sc_out[0], 0, KD, 256 * j, 256) for j in range(4)]
        ffn_units(1)
        n_units = len(units)

        Q_MIXIN = 0
        Q_MIXOUT = Q_MIXIN + 2 + NZ
        Q_IN = [Q_MIXOUT + KD, 0]
        Q_OUT = [Q_IN[0] + NU, 0]
        Q_SCIN = Q_OUT[0] + KD
        Q_SCOUT = Q_SCIN + 3 * KD
        Q_IN[1] = Q_SCOUT + KD
        Q_OUT[1] = Q_IN[1] + NU

        raw_loaded = [sem("raw_loaded0"), sem("raw_loaded1")]
        hi_made, lo_made = sem("hi_made"), sem("lo_made")
        tile0_done, unit_used, acc_free = sem("tile0_done"), sem("unit_used"), sem("acc_free")

        PR_MIXIN = 1
        PR_MIXOUT = PR_MIXIN + NZ // 2
        PR_IN = [PR_MIXOUT + 4, 0]
        PR_OUT = [PR_IN[0] + NF, 0]
        PR_SCIN = PR_OUT[0] + 4
        PR_SCOUT = PR_SCIN + 12
        PR_IN[1] = PR_SCOUT + 4
        PR_OUT[1] = PR_IN[1] + NF

        def load_unit(e, u):
            w, k0, k, c0, c = units[u]
            if u >= 2:
                e.wait_ge(lo_made, u - 1)
            e.dma_start(w_raw[:, u % 2, 0:k, 0:c],
                        w[k0 * P:(k0 + k) * P, c0:c0 + c].rearrange("(k p) c -> p k c", p=P)
                        ).then_inc(raw_loaded[u % 2], 16)

        def make_hi(e, u, par, loaded, k=KD, c=256):
            e.wait_ge(raw_loaded[par], loaded)
            if not (isinstance(u, int) and u < 2):
                e.wait_ge(unit_used, u - 1)
            e.activation(w_hi[:, par, 0:k, 0:c], w_raw[:, par, 0:k, 0:c], ACT.Copy).then_inc(hi_made, 1)

        def make_lo(e, u, par, k=KD, c=256):
            e.wait_ge(hi_made, u + 1)
            e.tensor_tensor(w_lo[:, par, 0:k, 0:c], w_raw[:, par, 0:k, 0:c],
                            w_hi[:, par, 0:k, 0:c].bitcast(F32), ALU.subtract).then_inc(lo_made, 1)

        def stage_hi(e, u):
            if u < n_units:
                make_hi(e, u, u % 2, 16 * (u // 2 + 1), units[u][2], units[u][4])

        def stage_lo(e, u):
            if u < n_units:
                make_lo(e, u, u % 2, units[u][2], units[u][4])

        def mm_tile(e, par, f, ks, xh, xl, first=True, last=True):
            for half, (lo, hi) in enumerate(HALVES):
                out = acc_half(f, half)
                for i, k in enumerate(ks):
                    wh = w_hi[:, par, i, f * P:(f + 1) * P]
                    wl = w_lo[:, par, i, f * P:(f + 1) * P]
                    e.matmul(out, wh, xh[:, k, lo:hi], start=(first and i == 0), stop=False)
                    e.matmul(out, wh, xl[:, k, lo:hi], start=False, stop=False)
                    mm = e.matmul(out, wl, xh[:, k, lo:hi], start=False, stop=(last and i == len(ks) - 1))
            return mm

        def mm_units(e, u, pr, n, par, xh, xl):
            for j in range(n):
                e.wait_ge(lo_made, u + j + 1)
                for f, done in enumerate((tile0_done, unit_used)):
                    e.wait_ge(acc_free, 2 * (pr + j) + f - 1)
                    mm_tile(e, (par + j) % 2, f, range(KD), xh, xl).then_inc(done, 1)

        def acc_wait(e, pr, u, f):
            if f == 0:
                e.wait_ge(tile0_done, pr)
            else:
                e.wait_ge(unit_used, u + 1)

        def vec(g, col, n=1):
            return vecs[:, g, col:col + n]

        def ffn_vec(l, j, tile):
            return vecs[:, 2 * l + j // 2, bass.ds((j % 2) * NU + tile, 1)]

        block = ctx.enter_context(nc.Block())

        v_blocks = [v_blk, v_blk2]
        stored = sem("stored")
        n_stored = [0]

        @block.sync
        def _(e):
            load, vec_loaded = sem("x_loaded"), sem("vec_loaded")
            e.dma_start(ident[:, :], c_ident).then_inc(load, 16)
            e.dma_start(x_tok[:, 0:4, :], x_prompt[0].rearrange("(t p) d -> p t d", p=P)).then_inc(load, 16)
            e.dma_start(x_tok[0:NS, 4, :], x_sample[:, 0, :]).then_inc(load, 16)
            load_unit(e, 0)
            load_unit(e, 1)
            def rows(g, r, src):
                n = src.shape[0]
                e.dma_start(v_rows[r:r + n, g, :], src).then_inc(vec_loaded, 16)
            for l in range(DEPTH):
                for j in range(4):
                    src = w_ffn_dw[l, j] if j < 3 else b_ffn_dw[l]
                    rows(2 * l + j // 2, (j % 2) * NU, src.rearrange("(t p) -> t p", p=P))
            for r, src in ((COL_LN1G, ln1_g), (COL_LN1B, ln1_b), (COL_LN2G, ln2_g), (COL_LN2B, ln2_b),
                           (COL_SCW, w_sc_dw[0]), (COL_SCB, b_sc_dw), (COL_BG, b_gla_gate),
                           (COL_GG, g_gla_norm), (COL_GR, g_ret_norm), (COL_BR, b_ret_norm)):
                rows(V_LN, r, src.rearrange("l (t p) -> (l t) p", p=P))
            for l, dst in ((0, s_rows0), (1, s_rows1)):
                e.dma_start(dst[:, :, :], state_ffn[l].rearrange("b j (t p) -> t (b j) p", p=P)
                            ).then_inc(sem("states_loaded"), 16)
            e.dma_start(s_rows2[:, :, :], state_conv[0].rearrange("b j (t p) -> (b j) t p", p=P)
                        ).then_inc(sem("states_loaded"), 16)
            e.dma_start(decay[:, :], c_decay).then_inc(sem("tables_loaded"), 16)
            e.dma_start(w_up[:, :], w_gla_gate_up[0]).then_inc(sem("tables_loaded"), 16)
            for l in range(DEPTH):
                e.dma_start(ffn_s[l, :, 0, :], state_ffn[l, :, 1, :]).then_inc(stored, 16)
            e.dma_start(conv_s[0, :, 0, :], state_conv[0, :, 1, :]).then_inc(stored, 16)
            n_stored[0] += 3
            e.wait_ge(sem("x_turned"), 8)
            e.dma_start(mask_rows[:, :, :], c_masks).then_inc(sem("tables_loaded"), 16)
            e.dma_start(rot[:, :, :], c_rotary).then_inc(sem("rot_loaded"), 16)
            def store_rows(n, tiles, p_dst, s_dst):
                e.wait_ge(sem("rows_out"), n)
                e.dma_start(p_dst.rearrange("n (t p) -> t n p", p=P), row_out[0:tiles, 0:2, :]
                            ).then_inc(sem("rows_stored"), 16)
                e.dma_start(s_dst.rearrange("b (t p) -> t b p", p=P), row_out[0:tiles, 2:2 + NS, :]
                            ).then_inc(sem("rows_stored"), 16)

            for u in range(2, U_OUT[0] + 3):
                load_unit(e, u)
            store_rows(1, NU, ffn_p[0, 0], ffn_s[0, :, 1, :])
            for u in range(U_OUT[0] + 3, U_SCOUT + 3):
                load_unit(e, u)
            store_rows(2, KD, conv_p[0, 0], conv_s[0, :, 1, :])
            for u in range(U_SCOUT + 3, U_OUT[1] + 3):
                load_unit(e, u)
            store_rows(3, NU, ffn_p[1, 0], ffn_s[1, :, 1, :])
            for u in range(U_OUT[1] + 3, n_units):
                load_unit(e, u)
            for j in range(5):
                e.wait_ge(sem("y_out"), j + 1)
                dst = y_prompt[0, j * P:(j + 1) * P, :] if j < 4 else y_sample[:, 0, :]
                e.dma_start(dst, y_tok[0:P if j < 4 else NS, j % 2, :]).then_inc(sem("y_stored%d" % (j % 2)), 16)
            e.wait_ge(stored, 16 * n_stored[0])
            e.wait_ge(sem("rows_stored"), 96)
            e.wait_ge(sem("y_stored0"), 48)
            e.wait_ge(sem("y_stored1"), 32)

        @block.tensor
        def _(e):
            e.wait_ge(sem("x_loaded"), 48)
            for f in range(KD):
                if f >= 4:
                    e.wait_ge(sem("x_copied"), f - 3)
                for j in range(5):
                    n = P if j < 4 else NS
                    o = (f % 4) * 1024 + 256 + j * P
                    tr = e.transpose(ps_t[:, o:o + n], x_tok[0:n, j, f * P:(f + 1) * P], ident[0:n, 0:n])
                tr.then_inc(sem("x_turned"), 1)
            e.wait_ge(sem("x_copied"), KD)
            e.wait_ge(sem("x_made"), KD)
            e.wait_ge(lo_made, 1)
            mm_tile(e, 0, 0, range(KD), x_hi, x_lo).then_inc(unit_used, 1)
            e.wait_ge(sem("vec_loaded"), 18 * 16)
            for g in range(5):
                n = 2 * NU if g < V_LN else N_V
                tr = e.transpose(bank(4, P, g * 88, n), v_rows[0:n, g, :], ident[0:n, 0:n])
            tr.then_inc(sem("vecs_turned"), 1)
            e.wait_ge(sem("states_loaded"), 48)
            for t in range(KD):
                tr = e.transpose(bank(7, P, t * 16, 16), s_rows2[:, t, :], ident[0:16, 0:16])
            tr.then_inc(sem("past_turned"), 1)
            for l, src in enumerate((s_rows0, s_rows1)):
                if l:
                    e.wait_ge(sem("past_made"), 2)
                for r in range(2 * NS):
                    tr = e.transpose(bank(5 + r // 8, P, (r % 8) * NU, NU), src[:, r, :], ident[0:NU, 0:NU])
                tr.then_inc(sem("past_turned"), 1)
            def unit_tile(u, f):
                if f == 0:
                    e.wait_ge(lo_made, u + 1)
                e.wait_ge(acc_free, 2 * u + f - 1)
                mm_tile(e, u % 2, f, range(KD), x_hi, x_lo).then_inc((tile0_done, unit_used)[f], 1)

            unit_tile(1, 0)
            unit_tile(1, 1)
            e.wait_ge(sem("tables_loaded"), 48)
            e.wait_ge(sem("vecs_made"), 1)
            e.wait_ge(sem("past_made"), DEPTH + 1)
            for g in range(2):
                for half, (lo, hi) in enumerate(HALVES):
                    mm = e.matmul(acc_half(2 + g, half), w_up[:, g * P:(g + 1) * P], a_lr[:, lo:hi], start=True, stop=True)
            mm.then_inc(sem("gate_summed"), 1)
            unit_tile(2, 0)
            unit_tile(2, 1)

            def level(n):
                if n == 0:
                    e.wait_ge(sem("gate_read"), 1)
                    e.wait_ge(sem("q_scaled"), 1)
                else:
                    e.wait_ge(sem("level_made"), n)
                    e.wait_ge(sem("level_added"), n)
                for h in range(GH):
                    p = slice((h % 2) * GDK, (h % 2 + 1) * GDK)
                    for c in range(NC):
                        t = slice(c * C, (c + 1) * C)
                        k, q = (k_t, q_t) if n else (k_g, q_g)
                        mm = e.matmul(bank(4 + h, P, c * C, C), k[p, h // 2, t], q[p, h // 2, t], start=True, stop=True)
                mm.then_inc(sem("level_summed"), 1)

            def gla_values():
                e.wait_ge(sem("level_added"), LEVELS + 1)
                for c in range(NC):
                    for h in range(GH):
                        tr = e.transpose(bank(4 + c, P, h * DV, DV), v_g[:, h, c * C:(c + 1) * C], ident[:, :])
                tr.then_inc(sem("gv_turned"), 1)

            def gla_keys():
                e.wait_ge(sem("gk_decayed"), 1)
                e.wait_ge(sem("gv_copied"), 1)
                for c in range(NC):
                    for g in range(2):
                        tr = e.transpose(bank(4 + c // 2, P, (c % 2) * 256 + g * P, P), k_t[:, g, c * C:(c + 1) * C], ident[:, :])
                tr.then_inc(sem("gk_turned"), 1)

            def gla_increments(cs):
                e.wait_ge(sem("gk_copied"), 1)
                for c in cs:
                    if c >= 2:
                        e.wait_ge(sem("gla_state"), c - 1)
                    for g in range(2):
                        mm = e.matmul(bank(6 + c % 2, P, g * 256, 256), k_tok[:, c, g * P:(g + 1) * P],
                                      v_tok[:, c, g * 256:(g + 1) * 256], start=True, stop=True)
                    mm.then_inc(sem("gla_inc"), 1)

            def gla_outputs():
                e.wait_ge(sem("gq_decayed"), 1)
                e.wait_ge(sem("gla_state"), NC)
                for h in range(GH):
                    p = slice((h % 2) * GDK, (h % 2 + 1) * GDK)
                    for c in range(NC):
                        t = slice(c * C, (c + 1) * C)
                        out = bank(4 + h, P, c * C, C)
                        mm = e.matmul(out, v_tok[:, c, h * DV:(h + 1) * DV], sc[:, h, t], start=True, stop=(c == 0))
                        if c:
                            mm = e.matmul(out, state_g[p, c - 1, h // 2, :], q_t[p, h // 2, t], start=False, stop=True)
                mm.then_inc(sem("gla_out"), 1)

            def ret_scores():
                e.wait_ge(sem("gla_copied"), 1)
                e.wait_ge(sem("rotated"), 2 * RH)
                for h in range(RH):
                    for c in range(NC):
                        t = slice(c * C, (c + 1) * C)
                        mm = e.matmul(bank(4 + h, P, c * C, C), k_r[:, h, t], q_r[:, h, t], start=True, stop=True)
                mm.then_inc(sem("rs_summed"), 1)

            def ret_keys():
                e.wait_ge(sem("rs_decayed"), 1)
                for c in range(NC):
                    for h in range(RH):
                        tr = e.transpose(bank(4 + c, P, h * RDK, RDK), k_r[:, h, c * C:(c + 1) * C], ident[:, :])
                tr.then_inc(sem("rk_turned"), 1)

            def gla_samples_turn():
                e.wait_ge(sem("rk_decayed"), 1)
                for j in range(2):
                    e.transpose(bank(4, NS, j * P, P), k_g[:, j, T:N], ident[:, :])
                for j in range(4):
                    tr = e.transpose(bank(5, NS, j * P, P), v_g[:, j, T:N], ident[:, :])
                tr.then_inc(sem("gs_turned"), 1)

            def ret_values():
                e.wait_ge(sem("gs_copied"), 1)
                e.wait_ge(acc_free, 2 * 11)
                for c in range(NC):
                    for h in range(RH):
                        tr = e.transpose(bank(4 + c, P, h * DV, DV), v_r[:, h, c * C:(c + 1) * C], ident[:, :])
                tr.then_inc(sem("rv_turned"), 1)

            def ret_chunks(cs):
                e.wait_ge(sem("rv_copied"), 1)
                for c in cs:
                    t = slice(c * C, (c + 1) * C)
                    if c >= 2:
                        e.wait_ge(sem("ret_state"), c - 1)
                    for h in range(RH):
                        mm = e.matmul(bank(6 + c % 2, P, h * DV, DV), k_tok[:, c, h * RDK:(h + 1) * RDK],
                                      v_tok[:, c, h * DV:(h + 1) * DV], start=True, stop=True)
                    mm.then_inc(sem("ret_inc"), 1)
                    if c:
                        e.wait_ge(sem("ret_state"), c)
                    if c >= 2:
                        e.wait_ge(sem("ret_copied"), c - 1)
                    for h in range(RH):
                        out = bank(4 + c % 2, P, h * C, C)
                        mm = e.matmul(out, v_tok[:, c, h * DV:(h + 1) * DV], sc[:, h, t], start=True, stop=(c == 0))
                        if c:
                            mm = e.matmul(out, state[:, (c - 1) % 2, h, :], q_dec[:, h, t], start=False, stop=True)
                    mm.then_inc(sem("ret_out"), 1)

            def ret_samples_turn():
                e.wait_ge(sem("ret_copied"), NC)
                e.wait_ge(sem("ret_state"), NC)
                for j in range(4):
                    e.transpose(bank(6, NS, j * P, P), k_r[:, j, T:N], ident[:, :])
                    tr = e.transpose(bank(7, NS, j * P, P), v_r[:, j, T:N], ident[:, :])
                tr.then_inc(sem("rs_turned"), 1)

            def outer(i):
                b = 4 + 2 * (i % 2)
                e.wait_ge(sem("rs_copied"), 1)
                if i >= 2:
                    e.wait_ge(sem("samp_out"), i - 1)
                for h in ((2 * i, 2 * i + 1) if i < 2 else (i + 2,)):
                    e.wait_ge(sem("v_blk_made"), h + 1)
                    for half in range(2):
                        rhs = v_blocks[h % 2][:, 4 * half:4 * half + 4, :]
                        if i < 2:
                            j = h % 2
                            mm = e.matmul(ps_t[j * GDK:(j + 1) * GDK, (b + half) * 512:(b + half + 1) * 512],
                                          tok_s[:, i, j * GDK:(j + 1) * GDK], rhs, start=True, stop=True)
                        else:
                            mm = e.matmul(bank(b + half), tok_r[:, i - 2, :], rhs, start=True, stop=True)
                    mm.then_inc(sem("outer_summed"), 1)

            def sample_out(i):
                b = 4 + 2 * (i % 2)
                e.wait_ge(sem("samp_made"), i + 1)
                if i < 2:
                    for j in range(2):
                        p = slice(j * GDK, (j + 1) * GDK)
                        for s in range(NS):
                            mm = e.matmul(bank(b + j, P, s, 1), samp[p, i, s, :], q_g[p, i, T + s:T + s + 1], start=True, stop=True)
                else:
                    for s in range(NS):
                        mm = e.matmul(bank(b, P, s, 1), samp[:, i % 2, s, :], q_r[:, i - 2, T + s:T + s + 1], start=True, stop=True)
                mm.then_inc(sem("samp_read"), 1)

            between = [[lambda n=n: level(n)] for n in range(LEVELS + 1)] + [
                [gla_values], [gla_keys], [lambda: gla_increments((0, 1))], [lambda: gla_increments((2, 3))],
                [gla_outputs], [ret_scores], [ret_keys], [gla_samples_turn], [ret_values],
                [lambda: ret_chunks((0, 1))], [lambda: ret_chunks((2, 3))],
                [ret_samples_turn, lambda: outer(0)],
                [lambda: outer(1), lambda: sample_out(0)], [lambda: outer(2), lambda: sample_out(1)],
                [lambda: outer(3), lambda: sample_out(2)], [lambda: outer(4), lambda: sample_out(3)]]
            for n, pieces in enumerate(between):
                unit_tile(3 + n // 2, n % 2)
                for piece in pieces:
                    piece()
            outer(5)
            sample_out(4)
            sample_out(5)

            def token_sums(out, squares, start=True, stop=True):
                for j in range(5):
                    t0 = j * P if j < 4 else N - P
                    mm = e.matmul(out[:, j:j + 1], squares[:, t0:t0 + P], ones[:, 0:1], start=(start and j == 0), stop=stop,
                                  skip_group_check=True)
                return mm

            def spread(slot_, inv_):
                for j in range(5):
                    n = P if j < 4 else NS
                    o = slot_ * 1024 + 256 + j * P
                    mm = e.matmul(ps_t[:, o:o + n], inv_[:, j:j + 1].broadcast_to([P, P]), ident[:, P - n:P],
                                  start=True, stop=True)
                return mm

            e.wait_ge(acc_free, 2 * PR_MIXOUT)
            for grp in range(2):
                if grp:
                    e.wait_ge(sem("samp_out"), 2 + RH)
                for h in range(4 * grp, 4 * grp + 4):
                    if grp:
                        if h > GH:
                            e.wait_ge(sem("hn_centered"), h - GH)
                        else:
                            e.wait_ge(sem("hn_done"), GH)
                        for half, (lo, hi) in enumerate(HALVES):
                            mm = e.matmul(acc_half(0, half), ones[:, :], o_att[h][:, lo:hi], start=True, stop=True)
                        mm.then_inc(sem("hn_mean"), 1)
                    e.wait_ge(sem("hn_squared"), h + 1)
                    token_sums(bank(4, P, 8 * h, 5), sq[:, h % 2, :]).then_inc(sem("hn_var"), 1)
                e.wait_ge(sem("hn_inv"), grp + 1)
                for h in range(4 * grp, 4 * grp + 4):
                    if h >= 2:
                        e.wait_ge(sem("hn_scaled"), h - 1)
                    spread(h % 2, inv[:, h, :]).then_inc(sem("hn_spread"), 1)

            def ln_shift(n):
                e.wait_ge(sem("ln_summed"), n + 1)
                for half, (lo, hi) in enumerate(HALVES):
                    mm = e.matmul(acc_half(2, half), ones[:, :], ln_sum[:, lo:hi], start=True, stop=True)
                mm.then_inc(sem("ln_mean"), 1)

            def ln_sums(n):
                e.wait_ge(sem("ln_added"), (KD - 2) * (n + 1))
                token_sums(bank(7, P, 0, 5), ln_s1, True, False)
                token_sums(bank(6, P, 0, 5), ln_s2, True, False)
                e.wait_ge(sem("ln_centered"), KD * (n + 1))
                token_sums(bank(7, P, 0, 5), x32[:, KD - 1, :], False).then_inc(sem("ln_var"), 1)
                e.wait_ge(sem("ln_squared"), KD * (n + 1))
                token_sums(bank(6, P, 0, 5), ln_sq[:, (KD - 1) % 4, :], False).then_inc(sem("ln_var"), 1)
                e.wait_ge(sem("ln_inverse"), 2 * n + 1)
                spread(3, ln_inv[:, 0, :]).then_inc(sem("ln_spread"), 1)
                e.wait_ge(sem("ln_inverse"), 2 * n + 2)
                spread(2, ln_inv[:, 1, :]).then_inc(sem("ln_spread"), 1)

            def turn_rows(n, tiles, ready):
                e.wait_ge(*ready)
                for r in range(2 + NS):
                    tr = e.transpose(bank(4 + r // 4, tiles, (r % 4) * P, P), last_rows[:, 0:tiles, r], ident[:, :])
                tr.then_inc(sem("rows_turned"), 1)

            def project_out(pr, u, kgroups, n, xh, xl):
                per = len(kgroups)
                for j in range(4):
                    for g, (k0, k) in enumerate(kgroups):
                        e.wait_ge(lo_made, u + per * j + g + 1)
                        for f in range(2):
                            if g == 0:
                                e.wait_ge(acc_free, 2 * (pr + j) + f - 1)
                            mm = mm_tile(e, (u + per * j + g) % 2, f, range(k0, k0 + k), xh, xl, g == 0, g == per - 1)
                            if f == 1:
                                mm.then_inc(unit_used, 1)
                            elif g == per - 1:
                                mm.then_inc(tile0_done, 1)
                                if j == 2:
                                    if n:
                                        e.wait_ge(sem("rows_out"), n)
                                    ln_shift(n)
                ln_sums(n)

            def first_unit(u, pr, n):
                e.wait_ge(lo_made, u + 1)
                e.wait_ge(acc_free, 2 * pr)
                for k in range(KD):
                    e.wait_ge(sem("x_made"), KD * (n + 1) + k + 1)
                    for f, done in enumerate((tile0_done, unit_used)):
                        for half, (lo, hi) in enumerate(HALVES):
                            wh, wl = (w[:, u % 2, k, f * P:(f + 1) * P] for w in (w_hi, w_lo))
                            e.matmul(acc_half(f, half), wh, x_hi[:, k, lo:hi], start=(k == 0), stop=False)
                            e.matmul(acc_half(f, half), wh, x_lo[:, k, lo:hi], start=False, stop=False)
                            mm = e.matmul(acc_half(f, half), wl, x_hi[:, k, lo:hi], start=False, stop=(k == KD - 1))
                        if k == KD - 1:
                            mm.then_inc(done, 1)

            def ffn(l):
                first_unit(U_IN[l], PR_IN[l], 2 * l)
                mm_units(e, U_IN[l] + 1, PR_IN[l] + 1, 1, U_IN[l] + 1, x_hi, x_lo)
                with e.Fori(0, NF // 2 - 1) as i:
                    mm_units(e, U_IN[l] + 2 + 2 * i, PR_IN[l] + 2 + 2 * i, 2, U_IN[l], x_hi, x_lo)
                turn_rows(2 * l, NU, (sem("t_made"), NU * (l + 1)))
                e.wait_ge(sem("h_made"), KD + NF * (l + 1) + KD * l)
                project_out(PR_OUT[l], U_OUT[l], K_GROUPS, 2 * l + 1, h_hi, h_lo)

            e.wait_ge(sem("h_made"), KD)
            project_out(PR_MIXOUT, U_MIXOUT, [(0, KD)], 0, h_hi, h_lo)
            ffn(0)
            first_unit(U_SCIN, PR_SCIN, 1)
            mm_units(e, U_SCIN + 1, PR_SCIN + 1, 1, U_SCIN + 1, x_hi, x_lo)
            with e.Fori(0, 5) as i:
                mm_units(e, U_SCIN + 2 + 2 * i, PR_SCIN + 2 + 2 * i, 2, U_SCIN, x_hi, x_lo)
            turn_rows(1, KD, (sem("ch_rows"), KD))
            e.wait_ge(sem("h_made"), KD + NF + KD)
            project_out(PR_SCOUT, U_SCOUT, [(0, KD)], 2, h_hi, h_lo)
            ffn(1)
            e.wait_ge(sem("x_final"), KD)
            for j in range(5):
                n = P if j < 4 else NS
                if j >= 2:
                    e.wait_ge(sem("y_out"), j - 1)
                for f in range(KD):
                    tr = e.transpose(bank(2 * (j % 2) + f // 4, n, (f % 4) * P, P), x32[:, f, j * P:j * P + n], ident[:, :])
                tr.then_inc(sem("y_turned"), 1)

        @block.gpsimd
        def _(e):
            def load_stage(i):
                if i < 2:
                    for j in range(2):
                        e.dma_start(samp[j * GDK:(j + 1) * GDK, i, :, :],
                                    state_gla[0, :, 2 * i + j].rearrange("b d v -> d b v")
                                    ).then_inc(sem("samp_loaded%d" % (i % 2)), 16)
                else:
                    for b in (slice(0, NS // 2), slice(NS // 2, NS)):
                        e.dma_start(samp[:, i % 2, b, :], state_ret[0, b, i - 2].rearrange("b d v -> d b v")
                                    ).then_inc(sem("samp_loaded%d" % (i % 2)), 16)

            def blocks(h):
                if h >= 2:
                    e.wait_ge(sem("outer_summed"), h - 1)
                v = tok_s[:, 4 + h, :] if h < GH else tok_r[:, h, :]
                e.tensor_tensor(v_blocks[h % 2][:, :, :], bc(v, 1, NS), bc(ident[0:NS, 0:NS], 2, DV), ALU.mult
                                ).then_inc(sem("v_blk_made"), 1)

            e.wait_ge(sem("past_turned"), 3)
            load_stage(0)
            load_stage(1)
            e.wait_ge(sem("gla_state"), NC)
            for g in range(2):
                e.dma_start(gla_p[0, 0, 2 * g:2 * g + 2].rearrange("h d v -> (h d) v"),
                            state_g[:, NC - 1, g, :]).then_inc(sem("gla_p_stored"), 16)
            e.wait_ge(sem("ret_state"), NC)
            e.dma_start(ret_p[0, 0].rearrange("h d v -> d h v"), state[:, (NC - 1) % 2, :, :]
                        ).then_inc(sem("ret_p_stored"), 16)
            e.wait_ge(sem("gs_copied"), 1)
            e.wait_ge(sem("rs_copied"), 1)
            for h in range(2):
                blocks(h)
            for i in range(2 + RH):
                if i + 1 < 2 + RH:
                    for h in ((2, 3) if i == 0 else (i + 3,)):
                        blocks(h)
                e.wait_ge(sem("samp_made"), i + 1)
                if i < 2:
                    for j in range(2):
                        e.dma_start(gla_s[0, :, 2 * i + j].rearrange("b d v -> d b v"),
                                    samp[j * GDK:(j + 1) * GDK, i, :, :]).then_inc(sem("samp_stored%d" % (i % 2)), 16)
                else:
                    for b in (slice(0, NS // 2), slice(NS // 2, NS)):
                        e.dma_start(ret_s[0, b, i - 2].rearrange("b d v -> d b v"), samp[:, i % 2, b, :]
                                    ).then_inc(sem("samp_stored%d" % (i % 2)), 16)
                if i + 2 < 2 + RH:
                    e.wait_ge(sem("samp_stored%d" % (i % 2)), 32 * (i // 2 + 1))
                    e.wait_ge(sem("samp_read"), i + 1)
                    load_stage(i + 2)
            e.wait_ge(sem("gla_p_stored"), 32)
            e.wait_ge(sem("ret_p_stored"), 16)
            for j in range(2):
                e.wait_ge(sem("samp_stored%d" % j), 32 * (2 + RH) // 2)
            for n in range(2 * DEPTH):
                for t in range(1, KD - 1):
                    k = (KD - 2) * n + t
                    e.wait_ge(sem("ln_centered"), KD * n + t + 1)
                    if t > 1:
                        e.wait_ge(sem("ln_added"), k - 1)
                    e.tensor_tensor(ln_s1, x32[:, 0, :] if t == 1 else ln_s1, x32[:, t, :], ALU.add)
                    e.wait_ge(sem("ln_squared"), KD * n + t + 1)
                    e.tensor_tensor(ln_s2, ln_sq[:, 0, :] if t == 1 else ln_s2, ln_sq[:, t % 4, :], ALU.add
                                    ).then_inc(sem("ln_added"), 1)
                for f in range(KD):
                    if n < 2 * DEPTH - 1:
                        e.wait_ge(sem("x_hi_made"), KD * (n + 1) + f + 1)
                        e.tensor_tensor(x_lo[:, f, :], x32[:, f, :], x_hi[:, f, :].bitcast(F32), ALU.subtract
                                        ).then_inc(sem("x_made"), 1)

        @block.scalar
        def _(e):
            step = [0]

            def link(ins):
                step[0] += 1
                ins.then_inc(sem("act_step"), 1)
                e.wait_ge(sem("act_step"), step[0])

            for f in range(KD):
                e.wait_ge(sem("x_copied"), f + 1)
                e.activation(x_hi[:, f, :], x32[:, f, :], ACT.Copy).then_inc(sem("x_hi_made"), 1)
            stage_hi(e, 0)
            stage_hi(e, 1)
            e.wait_ge(unit_used, 1)
            link(e.activation(a_lr[:, :], acc(0)[0:RANK, :], ACT.Copy))
            e.activation(a_samp[0:1, 0, 0:1], a_lr[0:1, 0:1], ACT.Copy).then_inc(acc_free, 1)
            e.activation(a_samp[0:1, 0, 1:2], a_lr[0:1, 0:1], ACT.Copy).then_inc(acc_free, 1)

            def tile_out(u, f):
                name, j = z_of[u]
                acc_wait(e, u, u, f)
                e.activation(zt[name][:, j + f, :], acc(f), ACT.Silu if name in ("r_g", "g_r") else ACT.Copy
                             ).then_inc(acc_free, 1)

            stage_hi(e, 2)
            tile_out(1, 0)
            tile_out(1, 1)
            e.wait_ge(sem("vecs_made"), 1)
            e.wait_ge(sem("gate_summed"), 1)
            for g in range(2):
                ins = e.activation(gate_t[:, g, :], acc(2 + g), ACT.Abs, bias=vec(V_LN, COL_BG + g))
            link(ins)
            link(e.activation(gate_t[:, :, :], gate_t[:, :, :], ACT.Exp, scale=-1.0))
            e.activation(gate_t[:, :, :], gate_t[:, :, :], ACT.Ln, bias=1.0).then_inc(sem("gate_ln"), 1)
            stage_hi(e, 3)
            tile_out(2, 0)
            tile_out(2, 1)

            def decay_exp(i):
                e.wait_ge(sem("dd_made"), i + 1)
                e.activation(dd[:, :, :], dd[:, :, :], ACT.Exp, scale=1.0 / TAU).then_inc(sem("dd_exp"), 1)

            def copy_blocks(n):
                h = C >> n
                e.wait_ge(sem("level_summed"), n + 1)
                scores, sums = sc[:, :, :].rearrange("p h (c t) -> p (h c) t", t=C), ps_t[:, 2048:4096].rearrange("p (m t) -> p m t", t=C)
                for s in range(0, C, 2 * h):
                    ins = e.activation(scores[s:s + h, :, s + h:s + 2 * h], sums[s:s + h, :, s + h:s + 2 * h], ACT.Copy)
                ins.then_inc(sem("level_added"), 1)

            def gla_decays():
                e.wait_ge(sem("gk_decayed"), 1)
                e.activation(dd[:, :, :], cum[:, :, :], ACT.Exp, scale=1.0 / TAU)
                e.activation(e_last[:, :, :], cum[:, :, C - 1::C], ACT.Exp, scale=1.0 / TAU).then_inc(sem("cum_exp"), 1)

            def gla_values():
                e.wait_ge(sem("gv_turned"), 1)
                for c in range(NC):
                    ins = e.activation(v_tok[:, c, :], bank(4 + c), ACT.Copy)
                ins.then_inc(sem("gv_copied"), 1)

            def gla_keys():
                e.wait_ge(sem("gk_turned"), 1)
                for c in range(NC):
                    ins = e.activation(k_tok[:, c, 0:256], bank(4 + c // 2, P, (c % 2) * 256, 256), ACT.Copy)
                ins.then_inc(sem("gk_copied"), 1)

            def gla_outputs():
                e.wait_ge(sem("gla_out"), 1)
                for h in range(GH):
                    ins = e.activation(o_att[h][:, 0:T], bank(4 + h), ACT.Copy)
                ins.then_inc(sem("gla_copied"), 1)

            def gla_samples():
                e.wait_ge(sem("gs_turned"), 1)
                e.activation(tok_s[:, 0:2, :], bank(4, NS, 0, 256), ACT.Copy)
                e.activation(tok_s[:, 4:8, :], bank(5, NS), ACT.Copy).then_inc(sem("gs_copied"), 1)

            def ret_values():
                e.wait_ge(sem("rv_turned"), 1)
                for c in range(NC):
                    ins = e.activation(v_tok[:, c, :], bank(4 + c), ACT.Copy)
                ins.then_inc(sem("rv_copied"), 1)

            def ret_outputs(cs):
                for c in cs:
                    e.wait_ge(sem("ret_out"), c + 1)
                    e.activation(v_r[:, :, c * C:(c + 1) * C], bank(4 + c % 2).rearrange("p (h t) -> p h t", h=RH), ACT.Copy
                                 ).then_inc(sem("ret_copied"), 1)

            def ret_samples():
                e.wait_ge(sem("rs_turned"), 1)
                e.activation(tok_r[:, 0:4, :], bank(6, NS), ACT.Copy, scale=RDK ** -0.5)
                e.activation(tok_r[:, 4:8, :], bank(7, NS), ACT.Copy).then_inc(sem("rs_copied"), 1)

            def sample_out(i):
                b = 4 + 2 * (i % 2)
                e.wait_ge(sem("samp_read"), i + 1)
                for j in range(2 if i < 2 else 1):
                    ins = e.activation(o_att[2 * i + j if i < 2 else i + 2][:, T:N], bank(b + j, P, 0, NS), ACT.Copy)
                ins.then_inc(sem("samp_out"), 1)

            after = [[lambda: decay_exp(1)], [lambda: copy_blocks(1), lambda: decay_exp(2)], [lambda: copy_blocks(2), lambda: decay_exp(3)],
                     [lambda: decay_exp(4)], [lambda: decay_exp(5)], [lambda: decay_exp(6)], [lambda: decay_exp(7)], [],
                     [gla_decays, gla_values], [gla_keys], [], [], [gla_outputs], [], [], [gla_samples], [ret_values],
                     [lambda: ret_outputs((0, 1))], [lambda: ret_outputs((2, 3))],
                     [ret_samples], [lambda: sample_out(0)], [lambda: sample_out(1)], [lambda: sample_out(2)],
                     [lambda: sample_out(3)]]
            for n, pieces in enumerate(after):
                u, f = 3 + n // 2, n % 2
                if f == 0:
                    stage_hi(e, u + 1)
                if n == 0:
                    e.wait_ge(sem("log_a_made"), 1)
                    e.activation(a_samp[:, :, :], log_a[:, :, T:N], ACT.Exp, scale=1.0 / TAU).then_inc(sem("a_samp_made"), 1)
                    decay_exp(0)
                if n == 16:
                    e.wait_ge(sem("gla_out"), 1)
                if n == 20:
                    e.wait_ge(sem("ret_out"), NC)
                tile_out(u, f)
                for piece in pieces:
                    piece()
            sample_out(4)
            sample_out(5)
            for grp in range(2):
                for h in range(4 * grp, 4 * grp + 4):
                    if grp:
                        e.wait_ge(sem("hn_centered"), h - GH + 1)
                    if h >= 2:
                        e.wait_ge(sem("hn_var"), h - 1)
                    e.activation(sq[:, h % 2, :], o_att[h], ACT.Square).then_inc(sem("hn_squared"), 1)
                e.wait_ge(sem("hn_var"), 4 * grp + 4)
                e.activation(inv[:, 4 * grp:4 * grp + 4, :],
                             bank(4, P, 32 * grp, 32).rearrange("p (h j) -> p h j", h=4)[:, :, 0:5],
                             ACT.Sqrt, bias=eps[:, :], scale=1.0 / DV).then_inc(sem("hn_root"), 1)
                for h in range(4 * grp, 4 * grp + 4):
                    e.wait_ge(sem("hn_done"), h + 1)
                    e.activation(h_hi[:, h, :], o_att[h], ACT.Copy).then_inc(sem("h_hi_made"), 1)

            def norm(n, u, per, g, col_g, col_b, last=False):
                if n == 0:
                    for name, count in (("samp_stored0", 96), ("samp_stored1", 96), ("gla_p_stored", 32), ("ret_p_stored", 16)):
                        e.wait_ge(sem(name), count)
                def squares(tiles):
                    for t in tiles:
                        e.wait_ge(sem("ln_centered"), KD * n + t + 1)
                        if t >= 5:
                            e.wait_ge(sem("ln_added"), (KD - 2) * n + t - 4)
                        elif t == 4:
                            e.wait_ge(sem("ln_added"), (KD - 2) * n + 1)
                        e.activation(ln_sq[:, t % 4, :], x32[:, t, :], ACT.Square).then_inc(sem("ln_squared"), 1)

                for j in range(3 * per):
                    stage_hi(e, u + j + 1)
                squares(range(5))
                for j in range(3 * per, 4 * per):
                    stage_hi(e, u + j + 1)
                squares(range(5, KD))
                e.wait_ge(sem("ln_varied"), n + 1)
                e.activation(ln_inv[:, 0, :], ln_var[:, 2, :], ACT.Sqrt, bias=eps[:, :]).then_inc(sem("ln_root"), 1)
                for f in range(KD):
                    e.wait_ge(sem("ln_scaled"), KD * n + f + 1)
                    ins = e.activation(x32[:, f, :], x32[:, f, :], ACT.Identity, bias=vec(g, col_b + f), scale=vec(g, col_g + f))
                    if last:
                        ins.then_inc(sem("x_final"), 1)
                        continue
                    link(ins)
                    e.activation(x_hi[:, f, :], x32[:, f, :], ACT.Copy).then_inc(sem("x_hi_made"), 1)

            def rows_back(n, tiles):
                e.wait_ge(sem("rows_turned"), n + 1)
                if n:
                    e.wait_ge(sem("rows_stored"), 32 * n)
                for r in range(0, 2 + NS, 4):
                    k = min(4, 2 + NS - r)
                    ins = e.activation(row_out[0:tiles, r:r + k, :], bank(4 + r // 4, tiles, 0, k * P), ACT.Copy)
                ins.then_inc(sem("rows_out"), 1)

            def ffn(l):
                u, pr = U_IN[l], PR_IN[l]
                e.activation(eps_copy[:, :], eps[:, :], ACT.Silu)
                with e.Fori(0, NF // 2) as i:
                    for s in range(2):
                        make_hi(e, u + 2 * i + s + 1, (u + s + 1) % 2, 16 * ((u + s + 1) // 2 + 1) + 16 * i)
                        if s == 0:
                            e.wait_ge(sem("mul_done"), NF * l + 2 * i + 1)
                        for f in range(2):
                            tile = NF * s + 2 * i + f
                            acc_wait(e, pr + 2 * i + s, u + 2 * i + s, f)
                            e.activation(tmp[:, 2 * s + f, :], acc(f), ACT.Identity,
                                         bias=ffn_vec(l, 3, tile), scale=ffn_vec(l, 2, tile))
                            e.activation(last_rows[:, bass.ds(tile, 1), :], acc(f)[:, T - 2:N].unsqueeze(1), ACT.Copy
                                         ).then_inc(sem("t_made"), 1)
                            if s == 0:
                                continue
                            e.wait_ge(acc_free, 2 * (pr + 2 * i + 1) + f + 1)
                            e.activation(tmp[:, 4 + f, :], tmp[:, 2 + f, :], ACT.Silu).then_inc(sem("silu_done"), 1)
                            e.wait_ge(sem("mul_done"), NF * l + 2 * i + f + 2)
                            e.activation(h_hi[:, bass.ds(2 * i + f, 1), :], tmp[:, 6 + f:7 + f, :], ACT.Copy
                                         ).then_inc(sem("h_hi_made"), 1)
                rows_back(2 * l, NU)
                norm(2 * l + 1, U_OUT[l], 3, V_LN, COL_LN2G + KD * l, COL_LN2B + KD * l, last=(l == 1))

            norm(0, U_MIXOUT, 1, V_LN, COL_LN1G, COL_LN1B)
            ffn(0)
            for j in range(4):
                for part in range(3):
                    u, pr = U_SCIN + 3 * j + part, PR_SCIN + 3 * j + part
                    stage_hi(e, u + 1)
                    for f in range(2):
                        if part < 2:
                            if part == 0 and j:
                                e.wait_ge(sem("sc_gated"), 2 * j)
                            acc_wait(e, pr, u, f)
                            e.activation(tmp[:, 2 * part + f, :], acc(f), ACT.Copy).then_inc(acc_free, 1)
                        else:
                            e.wait_ge(acc_free, 2 * pr + f + 1)
                            e.activation(tmp[:, 6 + f, :], tmp[:, 4 + f, :], ACT.Identity,
                                         bias=vec(V_LN, COL_SCB + 2 * j + f), scale=vec(V_LN, COL_SCW + 2 * KD + 2 * j + f))
                            e.activation(last_rows[:, 2 * j + f, :], tmp[:, 4 + f, T - 2:N], ACT.Copy
                                         ).then_inc(sem("ch_rows"), 1)
                for f in range(2):
                    e.wait_ge(sem("sc_gated"), 2 * j + f + 1)
                    e.activation(h_hi[:, 2 * j + f, :], tmp[:, 6 + f, :], ACT.Copy).then_inc(sem("h_hi_made"), 1)
            rows_back(1, KD)
            norm(2, U_SCOUT, 1, V_LN, COL_LN1G + KD, COL_LN1B + KD)
            ffn(1)
            for j in range(5):
                n = P if j < 4 else NS
                e.wait_ge(sem("y_turned"), j + 1)
                if j >= 2:
                    e.wait_ge(sem("y_stored%d" % (j % 2)), 16 * (j // 2))
                e.activation(y_tok[0:n, j % 2, 0:512], bank(2 * (j % 2), n), ACT.Copy)
                e.activation(y_tok[0:n, j % 2, 512:D], bank(2 * (j % 2) + 1, n), ACT.Copy).then_inc(sem("y_out"), 1)

        @block.vector
        def _(e):
            step = [0]

            def link(ins):
                step[0] += 1
                ins.then_inc(sem("vec_step"), 1)
                e.wait_ge(sem("vec_step"), step[0])

            def split_x(f, n):
                e.wait_ge(sem("x_hi_made"), n)
                e.tensor_tensor(x_lo[:, f, :], x32[:, f, :], x_hi[:, f, :].bitcast(F32), ALU.subtract
                                ).then_inc(sem("x_made"), 1)

            e.memset(ones[:, :], 1.0)
            link(e.memset(eps[:, :], EPS))
            for f in range(KD):
                e.wait_ge(sem("x_turned"), f + 1)
                o = (f % 4) * 1024 + 256
                e.tensor_copy(x32[:, f, :], ps_t[:, o:o + N]).then_inc(sem("x_copied"), 1)
            for f in range(KD):
                split_x(f, f + 1)
            stage_lo(e, 0)
            stage_lo(e, 1)
            stage_lo(e, 2)
            e.wait_ge(sem("vecs_turned"), 1)
            for g in range(5):
                n = 2 * NU if g < V_LN else N_V
                ins = e.tensor_copy(vecs[:, g, 0:n], bank(4, P, g * 88, n))
            link(ins)
            e.wait_ge(sem("past_turned"), 1)
            def conv_past(j):
                w = vec(V_LN, COL_SCW + j * KD, KD)
                return bank(7, P, 0, KD * 16).rearrange("p (t b j) -> p b t j", b=NS, j=2)[:, :, :, j], bc(w, 1, NS)
            scratch = past_t[:, :, :]
            a, w = conv_past(0)
            e.tensor_tensor(past_conv[:, :, :], a, w, ALU.mult)
            a, w = conv_past(1)
            link(e.tensor_tensor(scratch[:, :, 0:KD], a, w, ALU.mult))
            link(e.tensor_tensor(past_conv[:, :, :], past_conv[:, :, :], scratch[:, :, 0:KD], ALU.add))
            e.memset(ones_one[:, :], 1.0).then_inc(sem("past_made"), 1)
            for l in range(DEPTH):
                e.wait_ge(sem("past_turned"), l + 2)
                for half in range(2):
                    b = slice(4 * half, 4 * half + 4)
                    rows = bank(5 + half, P, 0, 8 * NU).rearrange("p (b j t) -> p b j t", b=4, j=2)
                    for j, out in ((0, past_ffn[:, l, b, :]), (1, scratch[:, b, :])):
                        w = vecs[:, 2 * l, j * NU:(j + 1) * NU]
                        ins = e.tensor_tensor(out, rows[:, :, j, :], bc(w, 1, 4), ALU.mult)
                link(ins)
                e.tensor_tensor(past_ffn[:, l], past_ffn[:, l], scratch, ALU.add).then_inc(sem("past_made"), 1)
                e.wait_ge(sem("past_made"), l + 2)
            e.memset(ones_one[:, :], 1.0).then_inc(sem("vecs_made"), 1)
            stage_lo(e, 3)
            e.wait_ge(sem("gate_ln"), 1)
            for g in range(2):
                ins = e.tensor_scalar(gate_m[:, g, :], acc(2 + g), vec(V_LN, COL_BG + g), 0.0, ALU.add, ALU.min)
            ins.then_inc(sem("gate_read"), 1)
            e.wait_ge(sem("gate_read"), 1)
            e.tensor_tensor(log_a[:, :, :], gate_m[:, :, :], gate_t[:, :, :], ALU.subtract).then_inc(sem("log_a_made"), 1)
            e.wait_ge(sem("log_a_made"), 1)
            for g in range(2):
                for c in range(NC):
                    t = slice(c * C, (c + 1) * C)
                    ins = e.tensor_tensor_scan(cum[:, g, t], ones[:, :], log_a[:, g, t], 0.0, ALU.mult, ALU.add)
            link(ins)

            def blocks(a, h):
                return a.rearrange("p g (m w) -> p g m w", w=2 * h)

            def level_diff(l):
                h = C >> (l + 1)
                c, d = blocks(cum[:, :, :], h), blocks(dd[:, :, :], h)
                ref = c[:, :, :, h - 1:h].broadcast_to([P, 2, T // (2 * h), h])
                e.tensor_tensor(d[:, :, :, 0:h], ref, c[:, :, :, 0:h], ALU.subtract)
                e.tensor_tensor(d[:, :, :, h:], c[:, :, :, h:], ref, ALU.subtract).then_inc(sem("dd_made"), 1)

            def level_parts(l):
                h = C >> (l + 1)
                e.wait_ge(sem("dd_exp"), l + 1)
                d = blocks(dd[:, :, :], h)
                k, q = blocks(k_g[:, :, 0:T], h), blocks(q_g[:, :, 0:T], h)
                e.tensor_tensor(blocks(k_t[:, :, :], h)[:, :, :, 0:h], k[:, :, :, 0:h], d[:, :, :, 0:h], ALU.mult)
                e.tensor_tensor(blocks(q_t[:, :, :], h)[:, :, :, h:], q[:, :, :, h:], d[:, :, :, h:], ALU.mult
                                ).then_inc(sem("level_made"), 1)
                e.wait_ge(sem("level_made"), l + 1)

            def keys_diff():
                for g in range(2):
                    c = per_chunk(cum[:, g, :])
                    ins = e.tensor_tensor(per_chunk(dd[:, g, :]), c[:, :, C - 1:C].broadcast_to([P, NC, C]), c, ALU.subtract)
                ins.then_inc(sem("dd_made"), 1)

            def per_chunk(a):
                return a.rearrange("p (c t) -> p c t", t=C)

            def add_level(n):
                e.copy_predicated(sc[:, :, :].rearrange("p h (c t) -> p (h c) t", t=C), bc(masks[:, (n - 1) % (LEVELS + 1), :], 1, GH * NC),
                                  ps_t[:, 4 * 512:8 * 512].rearrange("p (m t) -> p m t", t=C)).then_inc(sem("level_added"), 1)
                e.wait_ge(sem("level_added"), n + 1)

            def level_step(n):
                e.wait_ge(sem("level_summed"), n + 1)
                if 1 <= n < LEVELS:
                    level_parts(n)
                    if n + 1 < LEVELS:
                        level_diff(n + 1)
                    else:
                        keys_diff()
                if n not in (1, 2):
                    add_level(n)

            def gla_decayed():
                e.wait_ge(sem("dd_exp"), LEVELS + 1)
                e.tensor_tensor(k_t[:, :, :], k_g[:, :, 0:T], dd[:, :, :], ALU.mult).then_inc(sem("gk_decayed"), 1)
                e.wait_ge(sem("cum_exp"), 1)
                e.tensor_tensor(q_t[:, :, :], q_g[:, :, 0:T], dd[:, :, :], ALU.mult).then_inc(sem("gq_decayed"), 1)

            def gla_states(cs):
                for c in cs:
                    e.wait_ge(sem("gla_inc"), c + 1)
                    for j in range(2):
                        p = slice(j * GDK, (j + 1) * GDK)
                        for g in range(2):
                            o = (6 + c % 2) * 512 + g * 256 + j * P
                            if c == 0:
                                ins = e.tensor_copy(state_g[p, 0, g, :], ps_t[p, o:o + P])
                            else:
                                ins = e.scalar_tensor_tensor(state_g[p, c, g, :], state_g[p, c - 1, g, :],
                                                             e_last[p, g, c:c + 1], ps_t[p, o:o + P], ALU.mult, ALU.add)
                    ins.then_inc(sem("gla_state"), 1)
                    e.wait_ge(sem("gla_state"), c + 1)

            rotated = [0]

            def rotate(x, tiles, u):
                e.wait_ge(sem("rot_loaded"), 16)
                for h in tiles:
                    e.wait_ge(acc_free, 2 * (u + h // 2) + h % 2 + 1)
                    e.tensor_tensor(rot_t[:, 0, :], x[:, h, :], rot[:, 0, :], ALU.mult)
                    e.tensor_tensor(rot_t[0:64, 1, :], x[64:128, h, :], rot[64:128, 1, :], ALU.mult)
                    link(e.tensor_tensor(rot_t[64:128, 1, :], x[0:64, h, :], rot[0:64, 1, :], ALU.mult))
                    e.tensor_tensor(x[:, h, :], rot_t[:, 0, :], rot_t[:, 1, :], ALU.add).then_inc(sem("rotated"), 1)
                    rotated[0] += 1
                    e.wait_ge(sem("rotated"), rotated[0])

            def ret_queries():
                e.wait_ge(sem("gla_out"), 1)
                for h in range(RH):
                    ins = e.tensor_tensor(per_chunk(q_dec[:, h, :]), per_chunk(q_r[:, h, 0:T]),
                                          bc(decay[:, RH * C + h * C:RH * C + (h + 1) * C], 1, NC), ALU.mult)
                ins.then_inc(sem("rq_decayed"), 1)

            def ret_scores():
                e.wait_ge(sem("rs_summed"), 1)
                for h in range(RH):
                    ins = e.tensor_tensor(per_chunk(sc[:, h, :]), per_chunk(bank(4 + h)), bc(decay[:, h * C:(h + 1) * C], 1, NC), ALU.mult)
                ins.then_inc(sem("rs_decayed"), 1)

            def ret_keys():
                e.wait_ge(sem("rk_turned"), 1)
                for c in range(NC):
                    ins = e.tensor_tensor(k_tok[:, c, :].rearrange("p (h d) -> p h d", h=RH),
                                          bank(4 + c).rearrange("p (h d) -> p h d", h=RH),
                                          bc(decay[:, 2 * RH * C:2 * RH * C + RH], 2, RDK), ALU.mult)
                ins.then_inc(sem("rk_decayed"), 1)

            def ret_states(cs):
                e.wait_ge(sem("gla_p_stored"), 32)
                for c in cs:
                    e.wait_ge(sem("ret_inc"), c + 1)
                    if c == 0:
                        ins = e.tensor_copy(state[:, 0, :, :], bank(6))
                    else:
                        for h in range(RH):
                            ins = e.scalar_tensor_tensor(state[:, c % 2, h, :], state[:, (c - 1) % 2, h, :], GAMMA[h] ** C,
                                                         bank(6 + c % 2, P, h * DV, DV), ALU.mult, ALU.add)
                    ins.then_inc(sem("ret_state"), 1)
                    e.wait_ge(sem("ret_state"), c + 1)

            def sample_states(i):
                o = (4 + 2 * (i % 2)) * 512
                if i < 2:
                    e.wait_ge(sem("outer_summed"), 2 * i + 2)
                    e.wait_ge(sem("samp_loaded%d" % i), 32)
                    e.wait_ge(sem("a_samp_made"), 1)
                    for b in range(NS):
                        ins = e.scalar_tensor_tensor(samp[:, i, b, :], samp[:, i, b, :], a_samp[:, i, b:b + 1],
                                                     ps_t[:, o + b * DV:o + (b + 1) * DV], ALU.mult, ALU.add)
                else:
                    e.wait_ge(sem("outer_summed"), i + 3)
                    e.wait_ge(sem("samp_loaded%d" % (i % 2)), 32 * (i // 2 + 1))
                    ins = e.scalar_tensor_tensor(samp[:, i % 2, :, :], samp[:, i % 2, :, :], GAMMA[i - 2],
                                                 ps_t[:, o:o + 1024].rearrange("p (b d) -> p b d", b=NS), ALU.mult, ALU.add)
                ins.then_inc(sem("samp_made"), 1)

            e.memset(sc[:, :, :], 0.0)
            e.memset(q_t[:, :, :], 0.0)
            e.memset(k_t[:, :, :], 0.0)
            e.wait_ge(sem("tables_loaded"), 48)
            link(e.tensor_copy(masks[:, :, :], mask_rows[:, :, :]))
            level_diff(0)
            steps = [[lambda n=n: level_step(n)] for n in range(LEVELS + 1)] + [
                [gla_decayed, lambda: rotate(q_r, (0, 1), 5)], [lambda: rotate(q_r, (2, 3), 5)],
                [lambda: gla_states((0, 1)), lambda: rotate(k_r, (0,), 7)], [lambda: gla_states((2, 3)), lambda: rotate(k_r, (1,), 7)],
                [lambda: rotate(k_r, (2, 3), 7)], [ret_queries], [ret_scores], [ret_keys], [], [lambda: ret_states((0, 1))],
                [lambda: ret_states((2, 3))], [], [lambda: sample_states(0)], [lambda: sample_states(1)],
                [lambda: sample_states(2)], [lambda: sample_states(3)]]
            for n, pieces in enumerate(steps):
                if n % 2 == 0:
                    stage_lo(e, 4 + n // 2)
                if n == 0:
                    e.wait_ge(acc_free, 2 * 3)
                    e.tensor_scalar(q_g[:, :, :], q_g[:, :, :], GDK ** -0.5, None, ALU.mult).then_inc(sem("q_scaled"), 1)
                    e.wait_ge(sem("q_scaled"), 1)
                    level_parts(0)
                    level_diff(1)
                for piece in pieces:
                    piece()
            sample_states(4)
            sample_states(5)
            for grp in range(2):
                if grp:
                    for h in range(GH, KD):
                        e.wait_ge(sem("hn_mean"), h - GH + 1)
                        e.scalar_tensor_tensor(o_att[h], acc(0), -1.0 / DV, o_att[h], ALU.mult, ALU.add
                                               ).then_inc(sem("hn_centered"), 1)
                e.wait_ge(sem("hn_root"), grp + 1)
                e.reciprocal(inv[:, 4 * grp:4 * grp + 4, :], inv[:, 4 * grp:4 * grp + 4, :]).then_inc(sem("hn_inv"), 1)
                for h in range(4 * grp, 4 * grp + 4):
                    gain = vec(V_LN, COL_GG) if h < GH else vec(V_LN, COL_GR + h - GH)
                    e.wait_ge(sem("hn_spread"), h + 1)
                    e.scalar_tensor_tensor(o_att[h], o_att[h], gain, acc(h % 2), ALU.mult, ALU.mult).then_inc(sem("hn_scaled"), 1)
                    e.wait_ge(sem("hn_scaled"), h + 1)
                    if h < GH:
                        ins = e.tensor_tensor(o_att[h], o_att[h], r_g[:, h, :], ALU.mult)
                    else:
                        ins = e.scalar_tensor_tensor(o_att[h], o_att[h], vec(V_LN, COL_BR + h - GH), g_r[:, h - GH, :], ALU.add, ALU.mult)
                    ins.then_inc(sem("hn_done"), 1)
                for h in range(4 * grp, 4 * grp + 4):
                    e.wait_ge(sem("h_hi_made"), h + 1)
                    e.tensor_tensor(h_lo[:, h, :], o_att[h], h_hi[:, h, :].bitcast(F32), ALU.subtract
                                    ).then_inc(sem("h_made"), 1)

            def residual(n, u, pr, per):
                for j in range(4):
                    for g in range(per):
                        stage_lo(e, u + per * j + g + 1)
                    for f in range(2):
                        t = 2 * j + f
                        acc_wait(e, pr + j, u + per * j + per - 1, f)
                        if t > KD // 2:
                            e.tensor_tensor(x32[:, t, :], x32[:, t, :], acc(f), ALU.add).then_inc(sem("ln_centered"), 1)
                            e.wait_ge(sem("ln_centered"), KD * n + t + 1)
                            e.memset(ones_one[:, :], 1.0).then_inc(acc_free, 1)
                            continue
                        e.scalar_tensor_tensor(x32[:, t, :], x32[:, t, :], ALPHA, acc(f), ALU.mult, ALU.add
                                               ).then_inc(acc_free, 1)
                        e.wait_ge(acc_free, 2 * (pr + j) + f + 1)
                        if 0 < t < KD // 2:
                            link(e.tensor_tensor(ln_sum[:, :], x32[:, 0, :] if t == 1 else ln_sum[:, :], x32[:, t, :], ALU.add))
                        if t == KD // 2 - 1:
                            e.tensor_scalar(ln_sum[:, :], ln_sum[:, :], -2.0 / D, None, ALU.mult).then_inc(sem("ln_summed"), 1)
                        if t == KD // 2:
                            e.wait_ge(sem("ln_mean"), n + 1)
                            for i in range(t + 1):
                                e.tensor_tensor(x32[:, i, :], x32[:, i, :], acc(2), ALU.add).then_inc(sem("ln_centered"), 1)
                            for i in range(t + 1, KD):
                                ins = e.scalar_tensor_tensor(x32[:, i, :], x32[:, i, :], ALPHA, acc(2), ALU.mult, ALU.add)
                            link(ins)

            def norm(n):
                d, d2, var = (ln_var[:, i, :] for i in range(3))
                e.wait_ge(sem("ln_var"), 2 * n + 1)
                link(e.tensor_scalar(d, bank(7, P, 0, 5), 1.0 / D, None, ALU.mult))
                link(e.tensor_tensor(d2, d, d, ALU.mult))
                e.wait_ge(sem("ln_var"), 2 * n + 2)
                e.scalar_tensor_tensor(var, bank(6, P, 0, 5), 1.0 / D, d2, ALU.mult, ALU.subtract).then_inc(sem("ln_varied"), 1)
                e.wait_ge(sem("ln_root"), n + 1)
                e.reciprocal(ln_inv[:, 0, :], ln_inv[:, 0, :]).then_inc(sem("ln_inverse"), 1)
                e.wait_ge(sem("ln_inverse"), 2 * n + 1)
                e.scalar_tensor_tensor(ln_inv[:, 1, :], d, -1.0, ln_inv[:, 0, :], ALU.mult, ALU.mult).then_inc(sem("ln_inverse"), 1)
                for f in range(KD + 1):
                    if f < KD:
                        e.wait_ge(sem("ln_spread"), 2 * n + 1)
                        e.tensor_tensor(x32[:, f, :], x32[:, f, :], acc(3), ALU.mult).then_inc(sem("ln_times"), 1)
                    if f:
                        e.wait_ge(sem("ln_spread"), 2 * n + 2)
                        e.wait_ge(sem("ln_times"), KD * n + f)
                        e.tensor_tensor(x32[:, f - 1, :], x32[:, f - 1, :], acc(2), ALU.add).then_inc(sem("ln_scaled"), 1)

            def ffn(l):
                u, pr = U_IN[l], PR_IN[l]
                with e.Fori(0, NF // 2) as i:
                    for s in range(2):
                        make_lo(e, u + 2 * i + s + 1, (u + s + 1) % 2)
                        for f in range(2):
                            tile = NF * s + 2 * i + f
                            n = NU * l + 4 * i + 2 * s + f
                            t = tmp[:, 2 * s + f, :]
                            e.wait_ge(sem("t_made"), n + 1)
                            e.tensor_tensor(t[:, T:N], t[:, T:N], past_col(l, tile), ALU.add)
                            e.scalar_tensor_tensor(t[:, 1:T], acc(f)[:, 0:T - 1], ffn_vec(l, 1, tile), t[:, 1:T],
                                                   ALU.mult, ALU.add).then_inc(sem("tap_done"), 1)
                            e.wait_ge(sem("tap_done"), n + 1)
                            e.scalar_tensor_tensor(t[:, 2:T], acc(f)[:, 0:T - 2], ffn_vec(l, 0, tile), t[:, 2:T],
                                                   ALU.mult, ALU.add).then_inc(acc_free, 1)
                            if s == 0:
                                continue
                            e.wait_ge(sem("silu_done"), NF * l + 2 * i + f + 1)
                            e.tensor_tensor(tmp[:, 6 + f, :], tmp[:, 4 + f, :], tmp[:, f, :], ALU.mult).then_inc(sem("mul_done"), 1)
                            e.wait_ge(sem("h_hi_made"), KD * (l + 1) + NF * l + 2 * i + f + 1)
                            e.tensor_tensor(h_lo[:, bass.ds(2 * i + f, 1), :], tmp[:, 6 + f:7 + f, :],
                                            h_hi[:, bass.ds(2 * i + f, 1), :].bitcast(F32), ALU.subtract).then_inc(sem("h_made"), 1)
                residual(2 * l + 1, U_OUT[l], PR_OUT[l], 3)
                norm(2 * l + 1)

            def past_col(l, tile):
                return past_ffn[:, l, :, bass.ds(tile, 1)].rearrange("p b o -> p (b o)")

            residual(0, U_MIXOUT, PR_MIXOUT, 1)
            norm(0)
            e.memset(ones_one[:, :], 1.0).then_inc(sem("mul_done"), 1)
            ffn(0)
            for j in range(4):
                for part in range(3):
                    u, pr = U_SCIN + 3 * j + part, PR_SCIN + 3 * j + part
                    stage_lo(e, u + 1)
                    if part == 2:
                        for f in range(2):
                            acc_wait(e, pr, u, f)
                            e.wait_ge(acc_free, 2 * pr)
                            if j:
                                e.wait_ge(sem("h_hi_made"), KD + NF + 2 * j)
                            e.tensor_tensor(tmp[:, 4 + f, :], acc(f), tmp[:, 2 + f, :], ALU.mult).then_inc(acc_free, 1)
                for f in range(2):
                    t = 2 * j + f
                    y, ch = tmp[:, 6 + f, :], tmp[:, 4 + f, :]
                    e.wait_ge(sem("ch_rows"), t + 1)
                    e.tensor_tensor(y[:, T:N], y[:, T:N], past_conv[:, :, t], ALU.add)
                    link(e.scalar_tensor_tensor(y[:, 1:T], ch[:, 0:T - 1], vec(V_LN, COL_SCW + KD + t), y[:, 1:T], ALU.mult, ALU.add))
                    link(e.scalar_tensor_tensor(y[:, 2:T], ch[:, 0:T - 2], vec(V_LN, COL_SCW + t), y[:, 2:T], ALU.mult, ALU.add))
                    e.tensor_tensor(y, y, tmp[:, f, :], ALU.mult).then_inc(sem("sc_gated"), 1)
                for f in range(2):
                    t = 2 * j + f
                    e.wait_ge(sem("h_hi_made"), KD + NF + t + 1)
                    e.tensor_tensor(h_lo[:, t, :], tmp[:, 6 + f, :], h_hi[:, t, :].bitcast(F32), ALU.subtract
                                    ).then_inc(sem("h_made"), 1)
            residual(2, U_SCOUT, PR_SCOUT, 1)
            norm(2)
            ffn(1)


INPUTS = ["x_prompt", "x_sample", "state_gla", "state_ret", "state_conv", "state_ffn", "w_mix_in", "w_gla_gate_up",
          "b_gla_gate", "g_gla_norm", "g_ret_norm", "b_ret_norm", "w_mix_out", "w_sc_in", "w_sc_dw", "b_sc_dw",
          "w_sc_out", "ln1_g", "ln1_b", "w_ffn_in", "w_ffn_dw", "b_ffn_dw", "w_ffn_out", "ln2_g", "ln2_b"]
OUTPUTS = [("y_prompt", (1, T, D)), ("y_sample", (NS, 1, D)), ("gla_p", (1, 1, GH, GDK, DV)),
           ("gla_s", (1, NS, GH, GDK, DV)), ("ret_p", (1, 1, RH, RDK, DV)), ("ret_s", (1, NS, RH, RDK, DV)),
           ("conv_p", (1, 1, 2, D)), ("conv_s", (1, NS, 2, D)), ("ffn_p", (DEPTH, 1, 2, 2 * FF)),
           ("ffn_s", (DEPTH, NS, 2, 2 * FF))]


def kernel(**inputs):
    import concourse.bacc as bacc
    from concourse.bass_utils import run_bass_kernel_spmd

    nc = bacc.Bacc("TRN2", target_bir_lowering=False, num_devices=1, dynamic_dma_scratch_size=1024)
    ident, decay, rotary, masks = host_constants()
    arrays = {n: np.ascontiguousarray(inputs[n]) for n in INPUTS}
    arrays |= {"c_ident": ident, "c_decay": decay, "c_rotary": rotary.reshape(P, 2, N), "c_masks": masks}
    args = {n: nc.dram_tensor("in_" + n, a.shape, mybir.dt.from_np(a.dtype), kind="ExternalInput").ap()
            for n, a in arrays.items()}
    for n, shape in OUTPUTS:
        args[n] = nc.dram_tensor("out_" + n, shape, F32, kind="ExternalOutput").ap()
    build(nc, **args)
    r = run_bass_kernel_spmd(nc, [{"in_" + n: a for n, a in arrays.items()}], core_ids=[0])
    return tuple(r.results[0]["out_" + n] for n, _ in OUTPUTS)
```

```python
from contextlib import ExitStack

import numpy as np
import concourse.bass as bass
from concourse import mybir
from concourse.alu_op_type import AluOpType as ALU

ACT = mybir.ActivationFunctionType
F32 = mybir.dt.float32
F32R = mybir.dt.float32r
U8 = mybir.dt.uint8

P = 128
D = 1024
KD = D // P
T = 512
NS = 8
N = T + NS
HA = 256
FF = 2816
NF = FF // P
NU = 2 * NF
CW = 3
GH, GDK, DV, RH, RDK = 4, 64, 128, 4, 128
RANK = 16
C = 128
NC = T // C
LEVELS = 7
EPS = 1e-5
DEPTH = 2
PAST = 4096
ALPHA = (2 * DEPTH) ** 0.25
TAU = 16.0
A_LR = 2 * GH * GDK + GH * DV
MIX_IN = 3600

PARTS = [("q_g", 0, 2), ("k_g", 256, 2), ("v_g", 512, 4), ("q_r", 1552, 4), ("k_r", 2064, 4), ("v_r", 2576, 4),
         ("r_g", 1040, 4), ("g_r", 3088, 4)]
NZ = sum(n for _, _, n in PARTS)

V_LN = 4
COL_LN1G, COL_LN1B, COL_LN2G, COL_LN2B = 0, 16, 32, 48
COL_SCW, COL_SCB, COL_BG, COL_GG, COL_GR, COL_BR = 64, 88, 96, 98, 99, 103
N_V = 107

GAMMA = [1.0 - 2.0 ** (-5.0 - h) for h in range(RH)]


def host_constants():
    ident = np.eye(P, dtype=np.float32)
    s = np.arange(C)[:, None]
    t = np.arange(C)[None, :]
    g = np.array(GAMMA, np.float64)
    dec = np.stack([np.where(s <= t, np.power(x, (t - s).astype(np.float64)), 0.0) * RDK ** -0.5 for x in g], 1)
    gpow = np.broadcast_to(np.power(g[:, None], np.arange(1, C + 1)[None, :])[None], (P, RH, C))
    kdec = np.power(g[None, :], (C - 1 - np.arange(C))[:, None].astype(np.float64)) * RDK ** -0.5
    inv = (np.float32(1.0) / np.power(np.float32(10000.0), np.arange(0, RDK, 2, dtype=np.float32) / np.float32(RDK))).astype(np.float32)
    pos = np.concatenate([np.arange(T), np.full(NS, PAST)]).astype(np.float32)
    ang = inv[:, None] * pos[None, :]
    cos = np.concatenate([np.cos(ang), np.cos(ang)], 0)
    sin = np.concatenate([np.sin(ang), -np.sin(ang)], 0)
    f = np.concatenate([dec.reshape(P, -1), gpow.reshape(P, -1), kdec], 1).astype(np.float32)
    rot = np.concatenate([cos, sin], 1).astype(np.float32)
    masks = []
    for l in range(LEVELS):
        h = C >> (l + 1)
        masks.append((s // (2 * h) == t // (2 * h)) & (s % (2 * h) < h) & (t % (2 * h) >= h))
    masks.append(s == t)
    m = np.stack(masks, 1).astype(np.float32)
    return ident, np.ascontiguousarray(f), np.ascontiguousarray(rot), np.ascontiguousarray(m)


def build(nc, x_prompt, x_sample, state_gla, state_ret, state_conv, state_ffn, w_mix_in, w_gla_gate_up,
          b_gla_gate, g_gla_norm, g_ret_norm, b_ret_norm, w_mix_out, w_sc_in, w_sc_dw, b_sc_dw, w_sc_out,
          ln1_g, ln1_b, w_ffn_in, w_ffn_dw, b_ffn_dw, w_ffn_out, ln2_g, ln2_b,
          c_ident, c_decay, c_rotary, c_masks,
          y_prompt, y_sample, gla_p, gla_s, ret_p, ret_s, conv_p, conv_s, ffn_p, ffn_s):
    ctx = ExitStack()
    base = nc.sbuf_base
    base += -base % 64
    room = nc.sbuf_usable_end - base - 64
    at = [base]

    def place(name, shape, dt, offset=None):
        n = int(np.prod(shape[1:])) * (1 if dt == U8 else 4)
        o = at[0] if offset is None else offset
        if offset is None:
            at[0] += n + -n % 64
        assert at[0] <= base + room and o + n <= base + room
        return nc.alloc_sbuf_tensor_at(name, shape, dt, offset=o)

    with ctx:
        slab = ctx.enter_context(nc.sbuf_tensor("slab", [P, room // 4], F32))
        B = 4 * N
        x32 = place("x32", [P, KD, N], F32)
        y_tok = place("y_tok", [P, NC + 1, D], F32, at[0])
        gain_rows = place("gain_rows", [P, D], F32, at[0] + (NC + 1) * D * 4)
        bias_rows = place("bias_rows", [P, D], F32, at[0] + (NC + 2) * D * 4)
        x_hi = place("x_hi", [P, KD, N], F32R)
        x_lo = place("x_lo", [P, KD, N], F32R)
        H = at[0]
        h_hi = place("h_hi", [P, NF, N], F32R, H)
        h_lo = place("h_lo", [P, NF, N], F32R, H + NF * B)
        at[0] = H + 2 * NF * B
        w_raw = place("w_raw", [P, 2, KD, 256], F32)
        w_hi = place("w_hi", [P, 2, KD, 256], F32R)
        w_lo = place("w_lo", [P, 2, KD, 256], F32R)

        ident = place("ident", [P, P], F32)
        ones = place("ones", [P, P], F32)
        centering = place("centering", [P, P], F32)
        vecs = place("vecs", [P, 5, P], F32)
        past_ffn = place("past_ffn", [P, DEPTH, NS, NU], F32)
        past_conv = place("past_conv", [P, NS, KD], F32)
        w_up = place("w_up", [RANK, 2 * P], F32, at[0])
        last_rows = place("last_rows", [P, NU, 2 + NS], F32)
        eps = place("eps", [P, 1], F32)
        eps_copy = place("eps_copy", [P, 1], F32)
        ones_one = place("ones_one", [P, 1], F32)

        def slot(name, first, shape):
            return place(name, shape, F32, H + first * B)

        zt = {"q_g": slot("q_g", 0, [P, 2, N]), "k_g": slot("k_g", 2, [P, 2, N]), "q_r": slot("q_r", 4, [P, 4, N]),
              "v_g": slot("v_g", 8, [P, 4, N]), "v_r": slot("v_r", 12, [P, 4, N]), "r_g": slot("r_g", 16, [P, 4, N]),
              "k_r": slot("k_r", 22, [P, 4, N]), "g_r": slot("g_r", 30, [P, 4, N])}
        q_g, k_g, v_g, r_g, q_r, k_r, v_r, g_r = (zt[n] for n in ("q_g", "k_g", "v_g", "r_g", "q_r", "k_r", "v_r", "g_r"))
        o_att = [v_g[:, h, :] for h in range(GH)] + [v_r[:, h, :] for h in range(RH)]
        cum = slot("cum", 16, [P, 2, T])
        dd = slot("dd", 18, [P, 2, T])
        q_t = slot("q_t", 30, [P, 2, T])
        k_t = slot("k_t", 32, [P, 2, T])
        q_dec = slot("q_dec", 30, [P, RH, T])
        rot = slot("rot", 20, [P, 2, N])
        sc = slot("sc", 26, [P, 4, T])
        gate_t = slot("gate_t", 26, [P, 2, N])
        v_tok = slot("v_tok", 34, [P, NC, 512])
        gate_m = slot("gate_m", 34, [P, 2, N])
        k_tok = slot("k_tok", 38, [P, NC, 512])
        log_a = slot("log_a", 42, [P, 2, N])
        rot_t = slot("rot_t", 42, [P, 2, N])
        sq = slot("sq", 40, [P, 4, N])
        tok_r = place("tok_r", [NS, 8, P], F32, H + 38 * B)
        v_blk2 = place("v_blk2", [NS, NS, DV], F32, H + 34 * B)
        x_tok = slot("x_tok", 8, [P, 5, D])
        v_rows = slot("v_rows", 34, [P, 5, P])
        s_rows0 = place("s_rows0", [NU, 2 * NS, P], F32, H + 34 * B + 2560)
        past_t = slot("past_t", 22, [P, NS, NU])
        a_lr = place("a_lr", [RANK, N], F32, H + 24 * B)
        mask_rows = slot("mask_rows", 40, [P, LEVELS + 1, P])

        shared = at[0]
        masks = place("masks", [P, LEVELS + 1, P], U8)
        decay = place("decay", [P, 2 * RH * C + RH], F32)
        samp = place("samp", [P, 2, NS, DV], F32)
        s_rows1 = place("s_rows1", [NU, 2 * NS, P], F32, at[0] - 8192)
        state = place("state", [P, 2, 4, DV], F32)
        state_g = place("state_g", [P, NC, 2, DV], F32, at[0] - 4096)
        tok_s = place("tok_s", [NS, 8, P], F32)
        v_blk = place("v_blk", [NS, NS, DV], F32)
        s_rows2 = place("s_rows2", [2 * NS, KD, P], F32, at[0] - 4096)
        e_last = place("e_last", [P, 2, NC], F32)
        a_samp = place("a_samp", [P, 2, NS], F32)
        inv = place("inv", [P, KD, 5], F32)
        end_att = at[0]
        at[0] = shared
        tmp = place("tmp", [P, 8, N], F32)
        row_out = place("row_out", [NU, 2 + NS, P], F32)
        ln_sum = place("ln_sum", [P, N], F32)
        ln_inv = place("ln_inv", [P, 2, 5], F32)
        ln_var = place("ln_var", [P, 2, 5], F32)
        ln_sq, ln_s1, ln_s2 = tmp[:, 0:4, :], tmp[:, 4, :], tmp[:, 5, :]
        at[0] = max(at[0], end_att)

        ps_t = ctx.enter_context(nc.psum_tensor("ps", [P, 8 * 512], F32))
        ps = ps_t[:, :]

        def bank(b, rows=P, lo=0, n=512):
            return ps_t[0:rows, b * 512 + lo:b * 512 + lo + n]

        def acc(slot):
            o = slot * 1024 + 256
            return ps_t[:, o:o + N]

        HALVES = [(0, HA), (HA, N)]

        def acc_half(slot, half):
            lo, hi = HALVES[half]
            o = slot * 1024 + 256
            return ps_t[:, o + lo:o + hi]

        made = {}

        def sem(name):
            if name not in made:
                made[name] = ctx.enter_context(nc.semaphore(name))
            return made[name]

        def bc(ap, dim, n):
            a = ap.unsqueeze(dim)
            return a.broadcast_to([*a.shape[:dim], n, *a.shape[dim + 1:]])

        units = [(w_mix_in[0], 0, KD, A_LR, P)]
        z_of = [None]
        for name, c0, n in PARTS:
            for j in range(0, n, 2):
                units.append((w_mix_in[0], 0, KD, c0 + j * P, 256))
                z_of.append((name, j))
        U_MIXOUT = len(units)
        units += [(w_mix_out[0], 0, KD, 256 * j, 256) for j in range(4)]
        U_IN, U_OUT = [0, 0], [0, 0]

        def ffn_units(l):
            U_IN[l] = len(units)
            for j in range(NF // 2):
                units.append((w_ffn_in[l], 0, KD, 256 * j, 256))
                units.append((w_ffn_in[l], 0, KD, FF + 256 * j, 256))
            U_OUT[l] = len(units)
            for j in range(4):
                for k0, k in K_GROUPS:
                    units.append((w_ffn_out[l], k0, k, 256 * j, 256))

        K_GROUPS = [(0, 8), (8, 8), (16, 6)]
        ffn_units(0)
        U_SCIN = len(units)
        for j in range(4):
            for part in range(3):
                units.append((w_sc_in[0], 0, KD, part * D + 256 * j, 256))
        U_SCOUT = len(units)
        units += [(w_sc_out[0], 0, KD, 256 * j, 256) for j in range(4)]
        ffn_units(1)
        n_units = len(units)
        Y_ORDER = (0, 1, 3, 2, NC)
        NEXT = [U_IN[0], U_SCIN, U_IN[1]]

        Q_MIXIN = 0
        Q_MIXOUT = Q_MIXIN + 2 + NZ
        Q_IN = [Q_MIXOUT + KD, 0]
        Q_OUT = [Q_IN[0] + NU, 0]
        Q_SCIN = Q_OUT[0] + KD
        Q_SCOUT = Q_SCIN + 3 * KD
        Q_IN[1] = Q_SCOUT + KD
        Q_OUT[1] = Q_IN[1] + NU

        raw_loaded = [sem("raw_loaded0"), sem("raw_loaded1")]
        hi_made, lo_made = sem("hi_made"), sem("lo_made")
        tile0_done, unit_used, acc_free = sem("tile0_done"), sem("unit_used"), sem("acc_free")

        PR_MIXIN = 1
        PR_MIXOUT = PR_MIXIN + NZ // 2
        PR_IN = [PR_MIXOUT + 4, 0]
        PR_OUT = [PR_IN[0] + NF, 0]
        PR_SCIN = PR_OUT[0] + 4
        PR_SCOUT = PR_SCIN + 12
        PR_IN[1] = PR_SCOUT + 4
        PR_OUT[1] = PR_IN[1] + NF

        def load_unit(e, u):
            w, k0, k, c0, c = units[u]
            if u >= 2:
                e.wait_ge(lo_made, u - 1)
            e.dma_start(w_raw[:, u % 2, 0:k, 0:c],
                        w[k0 * P:(k0 + k) * P, c0:c0 + c].rearrange("(k p) c -> p k c", p=P)
                        ).then_inc(raw_loaded[u % 2], 16)

        def make_hi(e, u, par, loaded, k=KD, c=256):
            e.wait_ge(raw_loaded[par], loaded)
            if not (isinstance(u, int) and u < 2):
                e.wait_ge(unit_used, u - 1)
            e.activation(w_hi[:, par, 0:k, 0:c], w_raw[:, par, 0:k, 0:c], ACT.Copy).then_inc(hi_made, 1)

        def make_lo(e, u, par, k=KD, c=256):
            e.wait_ge(hi_made, u + 1)
            e.tensor_tensor(w_lo[:, par, 0:k, 0:c], w_raw[:, par, 0:k, 0:c],
                            w_hi[:, par, 0:k, 0:c].bitcast(F32), ALU.subtract).then_inc(lo_made, 1)

        def stage_hi(e, u):
            if u < n_units:
                make_hi(e, u, u % 2, 16 * (u // 2 + 1), units[u][2], units[u][4])

        def stage_lo(e, u):
            if u < n_units:
                make_lo(e, u, u % 2, units[u][2], units[u][4])

        def mm_tile(e, par, f, ks, xh, xl, first=True, last=True, pieces=()):
            for half, (lo, hi) in enumerate(HALVES):
                if half:
                    for piece in pieces:
                        piece()
                out = acc_half(f, half)
                for i, k in enumerate(ks):
                    wh = w_hi[:, par, i, f * P:(f + 1) * P]
                    wl = w_lo[:, par, i, f * P:(f + 1) * P]
                    e.matmul(out, wh, xh[:, k, lo:hi], start=(first and i == 0), stop=False)
                    e.matmul(out, wh, xl[:, k, lo:hi], start=False, stop=False)
                    mm = e.matmul(out, wl, xh[:, k, lo:hi], start=False, stop=(last and i == len(ks) - 1))
            return mm

        def k_step(e, par, f, k, xh, xl, hi_ready, lo_ready):
            wh, wl = (w[:, par, k, f * P:(f + 1) * P] for w in (w_hi, w_lo))
            e.wait_ge(*hi_ready)
            for w in (wh, wl):
                for half, (lo, hi) in enumerate(HALVES):
                    e.matmul(acc_half(f, half), w, xh[:, k, lo:hi], start=(k == 0 and w is wh), stop=False)
            e.wait_ge(*lo_ready)
            for half, (lo, hi) in enumerate(HALVES):
                mm = e.matmul(acc_half(f, half), wh, xl[:, k, lo:hi], start=False, stop=(k == KD - 1))
            return mm

        def mm_units(e, u, pr, n, par, xh, xl):
            for j in range(n):
                e.wait_ge(lo_made, u + j + 1)
                for f, done in enumerate((tile0_done, unit_used)):
                    e.wait_ge(acc_free, 2 * (pr + j) + f - 1)
                    mm_tile(e, (par + j) % 2, f, range(KD), xh, xl).then_inc(done, 1)

        def acc_wait(e, pr, u, f):
            if f == 0:
                e.wait_ge(tile0_done, pr)
            else:
                e.wait_ge(unit_used, u + 1)

        def vec(g, col, n=1):
            return vecs[:, g, col:col + n]

        def ffn_vec(l, j, tile):
            return vecs[:, 2 * l + j // 2, bass.ds((j % 2) * NU + tile, 1)]

        block = ctx.enter_context(nc.Block())

        v_blocks = [v_blk, v_blk2]
        stored = sem("stored")
        n_stored = [0]

        @block.sync
        def _(e):
            load, vec_loaded = sem("x_loaded"), sem("vec_loaded")
            e.dma_start(ident[:, :], c_ident).then_inc(load, 16)
            x_rows = x_prompt[0].rearrange("(t p) d -> p t d", p=P)
            e.dma_start(x_tok[:, 0:4, 0:D // 2], x_rows[:, :, 0:D // 2]).then_inc(load, 16)
            e.dma_start(x_tok[0:NS, 4, :], x_sample[:, 0, :]).then_inc(load, 16)
            e.dma_start(x_tok[:, 0:4, D // 2:D], x_rows[:, :, D // 2:D]).then_inc(sem("x_rest_loaded"), 16)
            load_unit(e, 0)
            load_unit(e, 1)
            def rows(g, r, src):
                n = src.shape[0]
                e.dma_start(v_rows[r:r + n, g, :], src).then_inc(vec_loaded, 16)
            for l in range(DEPTH):
                for j in range(4):
                    src = w_ffn_dw[l, j] if j < 3 else b_ffn_dw[l]
                    rows(2 * l + j // 2, (j % 2) * NU, src.rearrange("(t p) -> t p", p=P))
            for r, src in ((COL_LN1G, ln1_g), (COL_LN1B, ln1_b), (COL_LN2G, ln2_g), (COL_LN2B, ln2_b),
                           (COL_SCW, w_sc_dw[0]), (COL_SCB, b_sc_dw), (COL_BG, b_gla_gate),
                           (COL_GG, g_gla_norm), (COL_GR, g_ret_norm), (COL_BR, b_ret_norm)):
                rows(V_LN, r, src.rearrange("l (t p) -> (l t) p", p=P))
            for l, dst in ((0, s_rows0), (1, s_rows1)):
                e.dma_start(dst[:, :, :], state_ffn[l].rearrange("b j (t p) -> t (b j) p", p=P)
                            ).then_inc(sem("states_loaded"), 16)
            e.dma_start(s_rows2[:, :, :], state_conv[0].rearrange("b j (t p) -> (b j) t p", p=P)
                        ).then_inc(sem("states_loaded"), 16)
            e.dma_start(decay[:, :], c_decay).then_inc(sem("tables_loaded"), 16)
            e.dma_start(w_up[:, :], w_gla_gate_up[0]).then_inc(sem("tables_loaded"), 16)
            for l in range(DEPTH):
                e.dma_start(ffn_s[l, :, 0, :], state_ffn[l, :, 1, :]).then_inc(stored, 16)
            e.dma_start(conv_s[0, :, 0, :], state_conv[0, :, 1, :]).then_inc(stored, 16)
            n_stored[0] += 3
            e.wait_ge(sem("x_turned"), 8)
            e.dma_start(mask_rows[:, :, :], c_masks).then_inc(sem("tables_loaded"), 16)
            e.dma_start(rot[:, :, :], c_rotary).then_inc(sem("rot_loaded"), 16)
            def store_rows(n, tiles, p_dst, s_dst):
                e.wait_ge(sem("rows_out"), n)
                e.dma_start(p_dst.rearrange("n (t p) -> t n p", p=P), row_out[0:tiles, 0:2, :]
                            ).then_inc(sem("rows_stored"), 16)
                e.dma_start(s_dst.rearrange("b (t p) -> t b p", p=P), row_out[0:tiles, 2:2 + NS, :]
                            ).then_inc(sem("rows_stored"), 16)

            for u in range(2, 8):
                load_unit(e, u)
            e.wait_ge(sem("past_turned"), 3)
            for i in range(2):
                for j in range(2):
                    e.dma_start(samp[j * GDK:(j + 1) * GDK, i, :, :],
                                state_gla[0, :, 2 * i + j].rearrange("b d v -> d b v")
                                ).then_inc(sem("samp_loaded%d" % i), 16)
            for u in range(8, U_OUT[0] + 8):
                load_unit(e, u)
            store_rows(1, NU, ffn_p[0, 0], ffn_s[0, :, 1, :])
            for u in range(U_OUT[0] + 8, U_SCOUT + 4):
                load_unit(e, u)
            store_rows(2, KD, conv_p[0, 0], conv_s[0, :, 1, :])
            for u in range(U_SCOUT + 4, U_OUT[1] + 8):
                load_unit(e, u)
            e.wait_ge(unit_used, U_OUT[1])
            e.dma_start(gain_rows[:, :], ln2_g[DEPTH - 1].partition_broadcast(P)).then_inc(sem("ln_rows_loaded"), 16)
            e.dma_start(bias_rows[:, :], ln2_b[DEPTH - 1].partition_broadcast(P)).then_inc(sem("ln_rows_loaded"), 16)
            store_rows(3, NU, ffn_p[1, 0], ffn_s[1, :, 1, :])
            for u in range(U_OUT[1] + 8, n_units):
                load_unit(e, u)
            for j, ready, count in ((0, "y_biased", 1), (2, "y_out", 1), (1, "y_biased", 2), (3, "y_biased", 3)):
                e.wait_ge(sem(ready), count)
                e.dma_start(y_prompt[0, j * P:(j + 1) * P, :], y_tok[:, j, :]).then_inc(sem("y_stored"), 16)
            e.wait_ge(sem("y_out"), 2)
            e.dma_start(y_sample[:, 0, :], y_tok[P - NS:P, NC, :]).then_inc(sem("y_stored"), 16)
            e.wait_ge(stored, 16 * n_stored[0])
            e.wait_ge(sem("rows_stored"), 96)
            e.wait_ge(sem("y_stored"), 80)

        @block.tensor
        def _(e):
            e.wait_ge(sem("x_loaded"), 48)
            for f in range(KD):
                if f == KD // 2:
                    e.wait_ge(sem("x_rest_loaded"), 16)
                if f >= 4:
                    e.wait_ge(sem("x_copied"), f - 3)
                for j in range(5):
                    n = P if j < 4 else NS
                    o = (f % 4) * 1024 + 256 + j * P
                    tr = e.transpose(ps_t[:, o:o + n], x_tok[0:n, j, f * P:(f + 1) * P], ident[0:n, 0:n])
                tr.then_inc(sem("x_turned"), 1)
            e.wait_ge(sem("x_copied"), KD)
            e.wait_ge(lo_made, 1)
            for k in range(KD):
                mm = k_step(e, 0, 0, k, x_hi, x_lo, (sem("x_hi_made"), k + 1), (sem("x_made"), k + 1))
            mm.then_inc(unit_used, 1)
            e.wait_ge(sem("vec_loaded"), 18 * 16)
            for g in range(5):
                n = 2 * NU if g < V_LN else N_V
                tr = e.transpose(bank(4, P, g * 88, n), v_rows[0:n, g, :], ident[0:n, 0:n])
            tr.then_inc(sem("vecs_turned"), 1)
            e.wait_ge(sem("states_loaded"), 48)
            for t in range(KD):
                tr = e.transpose(bank(7, P, t * 16, 16), s_rows2[:, t, :], ident[0:16, 0:16])
            tr.then_inc(sem("past_turned"), 1)
            def turn_past(src):
                for r in range(2 * NS):
                    tr = e.transpose(bank(5 + r // 8, P, (r % 8) * NU, NU), src[:, r, :], ident[0:NU, 0:NU])
                tr.then_inc(sem("past_turned"), 1)

            turn_past(s_rows0)
            def unit_tile(u, f, pieces=()):
                if f == 0:
                    e.wait_ge(lo_made, u + 1)
                e.wait_ge(acc_free, 2 * u + f - 1)
                mm_tile(e, u % 2, f, range(KD), x_hi, x_lo, pieces=pieces).then_inc((tile0_done, unit_used)[f], 1)

            def turn_past_1():
                e.wait_ge(sem("past_made"), 2)
                turn_past(s_rows1)

            unit_tile(1, 0)
            unit_tile(1, 1, [turn_past_1])
            e.wait_ge(sem("tables_loaded"), 48)
            e.wait_ge(sem("vecs_made"), 1)
            e.wait_ge(sem("past_made"), DEPTH + 1)
            for g in range(2):
                for half, (lo, hi) in enumerate(HALVES):
                    mm = e.matmul(acc_half(2 + g, half), w_up[:, g * P:(g + 1) * P], a_lr[:, lo:hi], start=True, stop=True)
            mm.then_inc(sem("gate_summed"), 1)
            unit_tile(2, 0)
            unit_tile(2, 1)

            def level(n):
                if n == 0:
                    e.wait_ge(sem("gate_read"), 1)
                    e.wait_ge(sem("q_scaled"), 1)
                else:
                    e.wait_ge(sem("level_made"), n)
                    e.wait_ge(sem("level_added"), n)
                for h in range(GH):
                    p = slice((h % 2) * GDK, (h % 2 + 1) * GDK)
                    for c in range(NC):
                        t = slice(c * C, (c + 1) * C)
                        k, q = (k_t, q_t) if n else (k_g, q_g)
                        mm = e.matmul(bank(4 + h, P, c * C, C), k[p, h // 2, t], q[p, h // 2, t], start=True, stop=True)
                mm.then_inc(sem("level_summed"), 1)

            def gla_values():
                e.wait_ge(sem("level_added"), LEVELS + 1)
                for c in range(NC):
                    for h in range(GH):
                        tr = e.transpose(bank(4 + c, P, h * DV, DV), v_g[:, h, c * C:(c + 1) * C], ident[:, :])
                tr.then_inc(sem("gv_turned"), 1)

            def gla_keys():
                e.wait_ge(sem("gk_decayed"), 1)
                e.wait_ge(sem("gv_copied"), 1)
                for c in range(NC):
                    for g in range(2):
                        tr = e.transpose(bank(4 + c // 2, P, (c % 2) * 256 + g * P, P), k_t[:, g, c * C:(c + 1) * C], ident[:, :])
                tr.then_inc(sem("gk_turned"), 1)

            def gla_increments(cs):
                e.wait_ge(sem("gk_copied"), 1)
                for c in cs:
                    if c >= 2:
                        e.wait_ge(sem("gla_state"), c - 1)
                    for g in range(2):
                        mm = e.matmul(bank(6 + c % 2, P, g * 256, 256), k_tok[:, c, g * P:(g + 1) * P],
                                      v_tok[:, c, g * 256:(g + 1) * 256], start=True, stop=True)
                    mm.then_inc(sem("gla_inc"), 1)

            def gla_outputs():
                e.wait_ge(sem("gq_decayed"), 1)
                e.wait_ge(sem("gla_state"), NC)
                for h in range(GH):
                    p = slice((h % 2) * GDK, (h % 2 + 1) * GDK)
                    for c in range(NC):
                        t = slice(c * C, (c + 1) * C)
                        out = bank(4 + h, P, c * C, C)
                        mm = e.matmul(out, v_tok[:, c, h * DV:(h + 1) * DV], sc[:, h, t], start=True, stop=(c == 0))
                        if c:
                            mm = e.matmul(out, state_g[p, c - 1, h // 2, :], q_t[p, h // 2, t], start=False, stop=True)
                mm.then_inc(sem("gla_out"), 1)

            def ret_scores():
                e.wait_ge(sem("gla_copied"), 1)
                e.wait_ge(sem("rotated"), 2 * RH)
                for h in range(RH):
                    for c in range(NC):
                        t = slice(c * C, (c + 1) * C)
                        mm = e.matmul(bank(4 + h, P, c * C, C), k_r[:, h, t], q_r[:, h, t], start=True, stop=True)
                mm.then_inc(sem("rs_summed"), 1)

            def ret_keys():
                e.wait_ge(sem("rs_decayed"), 1)
                for c in range(NC):
                    for h in range(RH):
                        tr = e.transpose(bank(4 + c, P, h * RDK, RDK), k_r[:, h, c * C:(c + 1) * C], ident[:, :])
                tr.then_inc(sem("rk_turned"), 1)

            def gla_samples_turn():
                e.wait_ge(sem("rk_decayed"), 1)
                for j in range(2):
                    e.transpose(bank(4, NS, j * P, P), k_g[:, j, T:N], ident[:, :])
                for j in range(4):
                    tr = e.transpose(bank(5, NS, j * P, P), v_g[:, j, T:N], ident[:, :])
                tr.then_inc(sem("gs_turned"), 1)

            def ret_values():
                e.wait_ge(sem("gs_copied"), 1)
                e.wait_ge(acc_free, 2 * 11)
                for c in range(NC):
                    for h in range(RH):
                        tr = e.transpose(bank(4 + c, P, h * DV, DV), v_r[:, h, c * C:(c + 1) * C], ident[:, :])
                tr.then_inc(sem("rv_turned"), 1)

            def ret_chunks(cs):
                e.wait_ge(sem("rv_copied"), 1)
                for c in cs:
                    t = slice(c * C, (c + 1) * C)
                    if c >= 2:
                        e.wait_ge(sem("ret_state"), c - 1)
                    for h in range(RH):
                        mm = e.matmul(bank(6 + c % 2, P, h * DV, DV), k_tok[:, c, h * RDK:(h + 1) * RDK],
                                      v_tok[:, c, h * DV:(h + 1) * DV], start=True, stop=True)
                    mm.then_inc(sem("ret_inc"), 1)
                    if c:
                        e.wait_ge(sem("ret_state"), c)
                    if c >= 2:
                        e.wait_ge(sem("ret_copied"), c - 1)
                    for h in range(RH):
                        out = bank(4 + c % 2, P, h * C, C)
                        mm = e.matmul(out, v_tok[:, c, h * DV:(h + 1) * DV], sc[:, h, t], start=True, stop=(c == 0))
                        if c:
                            mm = e.matmul(out, state[:, (c - 1) % 2, h, :], q_dec[:, h, t], start=False, stop=True)
                    mm.then_inc(sem("ret_out"), 1)

            def ret_samples_turn():
                e.wait_ge(sem("ret_copied"), NC)
                e.wait_ge(sem("ret_state"), NC)
                for j in range(4):
                    e.transpose(bank(6, NS, j * P, P), k_r[:, j, T:N], ident[:, :])
                    tr = e.transpose(bank(7, NS, j * P, P), v_r[:, j, T:N], ident[:, :])
                tr.then_inc(sem("rs_turned"), 1)

            def outer(i):
                b = 4 + 2 * (i % 2)
                e.wait_ge(sem("rs_copied"), 1)
                if i >= 2:
                    e.wait_ge(sem("samp_out"), i - 1)
                for h in ((2 * i, 2 * i + 1) if i < 2 else (i + 2,)):
                    e.wait_ge(sem("v_blk_made"), h + 1)
                    for half in range(2):
                        rhs = v_blocks[h % 2][:, 4 * half:4 * half + 4, :]
                        if i < 2:
                            j = h % 2
                            mm = e.matmul(ps_t[j * GDK:(j + 1) * GDK, (b + half) * 512:(b + half + 1) * 512],
                                          tok_s[:, i, j * GDK:(j + 1) * GDK], rhs, start=True, stop=True)
                        else:
                            mm = e.matmul(bank(b + half), tok_r[:, i - 2, :], rhs, start=True, stop=True)
                    mm.then_inc(sem("outer_summed"), 1)

            def sample_out(i):
                b = 4 + 2 * (i % 2)
                e.wait_ge(sem("samp_made"), i + 1)
                if i < 2:
                    for j in range(2):
                        p = slice(j * GDK, (j + 1) * GDK)
                        for s in range(NS):
                            mm = e.matmul(bank(b + j, P, s, 1), samp[p, i, s, :], q_g[p, i, T + s:T + s + 1], start=True, stop=True)
                else:
                    for s in range(NS):
                        mm = e.matmul(bank(b, P, s, 1), samp[:, i % 2, s, :], q_r[:, i - 2, T + s:T + s + 1], start=True, stop=True)
                mm.then_inc(sem("samp_read"), 1)

            def token_sums(out, squares, start=True, stop=True):
                for j in range(5):
                    t0 = j * P if j < 4 else N - P
                    mm = e.matmul(out[:, j:j + 1], squares[:, t0:t0 + P], ones[:, 0:1], start=(start and j == 0), stop=stop,
                                  skip_group_check=True)
                return mm

            def spread(slot_, inv_):
                for j in range(5):
                    n = P if j < 4 else NS
                    o = slot_ * 1024 + 256 + j * P
                    mm = e.matmul(ps_t[:, o:o + n], inv_[:, j:j + 1].broadcast_to([P, P]), ident[:, P - n:P],
                                  start=True, stop=True)
                return mm

            def hn_center(hs):
                e.wait_ge(sem("samp_out"), 2 + RH)
                for h in hs:
                    if h < GH + 2:
                        e.wait_ge(sem("hn_scaled"), h - 1)
                    else:
                        e.wait_ge(sem("hn_centered"), h - GH - 1)
                    for half, (lo, hi) in enumerate(HALVES):
                        mm = e.matmul(acc_half(2 + h % 2, half), centering[:, :], o_att[h][:, lo:hi], start=True, stop=True)
                    mm.then_inc(sem("hn_mean"), 1)

            def hn_sums(grp):
                if grp:
                    e.wait_ge(sem("hn_centered"), RH)
                else:
                    e.wait_ge(sem("samp_out"), 2 + RH)
                for h in range(4 * grp, 4 * grp + 4):
                    e.wait_ge(sem("hn_squared"), h + 1)
                    mm = token_sums(bank(4, P, 8 * h, 5), sq[:, h % 4, :])
                mm.then_inc(sem("hn_var"), 1)

            def hn_spread(h):
                e.wait_ge(sem("hn_inv"), h // 4 + 1)
                if h % 4 >= 2:
                    e.wait_ge(sem("hn_scaled"), h - 1)
                spread(2 + h % 2, inv[:, h, :]).then_inc(sem("hn_spread"), 1)

            after = [[lambda n=n: level(n)] for n in range(LEVELS + 1)] + [
                [gla_values], [gla_keys], [lambda: gla_increments((0, 1))], [lambda: gla_increments((2, 3))],
                [gla_outputs], [ret_scores], [ret_keys], [gla_samples_turn], [lambda: ret_chunks((0, 1))],
                [ret_samples_turn], [lambda: outer(1), lambda: sample_out(0)], [lambda: outer(3), lambda: sample_out(2)],
                [lambda: outer(5), lambda: sample_out(4)], [lambda: hn_sums(0)], [lambda: hn_spread(2), lambda: hn_spread(3)],
                [lambda: hn_center((GH + 2, GH + 3))]]
            inside = [[] for _ in range(16)] + [
                [ret_values], [lambda: ret_chunks((2, 3))], [lambda: outer(0)],
                [lambda: outer(2), lambda: sample_out(1)], [lambda: outer(4), lambda: sample_out(3)],
                [lambda: sample_out(5)], [lambda: hn_spread(0), lambda: hn_spread(1)], [lambda: hn_center((GH, GH + 1))]]
            for n in range(24):
                unit_tile(3 + n // 2, n % 2, inside[n])
                for piece in after[n]:
                    piece()
            hn_sums(1)

            def ln_shift(n):
                e.wait_ge(sem("ln_summed"), n + 1)
                for half, (lo, hi) in enumerate(HALVES):
                    mm = e.matmul(acc_half(2, half), ones[:, :], ln_sum[:, lo:hi], start=True, stop=True)
                mm.then_inc(sem("ln_shift"), 1)

            def turn_x(tiles):
                for t in tiles:
                    e.wait_ge(sem("ln_centered"), KD * (2 * DEPTH - 1) + max(t, 5) + 1)
                    if t >= 2:
                        e.wait_ge(sem("y_copied"), t - 1)
                    for j in range(NC):
                        tr = e.transpose(bank(4 + t % 2, P, j * P, P), x32[:, t, j * P:(j + 1) * P], ident[:, :])
                    tr.then_inc(sem("y_turned"), 1)

            def ln_sums(n):
                e.wait_ge(sem("ln_added"), (KD - 2) * (n + 1))
                token_sums(bank(6, P, 0, 5), ln_s2, True, False)
                e.wait_ge(sem("ln_totaled"), KD * (n + 1))
                token_sums(bank(7, P, 0, 5), ln_s1).then_inc(sem("ln_var"), 1)
                if n == 2 * DEPTH - 1:
                    turn_x((KD - 2, KD - 1))
                e.wait_ge(sem("ln_squared"), KD * (n + 1))
                token_sums(bank(6, P, 0, 5), ln_sq[:, (KD - 1) % 4, :], False).then_inc(sem("ln_var"), 1)
                if n == 2 * DEPTH - 1:
                    for f in range(KD):
                        tr = e.transpose(bank(2 + f // 4, P, (f % 4) * P, P), x32[:, f, N - P:N], ident[:, :])
                    tr.then_inc(sem("y_turned"), 1)
                    return
                e.wait_ge(sem("ln_mean_made"), n + 1)
                spread(2, ln_inv[:, 1, :]).then_inc(sem("ln_spread"), 1)
                e.wait_ge(sem("ln_inverse"), n + 1)
                spread(3, ln_inv[:, 0, :]).then_inc(sem("ln_spread"), 1)

            def turn_rows(n):
                tiles = KD if n == 2 else NU
                e.wait_ge(*((sem("ch_rows"), KD) if n == 2 else (sem("t_made"), NU * (n // 2 + 1))))
                for r in range(2 + NS):
                    tr = e.transpose(bank(4 + r // 4, tiles, (r % 4) * P, P), last_rows[:, 0:tiles, r], ident[:, :])
                tr.then_inc(sem("rows_turned"), 1)

            def first_unit(u, pr, operand_hi, made, count, xh, xl, heads=()):
                e.wait_ge(lo_made, u + 1)
                e.wait_ge(acc_free, 2 * pr)
                first_half = [(k, f) for k in range(KD // 2) for f in range(2)]
                for k, f in first_half + [(k, f) for f in range(2) for k in range(KD // 2, KD)]:
                    if f == 0:
                        for h in (heads[k] if heads else ()):
                            hn_spread(h)
                    mm = k_step(e, u % 2, f, k, xh, xl, (operand_hi, count + k + 1), (made, count + k + 1))
                    if k == KD - 1:
                        mm.then_inc((tile0_done, unit_used)[f], 1)

            def project_out(pr, u, kgroups, n, xh, xl, count):
                per = len(kgroups)
                if per == 1:
                    first_unit(u, pr, sem("h_hi_made"), sem("h_made"), count, xh, xl, () if n else [(), (), (), (4, 5), (6,), (7,), (), ()])
                for j in range(per == 1, 4):
                    for g, (k0, k) in enumerate(kgroups):
                        e.wait_ge(lo_made, u + per * j + g + 1)
                        if j == 0:
                            e.wait_ge(sem("h_made"), count + k0 + k)
                        for f in range(2):
                            if g == 0:
                                e.wait_ge(acc_free, 2 * (pr + j) + f - 1)
                            mm = mm_tile(e, (u + per * j + g) % 2, f, range(k0, k0 + k), xh, xl, g == 0, g == per - 1)
                            if f == 1:
                                mm.then_inc(unit_used, 1)
                                if j == 1 and g == 0 and n:
                                    turn_rows(n)
                            elif g == per - 1:
                                mm.then_inc(tile0_done, 1)
                                if j == 2:
                                    if n:
                                        e.wait_ge(sem("rows_out"), n)
                                    ln_shift(n)
                            if n == 2 * DEPTH - 1 and j == 3:
                                turn_x({(0, 1): (0, 1), (1, 0): (2, 3), (1, 1): (4, 5)}.get((g, f), ()))
                ln_sums(n)

            def ffn(l):
                first_unit(U_IN[l], PR_IN[l], sem("x_hi_made"), sem("x_made"), KD * (2 * l + 1), x_hi, x_lo)
                mm_units(e, U_IN[l] + 1, PR_IN[l] + 1, 1, U_IN[l] + 1, x_hi, x_lo)
                with e.Fori(0, NF // 2 - 1) as i:
                    mm_units(e, U_IN[l] + 2 + 2 * i, PR_IN[l] + 2 + 2 * i, 2, U_IN[l], x_hi, x_lo)
                project_out(PR_OUT[l], U_OUT[l], K_GROUPS, 2 * l + 1, h_hi, h_lo, KD + (NF + KD) * l)

            project_out(PR_MIXOUT, U_MIXOUT, [(0, KD)], 0, h_hi, h_lo, 0)
            ffn(0)
            first_unit(U_SCIN, PR_SCIN, sem("x_hi_made"), sem("x_made"), KD * 2, x_hi, x_lo)
            mm_units(e, U_SCIN + 1, PR_SCIN + 1, 1, U_SCIN + 1, x_hi, x_lo)
            with e.Fori(0, 5) as i:
                mm_units(e, U_SCIN + 2 + 2 * i, PR_SCIN + 2 + 2 * i, 2, U_SCIN, x_hi, x_lo)
            project_out(PR_SCOUT, U_SCOUT, [(0, KD)], 2, h_hi, h_lo, KD + NF)
            ffn(1)

        @block.gpsimd
        def _(e):
            def split_x(f, n):
                e.wait_ge(sem("x_hi_made"), n)
                e.tensor_tensor(x_lo[:, f, :], x32[:, f, :], x_hi[:, f, :].bitcast(F32), ALU.subtract
                                ).then_inc(sem("x_made"), 1)

            for f in range(KD):
                split_x(f, f + 1)
            e.memset(q_t[:, :, :], 0.0).then_inc(sem("cleared"), 1)
            e.memset(k_t[:, :, :], 0.0).then_inc(sem("cleared"), 1)
            e.wait_ge(sem("log_a_made"), 1)
            e.memset(sc[:, :, :], 0.0).then_inc(sem("cleared"), 1)

            def blocks(h):
                if h >= 2:
                    e.wait_ge(sem("outer_summed"), h - 1)
                v = tok_s[:, 4 + h, :] if h < GH else tok_r[:, h, :]
                e.tensor_tensor(v_blocks[h % 2][:, :, :], bc(v, 1, NS), bc(ident[0:NS, 0:NS], 2, DV), ALU.mult
                                ).then_inc(sem("v_blk_made"), 1)

            e.wait_ge(sem("gla_state"), NC)
            for g in range(2):
                e.dma_start(gla_p[0, 0, 2 * g:2 * g + 2].rearrange("h d v -> (h d) v"),
                            state_g[:, NC - 1, g, :]).then_inc(sem("gla_p_stored"), 16)
            e.wait_ge(sem("ret_state"), NC)
            e.dma_start(ret_p[0, 0].rearrange("h d v -> d h v"), state[:, (NC - 1) % 2, :, :]
                        ).then_inc(sem("ret_p_stored"), 16)
            e.wait_ge(sem("gs_copied"), 1)
            blocks(0)
            e.wait_ge(sem("rs_copied"), 1)
            for h in range(1, GH + RH):
                blocks(h)
            e.wait_ge(sem("gla_p_stored"), 32)
            e.wait_ge(sem("ret_p_stored"), 16)
            for j in range(2):
                e.wait_ge(sem("samp_stored%d" % j), 32 + 16 * RH // 2)
            for n in range(2 * DEPTH):
                for t in range(1, KD - 1):
                    if t > 1:
                        e.wait_ge(sem("ln_added"), (KD - 2) * n + t - 1)
                    e.wait_ge(sem("ln_squared"), KD * n + t + 1)
                    e.tensor_tensor(ln_s2, ln_sq[:, 0, :] if t == 1 else ln_s2, ln_sq[:, t % 4, :], ALU.add
                                    ).then_inc(sem("ln_added"), 1)
                for f in range(KD if n < 2 * DEPTH - 1 else 0):
                    split_x(f, KD * (n + 1) + f + 1)
            for i, j in enumerate(Y_ORDER[:3]):
                e.wait_ge(sem("y_gained"), i + 1)
                e.tensor_tensor(y_tok[:, j, :], y_tok[:, j, :], bias_rows[:, :], ALU.add).then_inc(sem("y_biased"), 1)

        @block.scalar
        def _(e):
            step = [0]

            def link(ins):
                step[0] += 1
                ins.then_inc(sem("act_step"), 1)
                e.wait_ge(sem("act_step"), step[0])

            for f in range(KD):
                if f == 5:
                    stage_hi(e, 0)
                e.wait_ge(sem("x_copied"), f + 1)
                e.activation(x_hi[:, f, :], x32[:, f, :], ACT.Copy).then_inc(sem("x_hi_made"), 1)
            stage_hi(e, 1)
            e.wait_ge(unit_used, 1)
            link(e.activation(a_lr[:, :], acc(0)[0:RANK, :], ACT.Copy))
            e.activation(a_samp[0:1, 0, 0:1], a_lr[0:1, 0:1], ACT.Copy).then_inc(acc_free, 1)
            e.activation(a_samp[0:1, 0, 1:2], a_lr[0:1, 0:1], ACT.Copy).then_inc(acc_free, 1)

            def tile_out(u, f):
                name, j = z_of[u]
                acc_wait(e, u, u, f)
                e.activation(zt[name][:, j + f, :], acc(f), ACT.Silu if name in ("r_g", "g_r") else ACT.Copy
                             ).then_inc(acc_free, 1)

            stage_hi(e, 2)
            tile_out(1, 0)
            tile_out(1, 1)
            e.wait_ge(sem("vecs_made"), 1)
            e.wait_ge(sem("gate_summed"), 1)
            for g in range(2):
                ins = e.activation(gate_t[:, g, :], acc(2 + g), ACT.Abs, bias=vec(V_LN, COL_BG + g))
            link(ins)
            link(e.activation(gate_t[:, :, :], gate_t[:, :, :], ACT.Exp, scale=-1.0))
            e.activation(gate_t[:, :, :], gate_t[:, :, :], ACT.Ln, bias=1.0).then_inc(sem("gate_ln"), 1)
            stage_hi(e, 3)
            tile_out(2, 0)
            tile_out(2, 1)

            def decay_exp(i):
                e.wait_ge(sem("dd_made"), i + 1)
                e.activation(dd[:, :, :], dd[:, :, :], ACT.Exp, scale=1.0 / TAU).then_inc(sem("dd_exp"), 1)

            def copy_blocks(n):
                h = C >> n
                e.wait_ge(sem("level_summed"), n + 1)
                scores, sums = sc[:, :, :].rearrange("p h (c t) -> p (h c) t", t=C), ps_t[:, 2048:4096].rearrange("p (m t) -> p m t", t=C)
                for s in range(0, C, 2 * h):
                    ins = e.activation(scores[s:s + h, :, s + h:s + 2 * h], sums[s:s + h, :, s + h:s + 2 * h], ACT.Copy)
                ins.then_inc(sem("level_added"), 1)

            def gla_decays():
                e.wait_ge(sem("gk_decayed"), 1)
                e.activation(dd[:, :, :], cum[:, :, :], ACT.Exp, scale=1.0 / TAU)
                e.activation(e_last[:, :, :], cum[:, :, C - 1::C], ACT.Exp, scale=1.0 / TAU).then_inc(sem("cum_exp"), 1)

            def gla_values():
                e.wait_ge(sem("gv_turned"), 1)
                for c in range(NC):
                    ins = e.activation(v_tok[:, c, :], bank(4 + c), ACT.Copy)
                ins.then_inc(sem("gv_copied"), 1)

            def gla_keys():
                e.wait_ge(sem("gk_turned"), 1)
                for c in range(NC):
                    ins = e.activation(k_tok[:, c, 0:256], bank(4 + c // 2, P, (c % 2) * 256, 256), ACT.Copy)
                ins.then_inc(sem("gk_copied"), 1)

            def gla_outputs():
                e.wait_ge(sem("gla_out"), 1)
                for h in range(GH):
                    ins = e.activation(o_att[h][:, 0:T], bank(4 + h), ACT.Copy)
                ins.then_inc(sem("gla_copied"), 1)

            def gla_samples():
                e.wait_ge(sem("gs_turned"), 1)
                e.activation(tok_s[:, 0:2, :], bank(4, NS, 0, 256), ACT.Copy)
                e.activation(tok_s[:, 4:8, :], bank(5, NS), ACT.Copy).then_inc(sem("gs_copied"), 1)

            def ret_values():
                e.wait_ge(sem("rv_turned"), 1)
                for c in range(NC):
                    ins = e.activation(v_tok[:, c, :], bank(4 + c), ACT.Copy)
                ins.then_inc(sem("rv_copied"), 1)

            def ret_outputs(cs):
                for c in cs:
                    e.wait_ge(sem("ret_out"), c + 1)
                    e.activation(v_r[:, :, c * C:(c + 1) * C], bank(4 + c % 2).rearrange("p (h t) -> p h t", h=RH), ACT.Copy
                                 ).then_inc(sem("ret_copied"), 1)

            def ret_samples():
                e.wait_ge(sem("rs_turned"), 1)
                e.activation(tok_r[:, 0:4, :], bank(6, NS), ACT.Copy, scale=RDK ** -0.5)
                e.activation(tok_r[:, 4:8, :], bank(7, NS), ACT.Copy).then_inc(sem("rs_copied"), 1)

            def sample_out(i):
                b = 4 + 2 * (i % 2)
                was_stored = sem("samp_stored%d" % (i % 2))
                e.wait_ge(sem("samp_made"), i + 1)
                if i < 2:
                    for j in range(2):
                        e.dma_start(gla_s[0, :, 2 * i + j].rearrange("b d v -> d b v"),
                                    samp[j * GDK:(j + 1) * GDK, i, :, :]).then_inc(was_stored, 16)
                else:
                    e.dma_start(ret_s[0, :, i - 2].rearrange("b d v -> d b v"), samp[:, i % 2, :, :]).then_inc(was_stored, 16)
                e.wait_ge(sem("samp_read"), i + 1)
                for j in range(2 if i < 2 else 1):
                    ins = e.activation(o_att[2 * i + j if i < 2 else i + 2][:, T:N], bank(b + j, P, 0, NS), ACT.Copy)
                ins.then_inc(sem("samp_out"), 1)
                if i < RH:
                    e.wait_ge(was_stored, 32 + 16 * (i // 2))
                    e.dma_start(samp[:, i % 2, :, :], state_ret[0, :, i].rearrange("b d v -> d b v")
                                ).then_inc(sem("samp_loaded%d" % (i % 2)), 16)

            def hn_square(hs):
                for h in hs:
                    if h < GH:
                        e.wait_ge(sem("samp_out"), 2)
                    else:
                        e.wait_ge(sem("hn_centered"), h - GH + 1)
                    e.activation(sq[:, h % 4, :], o_att[h], ACT.Square).then_inc(sem("hn_squared"), 1)

            def hn_root(grp):
                e.wait_ge(sem("hn_var"), grp + 1)
                e.activation(inv[:, 4 * grp:4 * grp + 4, :],
                             bank(4, P, 32 * grp, 32).rearrange("p (h j) -> p h j", h=4)[:, :, 0:5],
                             ACT.Sqrt, bias=eps[:, :], scale=1.0 / DV).then_inc(sem("hn_root"), 1)

            def head_hi(hs):
                for h in hs:
                    e.wait_ge(sem("hn_done"), h + 1)
                    e.activation(h_hi[:, h, :], o_att[h], ACT.Copy).then_inc(sem("h_hi_made"), 1)

            after = [[lambda: decay_exp(1)], [lambda: copy_blocks(1), lambda: decay_exp(2)], [lambda: copy_blocks(2), lambda: decay_exp(3)],
                     [lambda: decay_exp(4)], [lambda: decay_exp(5)], [lambda: decay_exp(6)], [lambda: decay_exp(7)], [],
                     [gla_decays, gla_values], [gla_keys], [], [], [gla_outputs], [], [], [gla_samples],
                     [lambda: ret_outputs((0, 1))], [ret_samples], [lambda: sample_out(0)], [lambda: sample_out(2)],
                     [lambda: sample_out(4)], [lambda: hn_root(0)], [lambda: head_hi((0, 1, 2, 3))],
                     [lambda: hn_square((GH + 2, GH + 3))]]
            inside = [[] for _ in range(16)] + [
                [ret_values], [lambda: ret_outputs((2, 3))], [], [lambda: sample_out(1), lambda: hn_square(range(GH))],
                [lambda: sample_out(3)], [lambda: sample_out(5)], [], [lambda: hn_square((GH, GH + 1))]]
            for n in range(24):
                u, f = 3 + n // 2, n % 2
                if f == 0:
                    stage_hi(e, u + 1)
                if n == 0:
                    e.wait_ge(sem("log_a_made"), 1)
                    e.activation(a_samp[:, :, :], log_a[:, :, T:N], ACT.Exp, scale=1.0 / TAU).then_inc(sem("a_samp_made"), 1)
                    decay_exp(0)
                for piece in inside[n]:
                    piece()
                if n == 16:
                    e.wait_ge(sem("gla_out"), 1)
                if n == 20:
                    e.wait_ge(sem("ret_out"), NC)
                tile_out(u, f)
                if n == 23:
                    e.activation(eps_copy[:, :], eps[:, :], ACT.Sqrt)
                for piece in after[n]:
                    piece()
            hn_root(1)
            head_hi(range(GH, KD))

            def rows_back(n, tiles):
                e.wait_ge(sem("rows_turned"), n + 1)
                if n:
                    e.wait_ge(sem("rows_stored"), 32 * n)
                for r in range(0, 2 + NS, 4):
                    k = min(4, 2 + NS - r)
                    ins = e.activation(row_out[0:tiles, r:r + k, :], bank(4 + r // 4, tiles, 0, k * P), ACT.Copy)
                ins.then_inc(sem("rows_out"), 1)

            def norm(n, u, per, g, col_g, col_b, last=False):
                if n == 0:
                    for name, count in (("samp_stored0", 64), ("samp_stored1", 64), ("gla_p_stored", 32), ("ret_p_stored", 16)):
                        e.wait_ge(sem(name), count)
                e.activation(eps_copy[:, :], eps[:, :], ACT.Sqrt)

                def copy_x(tiles):
                    for t in tiles:
                        e.wait_ge(sem("y_turned"), t + 1)
                        e.activation(y_tok[:, 0:NC, t * P:(t + 1) * P], bank(4 + t % 2).rearrange("p (j f) -> p j f", j=NC), ACT.Copy
                                     ).then_inc(sem("y_copied"), 1)

                def squares(tiles):
                    for t in tiles:
                        e.wait_ge(sem("ln_centered"), KD * n + t + 1)
                        if t >= 4:
                            e.wait_ge(sem("ln_added"), (KD - 2) * n + max(t - 4, 1))
                        e.activation(ln_sq[:, t % 4, :], x32[:, t, :], ACT.Square).then_inc(sem("ln_squared"), 1)

                for j in range(3 * per):
                    stage_hi(e, u + j + 1)
                    if n and j == 2 * per - 1:
                        rows_back(n - 1, KD if n == 2 else NU)
                squares(range(5))
                for j in range(3 * per, 4 * per):
                    stage_hi(e, u + j + 1)
                squares((5,))
                if last:
                    copy_x(range(6))
                squares((6,))
                if last:
                    copy_x((6,))
                squares((7,))
                if last:
                    copy_x((7,))
                else:
                    stage_hi(e, u + 4 * per + 1)
                e.wait_ge(sem("ln_varied"), n + 1)
                e.activation(ln_inv[:, 0, :], ln_var[:, 1, :], ACT.Sqrt, bias=eps[:, :]).then_inc(sem("ln_root"), 1)
                if last:
                    e.wait_ge(sem("ln_inverse"), n + 2)
                    e.wait_ge(sem("y_copied"), KD)
                    for j in Y_ORDER:
                        if j == NC:
                            e.wait_ge(sem("y_turned"), KD + 1)
                            for i in range(2):
                                ins = e.activation(y_tok[:, NC, i * 512:(i + 1) * 512], bank(2 + i), ACT.Copy)
                            ins.then_inc(sem("y_copied"), 1)
                            e.wait_ge(sem("y_copied"), KD + 1)
                        e.activation(y_tok[:, j, :], y_tok[:, j, :], ACT.Identity, bias=ln_inv[:, 1, j:j + 1],
                                     scale=ln_inv[:, 0, j:j + 1]).then_inc(sem("y_normed"), 1)
                    return
                for f in range(KD):
                    e.wait_ge(sem("ln_scaled"), KD * n + f + 1)
                    link(e.activation(x32[:, f, :], x32[:, f, :], ACT.Identity, bias=vec(g, col_b + f), scale=vec(g, col_g + f)))
                    e.activation(x_hi[:, f, :], x32[:, f, :], ACT.Copy).then_inc(sem("x_hi_made"), 1)

            def ffn(l):
                u, pr = U_IN[l], PR_IN[l]
                e.activation(eps_copy[:, :], eps[:, :], ACT.Silu)

                def step(i, first=False):
                    for s in range(2):
                        for f in range(2):
                            if f != s and not (first and s == 0):
                                make_hi(e, u + 2 * i + s + 1, (u + s + 1) % 2, 16 * ((u + s + 1) // 2 + 1) + 16 * i)
                            if s == 0 and f == 0:
                                e.wait_ge(sem("mul_done"), NF * l + 2 * i + 1)
                            tile = NF * s + 2 * i + f
                            acc_wait(e, pr + 2 * i + s, u + 2 * i + s, f)
                            e.activation(tmp[:, 2 * s + f, :], acc(f), ACT.Identity,
                                         bias=ffn_vec(l, 3, tile), scale=ffn_vec(l, 2, tile))
                            e.activation(last_rows[:, bass.ds(tile, 1), :], acc(f)[:, T - 2:N].unsqueeze(1), ACT.Copy
                                         ).then_inc(sem("t_made"), 1)
                            if s == 0:
                                continue
                            e.wait_ge(acc_free, 2 * (pr + 2 * i + 1) + f + 1)
                            e.activation(tmp[:, 4 + f, :], tmp[:, 2 + f, :], ACT.Silu).then_inc(sem("silu_done"), 1)
                            e.wait_ge(sem("mul_done"), NF * l + 2 * i + f + 2)
                            e.activation(h_hi[:, bass.ds(2 * i + f, 1), :], tmp[:, 6 + f:7 + f, :], ACT.Copy
                                         ).then_inc(sem("h_hi_made"), 1)

                step(0, True)
                with e.Fori(0, NF // 2 - 1) as i:
                    step(i + 1)
                norm(2 * l + 1, U_OUT[l], 3, V_LN, COL_LN2G + KD * l, COL_LN2B + KD * l, last=(l == 1))

            norm(0, U_MIXOUT, 1, V_LN, COL_LN1G, COL_LN1B)
            ffn(0)
            for j in range(4):
                for part in range(3):
                    u, pr = U_SCIN + 3 * j + part, PR_SCIN + 3 * j + part
                    if u > U_SCIN:
                        stage_hi(e, u + 1)
                    for f in range(2):
                        if part < 2:
                            if part == 0 and j:
                                e.wait_ge(sem("sc_gated"), 2 * j)
                            acc_wait(e, pr, u, f)
                            e.activation(tmp[:, 2 * part + f, :], acc(f), ACT.Copy).then_inc(acc_free, 1)
                        else:
                            e.wait_ge(acc_free, 2 * pr + f + 1)
                            e.activation(tmp[:, 6 + f, :], tmp[:, 4 + f, :], ACT.Identity,
                                         bias=vec(V_LN, COL_SCB + 2 * j + f), scale=vec(V_LN, COL_SCW + 2 * KD + 2 * j + f))
                            e.activation(last_rows[:, 2 * j + f, :], tmp[:, 4 + f, T - 2:N], ACT.Copy
                                         ).then_inc(sem("ch_rows"), 1)
                for f in range(2):
                    e.wait_ge(sem("sc_gated"), 2 * j + f + 1)
                    e.activation(h_hi[:, 2 * j + f, :], tmp[:, 6 + f, :], ACT.Copy).then_inc(sem("h_hi_made"), 1)
            norm(2, U_SCOUT, 1, V_LN, COL_LN1G + KD, COL_LN1B + KD)
            ffn(1)

        @block.vector
        def _(e):
            step = [0]

            def link(ins):
                step[0] += 1
                ins.then_inc(sem("vec_step"), 1)
                e.wait_ge(sem("vec_step"), step[0])

            e.memset(ones[:, :], 1.0)
            link(e.memset(eps[:, :], EPS))
            for f in range(KD):
                if f == 7:
                    stage_lo(e, 0)
                e.wait_ge(sem("x_turned"), f + 1)
                o = (f % 4) * 1024 + 256
                e.tensor_copy(x32[:, f, :], ps_t[:, o:o + N]).then_inc(sem("x_copied"), 1)
            stage_lo(e, 1)
            stage_lo(e, 2)
            e.wait_ge(sem("vecs_turned"), 1)
            for g in range(5):
                n = 2 * NU if g < V_LN else N_V
                ins = e.tensor_copy(vecs[:, g, 0:n], bank(4, P, g * 88, n))
            link(ins)
            e.wait_ge(sem("past_turned"), 1)
            def conv_past(j):
                w = vec(V_LN, COL_SCW + j * KD, KD)
                return bank(7, P, 0, KD * 16).rearrange("p (t b j) -> p b t j", b=NS, j=2)[:, :, :, j], bc(w, 1, NS)
            scratch = past_t[:, :, :]
            a, w = conv_past(0)
            e.tensor_tensor(past_conv[:, :, :], a, w, ALU.mult)
            a, w = conv_past(1)
            link(e.tensor_tensor(scratch[:, :, 0:KD], a, w, ALU.mult))
            link(e.tensor_tensor(past_conv[:, :, :], past_conv[:, :, :], scratch[:, :, 0:KD], ALU.add))
            e.memset(ones_one[:, :], 1.0).then_inc(sem("past_made"), 1)
            for l in range(DEPTH):
                e.wait_ge(sem("past_turned"), l + 2)
                for half in range(2):
                    b = slice(4 * half, 4 * half + 4)
                    rows = bank(5 + half, P, 0, 8 * NU).rearrange("p (b j t) -> p b j t", b=4, j=2)
                    for j, out in ((0, past_ffn[:, l, b, :]), (1, scratch[:, b, :])):
                        w = vecs[:, 2 * l, j * NU:(j + 1) * NU]
                        ins = e.tensor_tensor(out, rows[:, :, j, :], bc(w, 1, 4), ALU.mult)
                link(ins)
                e.tensor_tensor(past_ffn[:, l], past_ffn[:, l], scratch, ALU.add).then_inc(sem("past_made"), 1)
                e.wait_ge(sem("past_made"), l + 2)
            e.memset(ones_one[:, :], 1.0).then_inc(sem("vecs_made"), 1)
            e.wait_ge(sem("gate_ln"), 1)
            for g in range(2):
                ins = e.tensor_scalar(gate_m[:, g, :], acc(2 + g), vec(V_LN, COL_BG + g), 0.0, ALU.add, ALU.min)
            ins.then_inc(sem("gate_read"), 1)
            e.wait_ge(sem("gate_read"), 1)
            e.tensor_tensor(log_a[:, :, :], gate_m[:, :, :], gate_t[:, :, :], ALU.subtract).then_inc(sem("log_a_made"), 1)
            stage_lo(e, 3)
            e.wait_ge(sem("log_a_made"), 1)
            for g in range(2):
                for c in range(NC):
                    t = slice(c * C, (c + 1) * C)
                    ins = e.tensor_tensor_scan(cum[:, g, t], ones[:, :], log_a[:, g, t], 0.0, ALU.mult, ALU.add)
            link(ins)

            def blocks(a, h):
                return a.rearrange("p g (m w) -> p g m w", w=2 * h)

            def level_diff(l):
                h = C >> (l + 1)
                c, d = blocks(cum[:, :, :], h), blocks(dd[:, :, :], h)
                ref = c[:, :, :, h - 1:h].broadcast_to([P, 2, T // (2 * h), h])
                e.tensor_tensor(d[:, :, :, 0:h], ref, c[:, :, :, 0:h], ALU.subtract)
                e.tensor_tensor(d[:, :, :, h:], c[:, :, :, h:], ref, ALU.subtract).then_inc(sem("dd_made"), 1)

            def level_parts(l):
                h = C >> (l + 1)
                e.wait_ge(sem("dd_exp"), l + 1)
                d = blocks(dd[:, :, :], h)
                k, q = blocks(k_g[:, :, 0:T], h), blocks(q_g[:, :, 0:T], h)
                e.tensor_tensor(blocks(k_t[:, :, :], h)[:, :, :, 0:h], k[:, :, :, 0:h], d[:, :, :, 0:h], ALU.mult)
                e.tensor_tensor(blocks(q_t[:, :, :], h)[:, :, :, h:], q[:, :, :, h:], d[:, :, :, h:], ALU.mult
                                ).then_inc(sem("level_made"), 1)
                e.wait_ge(sem("level_made"), l + 1)

            def keys_diff():
                for g in range(2):
                    c = per_chunk(cum[:, g, :])
                    ins = e.tensor_tensor(per_chunk(dd[:, g, :]), c[:, :, C - 1:C].broadcast_to([P, NC, C]), c, ALU.subtract)
                ins.then_inc(sem("dd_made"), 1)

            def per_chunk(a):
                return a.rearrange("p (c t) -> p c t", t=C)

            def add_level(n):
                e.copy_predicated(sc[:, :, :].rearrange("p h (c t) -> p (h c) t", t=C), bc(masks[:, (n - 1) % (LEVELS + 1), :], 1, GH * NC),
                                  ps_t[:, 4 * 512:8 * 512].rearrange("p (m t) -> p m t", t=C)).then_inc(sem("level_added"), 1)
                e.wait_ge(sem("level_added"), n + 1)

            def level_step(n):
                e.wait_ge(sem("level_summed"), n + 1)
                if 1 <= n < LEVELS:
                    level_parts(n)
                    if n + 1 < LEVELS:
                        level_diff(n + 1)
                    else:
                        keys_diff()
                if n not in (1, 2):
                    add_level(n)

            def gla_decayed():
                e.wait_ge(sem("dd_exp"), LEVELS + 1)
                e.tensor_tensor(k_t[:, :, :], k_g[:, :, 0:T], dd[:, :, :], ALU.mult).then_inc(sem("gk_decayed"), 1)
                e.wait_ge(sem("cum_exp"), 1)
                e.tensor_tensor(q_t[:, :, :], q_g[:, :, 0:T], dd[:, :, :], ALU.mult).then_inc(sem("gq_decayed"), 1)

            def gla_states(cs):
                for c in cs:
                    e.wait_ge(sem("gla_inc"), c + 1)
                    for j in range(2):
                        p = slice(j * GDK, (j + 1) * GDK)
                        for g in range(2):
                            o = (6 + c % 2) * 512 + g * 256 + j * P
                            if c == 0:
                                ins = e.tensor_copy(state_g[p, 0, g, :], ps_t[p, o:o + P])
                            else:
                                ins = e.scalar_tensor_tensor(state_g[p, c, g, :], state_g[p, c - 1, g, :],
                                                             e_last[p, g, c:c + 1], ps_t[p, o:o + P], ALU.mult, ALU.add)
                    ins.then_inc(sem("gla_state"), 1)
                    e.wait_ge(sem("gla_state"), c + 1)

            rotated = [0]

            def rotate(x, tiles, u):
                e.wait_ge(sem("rot_loaded"), 16)
                for h in tiles:
                    e.wait_ge(acc_free, 2 * (u + h // 2) + h % 2 + 1)
                    e.tensor_tensor(rot_t[:, 0, :], x[:, h, :], rot[:, 0, :], ALU.mult)
                    e.tensor_tensor(rot_t[0:64, 1, :], x[64:128, h, :], rot[64:128, 1, :], ALU.mult)
                    link(e.tensor_tensor(rot_t[64:128, 1, :], x[0:64, h, :], rot[0:64, 1, :], ALU.mult))
                    e.tensor_tensor(x[:, h, :], rot_t[:, 0, :], rot_t[:, 1, :], ALU.add).then_inc(sem("rotated"), 1)
                    rotated[0] += 1
                    e.wait_ge(sem("rotated"), rotated[0])

            def ret_queries():
                e.wait_ge(sem("gla_out"), 1)
                for h in range(RH):
                    ins = e.tensor_tensor(per_chunk(q_dec[:, h, :]), per_chunk(q_r[:, h, 0:T]),
                                          bc(decay[:, RH * C + h * C:RH * C + (h + 1) * C], 1, NC), ALU.mult)
                ins.then_inc(sem("rq_decayed"), 1)

            def ret_scores():
                e.wait_ge(sem("rs_summed"), 1)
                for h in range(RH):
                    ins = e.tensor_tensor(per_chunk(sc[:, h, :]), per_chunk(bank(4 + h)), bc(decay[:, h * C:(h + 1) * C], 1, NC), ALU.mult)
                ins.then_inc(sem("rs_decayed"), 1)

            def ret_keys():
                e.wait_ge(sem("rk_turned"), 1)
                for c in range(NC):
                    ins = e.tensor_tensor(k_tok[:, c, :].rearrange("p (h d) -> p h d", h=RH),
                                          bank(4 + c).rearrange("p (h d) -> p h d", h=RH),
                                          bc(decay[:, 2 * RH * C:2 * RH * C + RH], 2, RDK), ALU.mult)
                ins.then_inc(sem("rk_decayed"), 1)

            def ret_states(cs):
                e.wait_ge(sem("gla_p_stored"), 32)
                for c in cs:
                    e.wait_ge(sem("ret_inc"), c + 1)
                    if c == 0:
                        ins = e.tensor_copy(state[:, 0, :, :], bank(6))
                    else:
                        for h in range(RH):
                            ins = e.scalar_tensor_tensor(state[:, c % 2, h, :], state[:, (c - 1) % 2, h, :], GAMMA[h] ** C,
                                                         bank(6 + c % 2, P, h * DV, DV), ALU.mult, ALU.add)
                    ins.then_inc(sem("ret_state"), 1)
                    e.wait_ge(sem("ret_state"), c + 1)

            def sample_states(i):
                o = (4 + 2 * (i % 2)) * 512
                if i < 2:
                    e.wait_ge(sem("outer_summed"), 2 * i + 2)
                    e.wait_ge(sem("samp_loaded%d" % i), 32)
                    e.wait_ge(sem("a_samp_made"), 1)
                    for b in range(NS):
                        ins = e.scalar_tensor_tensor(samp[:, i, b, :], samp[:, i, b, :], a_samp[:, i, b:b + 1],
                                                     ps_t[:, o + b * DV:o + (b + 1) * DV], ALU.mult, ALU.add)
                else:
                    e.wait_ge(sem("outer_summed"), i + 3)
                    e.wait_ge(sem("samp_loaded%d" % (i % 2)), 32 + 16 * (i // 2))
                    ins = e.scalar_tensor_tensor(samp[:, i % 2, :, :], samp[:, i % 2, :, :], GAMMA[i - 2],
                                                 ps_t[:, o:o + 1024].rearrange("p (b d) -> p b d", b=NS), ALU.mult, ALU.add)
                ins.then_inc(sem("samp_made"), 1)

            def hn_centered(hs):
                for h in hs:
                    e.wait_ge(sem("hn_mean"), h - GH + 1)
                    e.tensor_copy(o_att[h], acc(2 + h % 2)).then_inc(sem("hn_centered"), 1)

            def hn_inverse(grp):
                e.wait_ge(sem("hn_root"), grp + 1)
                e.reciprocal(inv[:, 4 * grp:4 * grp + 4, :], inv[:, 4 * grp:4 * grp + 4, :]).then_inc(sem("hn_inv"), 1)

            def head_scaled(hs):
                for h in hs:
                    gain = vec(V_LN, COL_GG) if h < GH else vec(V_LN, COL_GR + h - GH)
                    e.wait_ge(sem("hn_spread"), h + 1)
                    e.scalar_tensor_tensor(o_att[h], o_att[h], gain, acc(2 + h % 2), ALU.mult, ALU.mult).then_inc(sem("hn_scaled"), 1)
                    e.wait_ge(sem("hn_scaled"), h + 1)
                    if h < GH:
                        ins = e.tensor_tensor(o_att[h], o_att[h], r_g[:, h, :], ALU.mult)
                    else:
                        ins = e.scalar_tensor_tensor(o_att[h], o_att[h], vec(V_LN, COL_BR + h - GH), g_r[:, h - GH, :], ALU.add, ALU.mult)
                    ins.then_inc(sem("hn_done"), 1)

            def head_lo(hs):
                for h in hs:
                    e.wait_ge(sem("h_hi_made"), h + 1)
                    e.tensor_tensor(h_lo[:, h, :], o_att[h], h_hi[:, h, :].bitcast(F32), ALU.subtract
                                    ).then_inc(sem("h_made"), 1)

            e.tensor_scalar(centering[:, :], ident[:, :], -1.0 / DV, None, ALU.add)
            e.wait_ge(sem("tables_loaded"), 48)
            link(e.tensor_copy(masks[:, :, :], mask_rows[:, :, :]))
            level_diff(0)
            steps = [[lambda n=n: level_step(n)] for n in range(LEVELS + 1)] + [
                [gla_decayed, lambda: rotate(q_r, (0, 1), 5)], [lambda: rotate(q_r, (2, 3), 5)],
                [lambda: gla_states((0, 1)), lambda: rotate(k_r, (0,), 7)], [lambda: gla_states((2, 3)), lambda: rotate(k_r, (1,), 7)],
                [lambda: rotate(k_r, (2, 3), 7)], [ret_queries], [ret_scores], [ret_keys], [lambda: ret_states((0, 1))],
                [lambda: ret_states((2, 3))], [lambda: sample_states(0), lambda: sample_states(1)],
                [lambda: sample_states(2), lambda: sample_states(3)], [lambda: sample_states(4), lambda: sample_states(5)],
                [lambda: hn_inverse(0)], [lambda: head_scaled((0, 1, 2, 3))],
                [lambda: hn_centered((GH, GH + 1)), lambda: head_lo(range(GH)), lambda: hn_centered((GH + 2, GH + 3))]]
            for n, pieces in enumerate(steps):
                if n % 2 == 0:
                    stage_lo(e, 4 + n // 2)
                if n == 0:
                    e.wait_ge(acc_free, 2 * 3)
                    e.tensor_scalar(q_g[:, :, :], q_g[:, :, :], GDK ** -0.5, None, ALU.mult).then_inc(sem("q_scaled"), 1)
                    e.wait_ge(sem("q_scaled"), 1)
                    e.wait_ge(sem("cleared"), 3)
                    level_parts(0)
                    level_diff(1)
                for piece in pieces:
                    piece()
            hn_inverse(1)
            for h in range(GH, KD):
                head_scaled((h,))
                if h > GH:
                    head_lo((h - 1,))
            head_lo((KD - 1,))

            def residual(n, u, pr, per):
                for j in range(4):
                    for g in range(per):
                        stage_lo(e, u + per * j + g + 1)
                    for f in range(2):
                        t = 2 * j + f
                        acc_wait(e, pr + j, u + per * j + per - 1, f)
                        if t > KD // 2:
                            e.tensor_tensor(x32[:, t, :], x32[:, t, :], acc(f), ALU.add).then_inc(sem("ln_centered"), 1)
                            e.wait_ge(sem("ln_centered"), KD * n + t + 1)
                            e.memset(ones_one[:, :], 1.0).then_inc(acc_free, 1)
                            for i in range(0 if t == 5 else t, t + 1):
                                if i:
                                    e.wait_ge(sem("ln_totaled"), KD * n + i)
                                    e.tensor_tensor(ln_s1, ln_s1, x32[:, i, :], ALU.add).then_inc(sem("ln_totaled"), 1)
                                else:
                                    e.tensor_copy(ln_s1, x32[:, 0, :]).then_inc(sem("ln_totaled"), 1)
                            continue
                        e.scalar_tensor_tensor(x32[:, t, :], x32[:, t, :], ALPHA, acc(f), ALU.mult, ALU.add
                                               ).then_inc(acc_free, 1)
                        e.wait_ge(acc_free, 2 * (pr + j) + f + 1)
                        if 0 < t < KD // 2:
                            link(e.tensor_tensor(ln_sum[:, :], x32[:, 0, :] if t == 1 else ln_sum[:, :], x32[:, t, :], ALU.add))
                        if t == KD // 2 - 1:
                            e.tensor_scalar(ln_sum[:, :], ln_sum[:, :], -2.0 / D, None, ALU.mult).then_inc(sem("ln_summed"), 1)
                        if t == KD // 2:
                            e.wait_ge(sem("ln_shift"), n + 1)
                            for i in range(t + 1):
                                e.tensor_tensor(x32[:, i, :], x32[:, i, :], acc(2), ALU.add).then_inc(sem("ln_centered"), 1)
                            for i in range(t + 1, KD):
                                ins = e.scalar_tensor_tensor(x32[:, i, :], x32[:, i, :], ALPHA, acc(2), ALU.mult, ALU.add)
                            link(ins)

            def norm(n):
                last = n == 2 * DEPTH - 1
                d2, var = (ln_var[:, i, :] for i in range(2))
                e.wait_ge(sem("ln_var"), 2 * n + 1)
                e.tensor_scalar(ln_inv[:, 1, :], bank(7, P, 0, 5), -1.0 / D, None, ALU.mult).then_inc(sem("ln_mean_made"), 1)
                e.wait_ge(sem("ln_mean_made"), n + 1)
                link(e.tensor_tensor(d2, ln_inv[:, 1, :], ln_inv[:, 1, :], ALU.mult))
                e.wait_ge(sem("ln_var"), 2 * n + 2)
                e.scalar_tensor_tensor(var, bank(6, P, 0, 5), 1.0 / D, d2, ALU.mult, ALU.subtract).then_inc(sem("ln_varied"), 1)
                e.wait_ge(sem("ln_root"), n + 1)
                e.reciprocal(ln_inv[:, 0, :], ln_inv[:, 0, :]).then_inc(sem("ln_inverse"), 1)
                if last:
                    e.wait_ge(sem("ln_inverse"), n + 1)
                    e.tensor_tensor(ln_inv[:, 1, :], ln_inv[:, 1, :], ln_inv[:, 0, :], ALU.mult).then_inc(sem("ln_inverse"), 1)
                if last:
                    e.wait_ge(sem("ln_rows_loaded"), 32)
                    for i, j in enumerate(Y_ORDER):
                        e.wait_ge(sem("y_normed"), i + 1)
                        e.tensor_tensor(y_tok[:, j, :], y_tok[:, j, :], gain_rows[:, :], ALU.mult).then_inc(sem("y_gained"), 1)
                        if i >= 3:
                            e.wait_ge(sem("y_gained"), i + 1)
                            e.tensor_tensor(y_tok[:, j, :], y_tok[:, j, :], bias_rows[:, :], ALU.add).then_inc(sem("y_out"), 1)
                    return
                for f in range(KD + 2):
                    if f < KD:
                        e.wait_ge(sem("ln_spread"), 2 * n + 1)
                        e.tensor_tensor(x32[:, f, :], x32[:, f, :], acc(2), ALU.add).then_inc(sem("ln_shifted"), 1)
                    if f >= 2:
                        e.wait_ge(sem("ln_spread"), 2 * n + 2)
                        e.wait_ge(sem("ln_shifted"), KD * n + f - 1)
                        e.tensor_tensor(x32[:, f - 2, :], x32[:, f - 2, :], acc(3), ALU.mult).then_inc(sem("ln_scaled"), 1)
                stage_lo(e, NEXT[n] + 1)

            def ffn(l):
                u, pr = U_IN[l], PR_IN[l]

                def step(i, first=False):
                    for s in range(2):
                        for f in range(2):
                            if f != s and not (first and s == 0):
                                make_lo(e, u + 2 * i + s + 1, (u + s + 1) % 2)
                            tile = NF * s + 2 * i + f
                            n = NU * l + 4 * i + 2 * s + f
                            t = tmp[:, 2 * s + f, :]
                            e.wait_ge(sem("t_made"), n + 1)
                            e.tensor_tensor(t[:, T:N], t[:, T:N], past_col(l, tile), ALU.add)
                            e.scalar_tensor_tensor(t[:, 1:T], acc(f)[:, 0:T - 1], ffn_vec(l, 1, tile), t[:, 1:T],
                                                   ALU.mult, ALU.add).then_inc(sem("tap_done"), 1)
                            e.wait_ge(sem("tap_done"), n + 1)
                            e.scalar_tensor_tensor(t[:, 2:T], acc(f)[:, 0:T - 2], ffn_vec(l, 0, tile), t[:, 2:T],
                                                   ALU.mult, ALU.add).then_inc(acc_free, 1)
                            if s == 0:
                                continue
                            e.wait_ge(sem("silu_done"), NF * l + 2 * i + f + 1)
                            e.tensor_tensor(tmp[:, 6 + f, :], tmp[:, 4 + f, :], tmp[:, f, :], ALU.mult).then_inc(sem("mul_done"), 1)
                            e.wait_ge(sem("h_hi_made"), KD * (l + 1) + NF * l + 2 * i + f + 1)
                            e.tensor_tensor(h_lo[:, bass.ds(2 * i + f, 1), :], tmp[:, 6 + f:7 + f, :],
                                            h_hi[:, bass.ds(2 * i + f, 1), :].bitcast(F32), ALU.subtract).then_inc(sem("h_made"), 1)

                step(0, True)
                with e.Fori(0, NF // 2 - 1) as i:
                    step(i + 1)
                residual(2 * l + 1, U_OUT[l], PR_OUT[l], 3)
                norm(2 * l + 1)

            def past_col(l, tile):
                return past_ffn[:, l, :, bass.ds(tile, 1)].rearrange("p b o -> p (b o)")

            residual(0, U_MIXOUT, PR_MIXOUT, 1)
            norm(0)
            e.memset(ones_one[:, :], 1.0).then_inc(sem("mul_done"), 1)
            ffn(0)
            for j in range(4):
                for part in range(3):
                    u, pr = U_SCIN + 3 * j + part, PR_SCIN + 3 * j + part
                    if u > U_SCIN:
                        stage_lo(e, u + 1)
                    if part == 2:
                        for f in range(2):
                            acc_wait(e, pr, u, f)
                            e.wait_ge(acc_free, 2 * pr)
                            if j:
                                e.wait_ge(sem("h_hi_made"), KD + NF + 2 * j)
                            e.tensor_tensor(tmp[:, 4 + f, :], acc(f), tmp[:, 2 + f, :], ALU.mult).then_inc(acc_free, 1)
                for f in range(2):
                    t = 2 * j + f
                    y, ch = tmp[:, 6 + f, :], tmp[:, 4 + f, :]
                    e.wait_ge(sem("ch_rows"), t + 1)
                    e.tensor_tensor(y[:, T:N], y[:, T:N], past_conv[:, :, t], ALU.add)
                    link(e.scalar_tensor_tensor(y[:, 1:T], ch[:, 0:T - 1], vec(V_LN, COL_SCW + KD + t), y[:, 1:T], ALU.mult, ALU.add))
                    link(e.scalar_tensor_tensor(y[:, 2:T], ch[:, 0:T - 2], vec(V_LN, COL_SCW + t), y[:, 2:T], ALU.mult, ALU.add))
                    e.tensor_tensor(y, y, tmp[:, f, :], ALU.mult).then_inc(sem("sc_gated"), 1)
                for f in range(2):
                    t = 2 * j + f
                    e.wait_ge(sem("h_hi_made"), KD + NF + t + 1)
                    e.tensor_tensor(h_lo[:, t, :], tmp[:, 6 + f, :], h_hi[:, t, :].bitcast(F32), ALU.subtract
                                    ).then_inc(sem("h_made"), 1)
            residual(2, U_SCOUT, PR_SCOUT, 1)
            norm(2)
            ffn(1)


INPUTS = ["x_prompt", "x_sample", "state_gla", "state_ret", "state_conv", "state_ffn", "w_mix_in", "w_gla_gate_up",
          "b_gla_gate", "g_gla_norm", "g_ret_norm", "b_ret_norm", "w_mix_out", "w_sc_in", "w_sc_dw", "b_sc_dw",
          "w_sc_out", "ln1_g", "ln1_b", "w_ffn_in", "w_ffn_dw", "b_ffn_dw", "w_ffn_out", "ln2_g", "ln2_b"]
OUTPUTS = [("y_prompt", (1, T, D)), ("y_sample", (NS, 1, D)), ("gla_p", (1, 1, GH, GDK, DV)),
           ("gla_s", (1, NS, GH, GDK, DV)), ("ret_p", (1, 1, RH, RDK, DV)), ("ret_s", (1, NS, RH, RDK, DV)),
           ("conv_p", (1, 1, 2, D)), ("conv_s", (1, NS, 2, D)), ("ffn_p", (DEPTH, 1, 2, 2 * FF)),
           ("ffn_s", (DEPTH, NS, 2, 2 * FF))]


def kernel(**inputs):
    import concourse.bacc as bacc
    from concourse.bass_utils import run_bass_kernel_spmd

    nc = bacc.Bacc("TRN2", target_bir_lowering=False, num_devices=1, dynamic_dma_scratch_size=1024)
    ident, decay, rotary, masks = host_constants()
    arrays = {n: np.ascontiguousarray(inputs[n]) for n in INPUTS}
    arrays |= {"c_ident": ident, "c_decay": decay, "c_rotary": rotary.reshape(P, 2, N), "c_masks": masks}
    args = {n: nc.dram_tensor("in_" + n, a.shape, mybir.dt.from_np(a.dtype), kind="ExternalInput").ap()
            for n, a in arrays.items()}
    for n, shape in OUTPUTS:
        args[n] = nc.dram_tensor("out_" + n, shape, F32, kind="ExternalOutput").ap()
    build(nc, **args)
    r = run_bass_kernel_spmd(nc, [{"in_" + n: a for n, a in arrays.items()}], core_ids=[0])
    return tuple(r.results[0]["out_" + n] for n, _ in OUTPUTS)
```
